# Optimizing a Trainium2 kernel written in Bass

```python
import jax, jax.numpy as jnp
from jax import lax
import numpy as np

D_MODEL = 1024
BATCH = 1
SEQ = 1024
DEPTH = 1
DEC_BATCH = 8
DEC_SEQ = 8
PAST_LEN = 8192
PAGE_SIZE = 128

D_MIX = D_MODEL
W_A = D_MIX // 2
W_B = D_MIX - W_A
H_A = 8
H_B = 8
HD_B = W_B // H_B
D_IN = 2 * W_A + 2 * W_B
D_FF = 4 * D_MODEL
CONV_A_WIDTH = 31
CONV_B_WIDTH = 4
RG_C = 8.0
EPS = 1e-6

kernel_name = "hymba_conformer_rglru_adaln_decoder_step"

def rms_norm(x, g):
    xf = x.astype(jnp.float32)
    y = xf * lax.rsqrt(jnp.mean(xf * xf, axis=-1, keepdims=True) + EPS)
    return (y * g.astype(jnp.float32)).astype(x.dtype)

def layer_norm(x, g, b):
    xf = x.astype(jnp.float32)
    mu = jnp.mean(xf, axis=-1, keepdims=True)
    xc = xf - mu
    var = jnp.mean(xc * xc, axis=-1, keepdims=True)
    y = xc * lax.rsqrt(var + EPS) * g.astype(jnp.float32) + b.astype(jnp.float32)
    return y.astype(x.dtype)

def causal_dwconv(x, buf, w, b):
    k, c = w.shape
    xp = jnp.concatenate([buf.astype(x.dtype), x], axis=1)
    y = lax.conv_general_dilated(xp, w[:, None, :].astype(x.dtype), window_strides=(1,),
                                 padding='VALID', dimension_numbers=('NWC', 'WIO', 'NWC'),
                                 feature_group_count=c)
    return y + b, xp[:, xp.shape[1] - (k - 1):]

def rg_lru(x, h0, w_ga, b_ga, w_gx, b_gx, lam, reset_first):
    bsz, t, w = x.shape
    xh = x.reshape(bsz, t, H_B, HD_B)
    gate_a = jnp.einsum('bthi,hij->bthj', xh, w_ga).reshape(bsz, t, w) + b_ga
    gate_x = jnp.einsum('bthi,hij->bthj', xh, w_gx).reshape(bsz, t, w) + b_gx
    log_a = -RG_C * jax.nn.sigmoid(gate_a.astype(jnp.float32)) * jax.nn.softplus(-lam.astype(jnp.float32))
    a = jnp.exp(log_a)
    mult = jnp.sqrt(-jnp.expm1(2.0 * log_a))
    if reset_first:
        mult = mult.at[:, 0].set(1.0)
    bterm = mult * jax.nn.sigmoid(gate_x.astype(jnp.float32)) * x.astype(jnp.float32)
    if h0 is not None:
        bterm = bterm.at[:, 0].add(a[:, 0] * h0.astype(jnp.float32))

    def combine(l, r):
        a1, b1 = l
        a2, b2 = r
        return a1 * a2, a2 * b1 + b2

    _, h = lax.associative_scan(combine, (a, bterm), axis=1)
    return h.astype(x.dtype), h[:, -1].astype(x.dtype)

def trunk(x, c, bufs_a, bufs_b, hs, reset_first, w_ada, b_ada, g_mix, w_in, b_in,
          conv_a_w, conv_a_b, ln_a_g, ln_a_b, conv_b_w, conv_b_b,
          w_gate_a, b_gate_a, w_gate_x, b_gate_x, lru_lambda, w_out,
          g_ffn, w_up, w_down, g_final):
    new_a, new_b, new_h = [], [], []
    sc = jax.nn.silu(c)
    for l in range(DEPTH):
        mod = (jnp.einsum('bd,de->be', sc, w_ada[l]) + b_ada[l])[:, None, :]
        sh_m, sc_m, gt_m, sh_f, sc_f, gt_f = jnp.split(mod, 6, axis=-1)
        h = rms_norm(x, g_mix[l]) * (1 + sc_m) + sh_m
        u = jnp.einsum('btd,de->bte', h, w_in[l]) + b_in[l]
        u_val, u_glu, u_rec, u_y = jnp.split(u, [W_A, 2 * W_A, 2 * W_A + W_B], axis=-1)
        ga = u_val * jax.nn.sigmoid(u_glu)
        ca, nba = causal_dwconv(ga, bufs_a[l], conv_a_w[l], conv_a_b[l])
        ya = jax.nn.silu(layer_norm(ca, ln_a_g[l], ln_a_b[l]))
        cb, nbb = causal_dwconv(u_rec, bufs_b[l], conv_b_w[l], conv_b_b[l])
        hb, hlast = rg_lru(cb, None if hs is None else hs[l], w_gate_a[l], b_gate_a[l],
                           w_gate_x[l], b_gate_x[l], lru_lambda[l], reset_first)
        yb = hb * jax.nn.gelu(u_y)
        mix = jnp.einsum('bte,ed->btd', jnp.concatenate([ya, yb], axis=-1), w_out[l])
        x = x + gt_m * mix
        h2 = rms_norm(x, g_ffn[l]) * (1 + sc_f) + sh_f
        ff = jnp.square(jax.nn.relu(jnp.einsum('btd,df->btf', h2, w_up[l])))
        x = x + gt_f * jnp.einsum('btf,fd->btd', ff, w_down[l])
        new_a.append(nba)
        new_b.append(nbb)
        new_h.append(hlast)
    y = rms_norm(x, g_final)
    return y, jnp.stack(new_a), jnp.stack(new_b), jnp.stack(new_h)

def setup_inputs(seed: int = 0) -> dict:
    key = jax.random.key(seed)
    ks = jax.random.split(key, 40)
    f32 = jnp.float32

    def nrm(k, shape, scale):
        return jax.random.normal(k, shape, f32) * scale

    u = jax.random.uniform(ks[0], (DEPTH, W_B), f32, 0.9, 0.999)
    a_base = u ** (1.0 / RG_C)
    lru_lambda = jnp.log(a_base) - jnp.log1p(-a_base)
    return {
        "x_prompt": nrm(ks[1], (BATCH, SEQ, D_MODEL), 1.0),
        "x_sample": nrm(ks[2], (DEC_BATCH, DEC_SEQ, D_MODEL), 1.0),
        "c_prompt": nrm(ks[3], (BATCH, D_MODEL), 1.0),
        "c_sample": nrm(ks[4], (DEC_BATCH, D_MODEL), 1.0),
        "state_conv_a": nrm(ks[5], (DEPTH, DEC_BATCH, CONV_A_WIDTH - 1, W_A), 1.0),
        "state_conv_b": nrm(ks[6], (DEPTH, DEC_BATCH, CONV_B_WIDTH - 1, W_B), 1.0),
        "state_lru_h": nrm(ks[7], (DEPTH, DEC_BATCH, W_B), 0.5),
        "w_ada": nrm(ks[8], (DEPTH, D_MODEL, 6 * D_MODEL), D_MODEL ** -0.5),
        "b_ada": nrm(ks[9], (DEPTH, 6 * D_MODEL), 0.02),
        "g_mix": 1.0 + nrm(ks[10], (DEPTH, D_MODEL), 0.02),
        "w_in": nrm(ks[11], (DEPTH, D_MODEL, D_IN), D_MODEL ** -0.5),
        "b_in": nrm(ks[12], (DEPTH, D_IN), 0.02),
        "conv_a_w": nrm(ks[13], (DEPTH, CONV_A_WIDTH, W_A), CONV_A_WIDTH ** -0.5),
        "conv_a_b": nrm(ks[14], (DEPTH, W_A), 0.02),
        "ln_a_g": 1.0 + nrm(ks[15], (DEPTH, W_A), 0.02),
        "ln_a_b": nrm(ks[16], (DEPTH, W_A), 0.02),
        "conv_b_w": nrm(ks[17], (DEPTH, CONV_B_WIDTH, W_B), CONV_B_WIDTH ** -0.5),
        "conv_b_b": nrm(ks[18], (DEPTH, W_B), 0.02),
        "w_gate_a": nrm(ks[19], (DEPTH, H_B, HD_B, HD_B), HD_B ** -0.5),
        "b_gate_a": nrm(ks[20], (DEPTH, W_B), 0.02),
        "w_gate_x": nrm(ks[21], (DEPTH, H_B, HD_B, HD_B), HD_B ** -0.5),
        "b_gate_x": nrm(ks[22], (DEPTH, W_B), 0.02),
        "lru_lambda": lru_lambda,
        "w_out": nrm(ks[23], (DEPTH, D_MIX, D_MODEL), D_MIX ** -0.5),
        "g_ffn": 1.0 + nrm(ks[24], (DEPTH, D_MODEL), 0.02),
        "w_up": nrm(ks[25], (DEPTH, D_MODEL, D_FF), D_MODEL ** -0.5),
        "w_down": nrm(ks[26], (DEPTH, D_FF, D_MODEL), D_FF ** -0.5),
        "g_final": 1.0 + nrm(ks[27], (D_MODEL,), 0.02),
    }

def reference(x_prompt, x_sample, c_prompt, c_sample, state_conv_a, state_conv_b, state_lru_h,
              w_ada, b_ada, g_mix, w_in, b_in, conv_a_w, conv_a_b, ln_a_g, ln_a_b,
              conv_b_w, conv_b_b, w_gate_a, b_gate_a, w_gate_x, b_gate_x, lru_lambda,
              w_out, g_ffn, w_up, w_down, g_final):
    bp = x_prompt.shape[0]
    zeros_a = jnp.zeros((DEPTH, bp, CONV_A_WIDTH - 1, W_A), x_prompt.dtype)
    zeros_b = jnp.zeros((DEPTH, bp, CONV_B_WIDTH - 1, W_B), x_prompt.dtype)
    y_prompt, pa, pb, ph = trunk(
        x_prompt, c_prompt, zeros_a, zeros_b, None, True,
        w_ada, b_ada, g_mix, w_in, b_in, conv_a_w, conv_a_b, ln_a_g, ln_a_b,
        conv_b_w, conv_b_b, w_gate_a, b_gate_a, w_gate_x, b_gate_x, lru_lambda,
        w_out, g_ffn, w_up, w_down, g_final)
    y_sample, sa, sb, sh = trunk(
        x_sample, c_sample, state_conv_a, state_conv_b, state_lru_h, False,
        w_ada, b_ada, g_mix, w_in, b_in, conv_a_w, conv_a_b, ln_a_g, ln_a_b,
        conv_b_w, conv_b_b, w_gate_a, b_gate_a, w_gate_x, b_gate_x, lru_lambda,
        w_out, g_ffn, w_up, w_down, g_final)
    return (y_prompt, y_sample, pa, pb, ph, sa, sb, sh)


_drawn_inputs = setup_inputs


def setup_inputs(seed=0):
    import zlib

    import numpy as np

    out = dict(_drawn_inputs(seed))
    spreads = {}
    factors = {'g_mix': 2.956,
     'conv_a_b': 8.0,
     'ln_a_g': 22.406,
     'ln_a_b': 23.601,
     'b_gate_a': 8.0,
     'b_gate_x': 8.0,
     'g_ffn': 3.649,
     'g_final': 9.787}
    for name, (base, spread) in spreads.items():
        noise = np.random.default_rng([zlib.crc32(name.encode()), seed]).standard_normal(out[name].shape)
        drawn = base * np.exp(spread * noise) if base else spread * noise
        out[name] = __import__('jax').numpy.asarray(drawn.astype(out[name].dtype))
    for name, factor in factors.items():
        out[name] = (out[name] * factor).astype(out[name].dtype)
    return out
```

```python
from contextlib import ExitStack

import concourse.bass as bass
from concourse import mybir

F32 = mybir.dt.float32
F32R = mybir.dt.float32r
ALU = mybir.AluOpType
ACT = mybir.ActivationFunctionType

P = 128
D = 1024
KD = D // P
SEQ = 1024
NB, TB = 8, 8
SMP = NB * TB
TOK = SEQ + SMP
NT = SEQ // P + 1
WA = 512
J = WA // P
KA, KB = 31, 4
FF = 4096
FI = 4
NBLK = FF // (FI * P)
CH = 384
NC = 3
CW = [CH, CH, TOK - 2 * CH]
PROMPT2 = SEQ - 2 * CH
GA_P = KA - 1 + SEQ
GA_S = KA - 1 + TB
GA_W = GA_P + NB * GA_S
RB_P = KB - 1 + SEQ
RB_S = KB - 1 + TB
RB_W = RB_P + NB * RB_S
EPS = 1e-6
N_ROWS_PAR = 15

C_BIN, C_BADA, C_GMIX, C_GFFN, C_CAB, C_LNG, C_LNB, C_CBB, C_BGA, C_BGX, C_LAM, C_CBW = (
    0, 16, 64, 72, 80, 84, 88, 92, 96, 100, 104, 108)
N_PAR = C_CBW + KB * J
M_SHM, M_SCM, M_GTM, M_SHF, M_SCF, M_GTF = (8 * i for i in range(6))
ADA0 = 16
W_OUT0 = 16
W_MLP0 = W_OUT0 + KD


def trunk(nc, x_prompt, x_sample, c_prompt, c_sample, state_conv_a, state_conv_b, state_lru_h,
          w_ada, b_ada, g_mix, w_in, b_in, conv_a_w, conv_a_b, ln_a_g, ln_a_b, conv_b_w, conv_b_b,
          w_gate_a, b_gate_a, w_gate_x, b_gate_x, lru_lambda, w_out, g_ffn, w_up, w_down, g_final,
          y_prompt, y_sample, ca_prompt, cb_prompt, h_prompt, ca_sample, cb_sample, h_sample):
    ctx = ExitStack()
    with ctx:
        def sb(name, shape, dt=F32):
            return ctx.enter_context(nc.sbuf_tensor(name, shape, dt))

        def shared(*layouts):
            out = {}
            for n, layout in enumerate(layouts):
                scope = ExitStack()
                for name, shape, dt in layout:
                    out[name] = scope.enter_context(nc.sbuf_tensor(name, shape, dt))
                if n < len(layouts) - 1:
                    scope.close()
                else:
                    ctx.push(scope)
            return out

        def sem(name):
            return ctx.enter_context(nc.semaphore(name))

        ident = sb("ident", [P, P])
        mean_w = sb("mean_w", [P, P])
        par = sb("par", [P, N_PAR])
        caw = sb("caw", [P, KA * J])
        mod = sb("mod", [P, 48, 9])
        sc_m = sb("sc_m", [P, KD, 9])
        sc_f = sb("sc_f", [P, KD, 9])
        cT = sb("cT", [P, KD, 9])
        h_end = sb("h_end", [P, J, 9])
        h0 = sb("h0", [P, NB, J])
        hb = sb("hb", [P, 2, J])
        k4 = sb("k4", [P, 2, J])
        sp = sb("sp", [P, 5, J])
        eps = sb("eps", [P, 1])
        ssq = sb("ssq", [P, 3, NT])
        tmp8 = sb("tmp8", [P, NB])
        raw = sb("raw", [P, 2, D])
        tail_b = sb("tail_b", [P, J, NB * (KB - 1)])
        rr = shared([("raw_ada", [P, KD, P], F32)], [("tail_a", [P, J, NB * (KA - 1)], F32)],
                    [("gt_tok", [P, 2, KD, SMP], F32)])
        raw_ada, tail_a, gt_tok = rr["raw_ada"], rr["tail_a"], rr["gt_tok"]
        w_hi = sb("w_hi", [P, 2, D], F32R)
        w_lo = sb("w_lo", [P, 2, D], F32R)
        stk = sb("stk", [P, KD, P], F32R)
        rx = shared([("conv_a", [P, J, TOK], F32), ("gel", [P, J, TOK], F32)],
                    [("x2", [P, NT, D], F32)])
        conv_a, gel, x2 = rx["conv_a"], rx["gel"], rx["x2"]
        rh = shared([("ada0", [P, 4, KD, 512], F32)],
                    [("act_hi", [P, KD, TOK], F32R), ("act_lo", [P, KD, TOK], F32R)])
        ada0, act_hi, act_lo = rh["ada0"], rh["act_hi"], rh["act_lo"]
        rw = shared([("ld_sa", [120, 2, WA], F32), ("ld_c", [9, 2, D], F32),
                     ("ld_par", [P, 3, P], F32), ("ld_sb", [NB * (KB - 1), WA], F32)],
                    [("cb", [P, J, TOK], F32), ("ga", [P, J, GA_W], F32), ("rec", [P, J, RB_W], F32),
                     ("sg", [P, TOK], F32)],
                    [("wb_hi", [P, KD, D], F32R), ("wb_lo", [P, KD, D], F32R)])
        ld_sa, ld_c, ld_par, ld_sb = (rw[n] for n in ("ld_sa", "ld_c", "ld_par", "ld_sb"))
        cb, ga, rec, sg, wb_hi, wb_lo = (rw[n] for n in ("cb", "ga", "rec", "sg", "wb_hi", "wb_lo"))
        rg = shared([("wg", [P, 2, J, P], F32)], [("rstd", [P, TOK], F32)],
                    [("gt_p", [P, D], F32), ("gt_s", [SMP, D], F32)])
        wg, rstd, gt_p, gt_s = rg["wg"], rg["rstd"], rg["gt_p"], rg["gt_s"]
        rt = shared([("sq", [P, J, CH], F32)], [("relu", [P, 2, CH], F32), ("relu2", [P, 2, CH], F32)],
                    [("stage", [P, 4, WA], F32)], [("xn", [P, 2, D], F32)])
        sq, relu, relu2, stage, xn = rt["sq"], rt["relu"], rt["relu2"], rt["stage"], rt["xn"]
        ps = ctx.enter_context(nc.psum_tensor("ps", [P, 8, 512], F32))

        c_in, par_in, sb_in, sa_in, wg_in = (sem(n) for n in ("c_in", "par_in", "sb_in", "sa_in", "wg_in"))
        x_in = [sem(f"x_in{t}") for t in range(NT)]
        ada0_in = [sem(f"ada0_in{g}") for g in range(4)]
        raw_in = [sem("raw_in0"), sem("raw_in1")]
        ada_in, gf_in, stored = sem("ada_in"), sem("gf_in"), sem("stored")
        staged_out = sem("staged_out")
        pool_set = sem("pool_set")
        pool_ord = sem("pool_ord")
        act_ord, dve_ord = sem("act_ord"), sem("dve_ord")
        c_sig, c_silu, c_tr, c_cp = sem("c_sig"), sem("c_silu"), sem("c_tr"), sem("c_cp")
        par_tr, par_cp, sa_tr, sa_cp = sem("par_tr"), sem("par_cp"), sem("sa_tr"), sem("sa_cp")
        ada_done, ada_evac = sem("ada_done"), sem("ada_evac")
        ssq_done, std_done, xn_done = sem("ssq_done"), sem("std_done"), sem("xn_done")
        tr_done, hf_d, hf_a = sem("tr_done"), sem("hf_d"), sem("hf_a")
        nhi_done, nlo_done = sem("nhi_done"), sem("nlo_done")
        sc_done = sem("sc_done")
        hi_ready, lo_ready = sem("hi_ready"), sem("lo_ready")
        strip_a, strip_b = sem("strip_a"), sem("strip_b")
        evac_a, evac_b = sem("evac_a"), sem("evac_b")
        ga_ready, conva_tap, convb_tap = sem("ga_ready"), sem("conva_tap"), sem("convb_tap")
        gated, tails = sem("gated"), sem("tails")
        st_tr, st_cp = sem("st_tr"), sem("st_cp")
        gate_a, gate_x, t_a, t_x = sem("gate_a"), sem("gate_x"), sem("t_a"), sem("t_x")
        a_done, a2_done, q_done, m_done, h_done, yb_done = (
            sem(n) for n in ("a_done", "a2_done", "q_done", "m_done", "h_done", "yb_done"))
        k_done = sem("k_done")
        mean_done, xc_done, sq_done, var_done, sd_done, xs_done, sig_done, ya_done = (
            sem(n) for n in ("mean_done", "xc_done", "sq_done", "var_done", "sd_done", "xs_done",
                             "sig_done", "ya_done"))
        yhi_done, ylo_done = sem("yhi_done"), sem("ylo_done")
        gt_mm, gt_cp = sem("gt_mm"), sem("gt_cp")
        tile_done, rmw_done = sem("tile_done"), sem("rmw_done")
        up_done, up_evac, r2_done, ffhi_done, fflo_done = (
            sem(n) for n in ("up_done", "up_evac", "r2_done", "ffhi_done", "fflo_done"))
        fin_ssq, fin_std, fin_y = sem("fin_ssq"), sem("fin_std"), sem("fin_y")

        ga_s = ga[:, :, GA_P:GA_W].rearrange("p j (b s) -> p j b s", s=GA_S)
        rec_s = rec[:, :, RB_P:RB_W].rearrange("p j (b s) -> p j b s", s=RB_S)
        win_v = w_in[0].rearrange("(k p) n -> p k n", p=P)
        wada_v = w_ada[0].rearrange("(k p) n -> p k n", p=P)
        wdown_v = w_down[0].rearrange("(n p) d -> n p d", p=P)
        wup_v = w_up[0].rearrange("(k p) n -> p k n", p=P)
        raw_k = raw[:, :, :].rearrange("p s (k n) -> p s k n", n=P)
        xs_rows = x_sample.rearrange("b t d -> (b t) d")
        ys_rows = y_sample.rearrange("b t d -> (b t) d")
        rows = [P] * (NT - 1) + [SMP]

        def wait(eng, s, value):
            if not isinstance(value, int) or value > 0:
                eng.wait_ge(s, value)

        def wait_apart(eng, s, value):
            eng.wait_ge(pool_set, 1)
            eng.wait_ge(s, value)

        def bank_pair(n):
            return 4 if n % 2 == 0 else 6

        block = ctx.enter_context(nc.Block())

        @block.sync
        def _(sp):
            def load_x(t):
                src = x_prompt[0, t * P:(t + 1) * P, :] if t < NT - 1 else xs_rows
                sp.dma_start(x2[0:rows[t], t, :], src).then_inc(x_in[t], 16)

            def load_piece(n_ge, slot, src, view):
                wait(sp, lo_ready, n_ge)
                dst = raw_k[:, slot, :, :] if view else raw[:, slot, :]
                sp.dma_start(dst, src).then_inc(raw_in[slot], 16)

            def load_ada(e):
                wait_apart(sp, ada_done, e)
                sp.dma_start(raw_ada[:, :, :], wada_v[:, :, bass.ds(e * P, P)]).then_inc(ada_in, 16)

            load_x(0)
            for g in range(4):
                sp.dma_start(ada0[:, g, :, :], wada_v[:, :, g * 512:(g + 1) * 512]).then_inc(ada0_in[g], 16)
                if g < 2:
                    load_x(g + 1)
            for s in range(2):
                load_piece(0, s, win_v[:, :, s * WA:s * WA + P], True)
            for t in range(3, NT):
                load_x(t)

            def step(m, nxt):
                for s in range(2):
                    load_ada(ADA0 + 4 * m + 2 * s)
                    load_ada(ADA0 + 4 * m + 2 * s + 1)
                    if nxt is not None:
                        load_piece(2 * m + s + 1, s, win_v[:, :, bass.ds(nxt + s * WA, P)], True)

            with sp.Fori(0, J - 1) as j:
                step(j, (j + 1) * P)
            step(J - 1, 2 * WA)
            with sp.Fori(0, J - 1) as j:
                step(j + J, (j + 1) * P + 2 * WA)
            step(2 * J - 1, None)
            for k in range(KD):
                load_piece(W_OUT0 + k - 1, k % 2, w_out[0, k * P:(k + 1) * P, :], False)
            sp.wait_ge(yhi_done, J + NC)
            sp.wait_ge(ylo_done, J + NC)
            for t in range(NT):
                load_x(t)

            def down_piece(n, b, i, slot):
                load_piece(n - 1, slot, wdown_v[b * FI + i, :, :], False)

            def mlp(b, last):
                n = W_MLP0 + 2 + 8 * b
                down_piece(n, b, 0, 0)
                down_piece(n + 1, b, 1, 1)
                load_piece(n + 1, 0, wup_v[:, :, bass.ds(b * (FI * P) + 2 * P, P)], True)
                down_piece(n + 3, b, 2, 1)
                down_piece(n + 4, b, 3, 0)
                load_piece(n + 4, 1, wup_v[:, :, bass.ds(b * (FI * P) + 3 * P, P)], True)
                if not last:
                    load_piece(n + 5, 0, wup_v[:, :, bass.ds(b * (FI * P) + 4 * P, P)], True)
                    load_piece(n + 6, 1, wup_v[:, :, bass.ds(b * (FI * P) + 5 * P, P)], True)

            load_piece(W_MLP0 - 1, 0, wup_v[:, :, 0:P], True)
            load_piece(W_MLP0, 1, wup_v[:, :, P:2 * P], True)
            with sp.Fori(0, NBLK - 1) as b:
                mlp(b, False)
            mlp(NBLK - 1, True)
            sp.wait_ge(hi_ready, W_MLP0 + 8 * NBLK)
            sp.wait_ge(lo_ready, W_MLP0 + 8 * NBLK)
            sp.dma_start(raw[:, 0, :], g_final.partition_broadcast(P)).then_inc(gf_in, 16)
            for t in range(NT):
                sp.wait_ge(fin_y, t + 1)
                dst = y_prompt[0, t * P:(t + 1) * P, :] if t < NT - 1 else ys_rows
                sp.dma_start(dst, x2[0:rows[t], t, :]).then_inc(stored, 16)
            sp.wait_ge(stored, 16 * NT)

        @block.gpsimd
        def _(pool):
            pool.memset(ident[:, :], 0.0).then_inc(pool_ord, 1)
            pool.wait_ge(pool_ord, 1)
            pool.affine_select(out=ident[:, :], in_=ident[:, :], compare_op=ALU.not_equal, fill=1.0,
                               base=0, pattern=[[-1, P]], channel_multiplier=1).then_inc(pool_set, 1)
            pool.memset(mean_w[:, :], 1.0 / WA).then_inc(pool_set, 1)
            pool.memset(eps[:, :], EPS).then_inc(pool_set, 1)
            pool.memset(ga[:, :, 0:KA - 1], 0.0).then_inc(ga_ready, 1)
            pool.memset(rec[:, :, 0:KB - 1], 0.0).then_inc(pool_set, 1)
            pool.memset(wg[:, :, :, :], 0.0).then_inc(pool_set, 1)

            def lo(n, slot, dst, hi):
                pool.wait_ge(hi_ready, n + 1)
                pool.tensor_tensor(dst, raw[:, slot, :], hi.bitcast(F32), ALU.subtract).then_inc(lo_ready, 1)

            def strip_lo(n, slot, used, count):
                wait(pool, used, count)
                lo(n, slot, w_lo[:, slot, :], w_hi[:, slot, :])

            strip_lo(0, 0, strip_a, 0)
            strip_lo(1, 1, strip_b, 0)

            def step(m, glu, last):
                strip_lo(2 * m + 2, 0, strip_a, NC * (m + 1))
                if glu:
                    j = m
                    pool.wait_ge(evac_b, NC * (j + 1))
                    pool.wait_ge(evac_a, NC * (j + 1))
                    pool.tensor_tensor(ga[:, j, KA - 1:GA_P], ga[:, j, KA - 1:GA_P], sg[:, 0:SEQ],
                                       ALU.mult).then_inc(ga_ready, 1)
                    pool.tensor_tensor(ga_s[:, j, :, KA - 1:GA_S], ga_s[:, j, :, KA - 1:GA_S],
                                       sg[:, SEQ:TOK].rearrange("p (b t) -> p b t", t=TB),
                                       ALU.mult).then_inc(ga_ready, 1)
                strip_lo(2 * m + 3, 1, strip_b, NC * (m + 1))

            step(0, True, False)
            with pool.Fori(1, J) as j:
                step(j, True, False)
            with pool.Fori(J, 2 * J - 1) as m:
                step(m, False, False)
            pool.wait_ge(ada_done, 48)
            for j in range(J):
                pool.tensor_copy(tail_a[:, j, :].rearrange("p (b s) -> p b s", b=NB), ga_s[:, j, :, TB:GA_S])
            pool.wait_ge(evac_a, 2 * J * NC)
            for j in range(J):
                last = pool.tensor_copy(tail_b[:, j, :].rearrange("p (b s) -> p b s", b=NB), rec_s[:, j, :, TB:RB_S])
            last.then_inc(tails, 1)
            pool.wait_ge(st_tr, 5)
            pool.wait_ge(ada_evac, 48)
            for g, row0 in ((0, M_GTM), (1, M_GTF)):
                for k in range(KD):
                    last = pool.tensor_copy(gt_tok[:, g, k, :].rearrange("p (b t) -> p b t", t=TB),
                                            mod[:, row0 + k, 1:9].unsqueeze(2).broadcast_to([P, NB, TB]))
            last.then_inc(tails, 1)
            pool.wait_ge(yb_done, J)
            pool.wait_ge(conva_tap, 2 * KA * J)
            for k in range(KD):
                lo(W_OUT0 + k, k % 2, wb_lo[:, k, :], wb_hi[:, k, :])

            lo(W_MLP0, 0, w_lo[:, 0, :], w_hi[:, 0, :])
            lo(W_MLP0 + 1, 1, w_lo[:, 1, :], w_hi[:, 1, :])

            def mlp(b, last):
                n = W_MLP0 + 2 + 8 * b
                pool.wait_ge(tile_done, NT * (b + 1))
                lo(n, 0, wb_lo[:, 0, :], wb_hi[:, 0, :])
                lo(n + 1, 1, wb_lo[:, 1, :], wb_hi[:, 1, :])
                strip_lo(n + 2, 0, up_done, 12 * b + 3)
                lo(n + 3, 1, wb_lo[:, 2, :], wb_hi[:, 2, :])
                lo(n + 4, 0, wb_lo[:, 3, :], wb_hi[:, 3, :])
                strip_lo(n + 5, 1, up_done, 12 * b + 6)
                if not last:
                    strip_lo(n + 6, 0, up_done, 12 * b + 9)
                    strip_lo(n + 7, 1, up_done, 12 * b + 12)

            with pool.Fori(0, NBLK - 1) as b:
                mlp(b, False)
            mlp(NBLK - 1, True)

        @block.scalar
        def _(act):
            ordered = [0]

            def own(ins):
                ordered[0] += 1
                ins.then_inc(act_ord, 1)
                act.wait_ge(act_ord, ordered[0])

            def load_rows(dst, src, s):
                act.dma_start(dst, src).then_inc(s, 16)

            load_rows(ld_c[0:1, 0, :], c_prompt, c_in)
            load_rows(ld_c[1:9, 0, :], c_sample, c_in)
            for col, src in ((C_BIN, b_in), (C_BADA, b_ada), (C_CAB, conv_a_b), (C_LNG, ln_a_g),
                             (C_LNB, ln_a_b), (C_CBB, conv_b_b), (C_BGA, b_gate_a), (C_BGX, b_gate_x),
                             (C_LAM, lru_lambda), (C_GMIX, g_mix), (C_GFFN, g_ffn)):
                n = src.shape[1] // P
                load_rows(ld_par[col:col + n, 0, :], src[0].rearrange("(r p) -> r p", p=P), par_in)
            load_rows(ld_par[C_CBW:N_PAR, 0, :], conv_b_w[0].rearrange("k (j p) -> (k j) p", p=P), par_in)
            load_rows(ld_par[0:KA * J, 1, :], conv_a_w[0].rearrange("k (j p) -> (k j) p", p=P), par_in)
            load_rows(ld_par[0:NB * J, 2, :], state_lru_h[0].rearrange("b (j p) -> (b j) p", p=P), par_in)
            load_rows(ld_sb[:, :], state_conv_b[0].rearrange("b s c -> (b s) c"), par_in)
            for half in range(2):
                load_rows(ld_sa[:, half, :], state_conv_a[0, 4 * half:4 * half + 4].rearrange("b s c -> (b s) c"),
                          sa_in)


            act.wait_ge(c_in, 32)
            act.activation(ld_c[:, 1, :], ld_c[:, 0, :], ACT.Sigmoid).then_inc(c_sig, 1)
            act.wait_ge(c_tr, 1)
            act.activation(cT[:, :, :], ps[:, 0, 0:72].rearrange("p (k c) -> p k c", c=9), ACT.Copy).then_inc(c_cp, 1)

            act.wait_ge(par_cp, 1)
            lam = par[:, C_LAM:C_LAM + J]
            own(act.activation(sp[:, 0, :], lam, ACT.Abs))
            act.activation(sp[:, 1, :], sp[:, 0, :], ACT.Exp, scale=-1.0).then_inc(k_done, 1)
            act.wait_ge(k_done, 2)
            act.activation(sp[:, 3, :], sp[:, 2, :], ACT.Ln).then_inc(k_done, 1)

            def norm(n, t, src, junk, wait_free):
                wait_free()
                r = rows[t]
                own(act.activation(junk[0:r, 0:D], src[0:r, t, :], ACT.Square, accum_out=ssq[0:r, 0, t:t + 1]))
                act.activation(ssq[0:r, 1, t:t + 1], ssq[0:r, 0, t:t + 1], ACT.Sqrt, scale=1.0 / D,
                               bias=eps[0:r, :]).then_inc(std_done, 1)

            def modulate(n, t, scale, shift0, slot, free):
                hf = xn[:, slot, :].rearrange("p (k c) -> p k c", c=P)
                if t < NT - 1:
                    act.wait_ge(tr_done, n + 1)
                    wait(act, nlo_done, free)
                    for k in range(4, KD):
                        last = act.activation(hf[:, k, :], ps[:, bank_pair(n) + 1, (k - 4) * P:(k - 3) * P],
                                              ACT.Identity, scale=scale[:, k, 0:1],
                                              bias=mod[:, shift0 + k, 0:1])
                    last.then_inc(hf_a, 1)
                    act.wait_ge(hf_a, hfa(n))
                act.wait_ge(hf_d, n + 1)
                act.activation(act_hi[:, :, t * P:t * P + rows[t]], hf[:, :, 0:rows[t]], ACT.Copy).then_inc(nhi_done, 1)

            def hi(n, slot, dst, loaded):
                act.wait_ge(raw_in[slot], loaded)
                act.activation(dst, raw[:, slot, :], ACT.Copy).then_inc(hi_ready, 1)

            def strip_hi(n, slot, used, count):
                wait(act, used, count)
                hi(n, slot, w_hi[:, slot, :], 16 * (n // 2 + 1))

            def ada_out(e, bank):
                act.wait_ge(ada_done, e + 1)
                act.activation(mod[:, e, :], ps[:, bank, 0:9], ACT.Identity,
                               bias=par[:, bass.ds(C_BADA + e, 1)]).then_inc(ada_evac, 1)

            act.wait_ge(pool_set, 5)
            for g, w in ((0, w_gate_a), (1, w_gate_x)):
                for half in range(2):
                    at = slice(64 * half, 64 * half + 64)
                    act.dma_start(wg[at, g, :, at], w[0].rearrange("(j h) i o -> h i j o", h=2)[half]).then_inc(wg_in, 16)
            for t in range(3):
                norm(t, t, x2, sg, lambda: act.wait_ge(x_in[t], 16))
            for e in range(ADA0):
                ada_out(e, 6 + e % 2)
            act.wait_ge(sc_done, 1)
            for s in range(2):
                strip_hi(s, s, strip_a, 0)
            for t in range(NT):
                if t + 3 < NT:
                    norm(t + 3, t + 3, x2, sg, lambda: act.wait_ge(x_in[t + 3], 16))
                modulate(t, t, sc_m, M_SHM, t % 2, t - 1)

            def chunk_out(c, src_bank, dst_p, dst_s, func, bias, done):
                if c < 2:
                    act.activation(dst_p(c * CH, CH), ps[:, src_bank + c, 0:CH], func, bias=bias).then_inc(done, 1)
                else:
                    act.activation(dst_p(c * CH, PROMPT2), ps[:, src_bank + c, 0:PROMPT2], func, bias=bias)
                    act.activation(dst_s, ps[:, src_bank + c, PROMPT2:PROMPT2 + SMP].rearrange("p (b t) -> p b t", t=TB),
                                   func, bias=bias).then_inc(done, 1)

            def step(m, j, group_a, last):
                for c in range(NC):
                    wait_apart(act, strip_a, NC * m + c + 1)
                    if group_a:
                        chunk_out(c, 0, lambda o, w: ga[:, j, KA - 1 + o:KA - 1 + o + w],
                                  ga_s[:, j, :, KA - 1:GA_S], ACT.Identity, par[:, bass.ds(C_BIN + j, 1)], evac_a)
                    else:
                        chunk_out(c, 0, lambda o, w: rec[:, j, KB - 1 + o:KB - 1 + o + w],
                                  rec_s[:, j, :, KB - 1:RB_S], ACT.Identity,
                                  par[:, bass.ds(C_BIN + 2 * J + j, 1)], evac_a)
                if not last:
                    act.wait_ge(raw_in[0], 16 * (m + 2))
                    act.activation(w_hi[:, 0, :], raw[:, 0, :], ACT.Copy).then_inc(hi_ready, 1)
                for e in range(2):
                    ada_out(ADA0 + 4 * m + e, 6 + e)
                if group_a:
                    act.wait_ge(ga_ready, 2 * j + 1)
                for c in range(NC):
                    wait_apart(act, strip_b, NC * m + c + 1)
                    if group_a:
                        chunk_out(c, 3, lambda o, w: sg[:, o:o + w],
                                  sg[:, SEQ:TOK].rearrange("p (b t) -> p b t", t=TB), ACT.Sigmoid,
                                  par[:, bass.ds(C_BIN + J + j, 1)], evac_b)
                    else:
                        chunk_out(c, 3, lambda o, w: gel[:, j, o:o + w],
                                  gel[:, j, SEQ:TOK].rearrange("p (b t) -> p b t", t=TB), ACT.Gelu_apprx_tanh,
                                  par[:, bass.ds(C_BIN + 3 * J + j, 1)], evac_b)
                if not last:
                    act.wait_ge(raw_in[1], 16 * (m + 2))
                    act.activation(w_hi[:, 1, :], raw[:, 1, :], ACT.Copy).then_inc(hi_ready, 1)
                for e in range(2):
                    ada_out(ADA0 + 4 * m + 2 + e, 6 + e)

            step(0, 0, True, False)
            with act.Fori(1, J) as j:
                step(j, j, True, False)
            with act.Fori(0, J - 1) as j:
                step(j + J, j, False, False)
            step(2 * J - 1, J - 1, False, True)

            def staged(n, dst, bank, r):
                act.wait_ge(st_tr, n + 1)
                act.activation(dst, ps[0:r, bank, :], ACT.Copy).then_inc(st_cp, 1)
                act.wait_ge(st_cp, n + 1)

            half_rows = 4 * (KA - 1)
            staged(0, stage[0:KA - 1, 2, :], 6, KA - 1)
            act.dma_start(ca_prompt[0, 0], stage[0:KA - 1, 2, :]).then_inc(staged_out, 16)
            for h in range(2):
                staged(1 + h, stage[0:half_rows, h, :], 7 - h, half_rows)
                act.dma_start(ca_sample[0, 4 * h:4 * h + 4].rearrange("b s c -> (b s) c"),
                              stage[0:half_rows, h, :]).then_inc(staged_out, 16)
            staged(3, stage[64:64 + KB - 1, 2, :], 7, KB - 1)
            act.dma_start(cb_prompt[0, 0], stage[64:64 + KB - 1, 2, :]).then_inc(staged_out, 16)
            staged(4, stage[32:32 + NB * (KB - 1), 2, :], 6, NB * (KB - 1))
            act.dma_start(cb_sample[0].rearrange("b s c -> (b s) c"),
                          stage[32:32 + NB * (KB - 1), 2, :]).then_inc(staged_out, 16)

            act.wait_ge(k_done, 3 + 8)
            act.wait_ge(conva_tap, 2 * KA * J)
            ga_t = [ga[:, n, 0:TOK] for n in range(4)]
            a_t, th_t, sx_t, m_t = ga_t
            for j in range(J):
                wait(act, q_done, j)
                for c in range(NC):
                    act.wait_ge(gate_a, NC * j + c + 1)
                    act.activation(th_t[:, c * CH:c * CH + CW[c]], ps[:, c, 0:CW[c]], ACT.Tanh, scale=0.5,
                                   bias=hb[:, 0, j:j + 1]).then_inc(evac_a, 1)
                wait(act, h_done, j)
                for c in range(NC):
                    act.wait_ge(gate_x, NC * j + c + 1)
                    act.activation(sx_t[:, c * CH:c * CH + CW[c]], ps[:, 3 + c, 0:CW[c]], ACT.Tanh, scale=0.5,
                                   bias=hb[:, 1, j:j + 1]).then_inc(evac_b, 1)
                act.wait_ge(evac_a, NC * (2 * J + j + 1))
                own(act.activation(a_t, th_t, ACT.Exp, scale=k4[:, 1, j:j + 1], bias=k4[:, 1, j:j + 1]))
                act.activation(th_t, th_t, ACT.Tanh, scale=k4[:, 0, j:j + 1], bias=k4[:, 0, j:j + 1])
                wait(act, yb_done, j)
                act.activation(m_t, a_t, ACT.Square).then_inc(a2_done, 1)
                act.wait_ge(q_done, j + 1)
                act.activation(m_t, m_t, ACT.Sqrt).then_inc(m_done, 1)

            for c in range(NC):
                t0, w = c * CH, CW[c]
                act.wait_ge(xc_done, c + 1)
                if c == 0:
                    act.wait_ge(staged_out, 16 * 5)
                else:
                    act.wait_ge(var_done, c)
                act.activation(sq[:, :, 0:w], conv_a[:, :, t0:t0 + w], ACT.Square).then_inc(sq_done, 1)
                act.wait_ge(var_done, c + 1)
                act.activation(rstd[:, t0:t0 + w], ps[:, 7, 0:w], ACT.Sqrt, bias=eps[:, :]).then_inc(sd_done, 1)
            act.wait_ge(st_tr, 6)
            act.activation(stage[0:9, 3, :], ps[0:9, 6, :], ACT.Copy).then_inc(st_cp, 1)
            act.wait_ge(st_cp, 6)
            act.dma_start(h_prompt[0], stage[0:1, 3, :]).then_inc(staged_out, 16)
            act.dma_start(h_sample[0], stage[1:9, 3, :]).then_inc(staged_out, 16)

            act.wait_ge(strip_b, NC * 2 * J)
            for j in range(J):
                act.wait_ge(yb_done, j + 1)
                act.activation(act_hi[:, J + j, 0:SEQ], gel[:, j, 0:SEQ], ACT.Copy)
                act.activation(stk[:, J + j, 0:SMP], gel[:, j, SEQ:TOK], ACT.Copy).then_inc(yhi_done, 1)
            for k in range(4):
                hi(W_OUT0 + k, k % 2, wb_hi[:, k, :], 16 * ((W_OUT0 + k) // 2 + 1))
            for c in range(NC):
                t0, w = c * CH, CW[c]
                act.wait_ge(xs_done, c + 1)
                wait(act, ya_done, c)
                for i in range(J):
                    last = act.activation(sq[:, i, 0:w], conv_a[:, i, t0:t0 + w], ACT.Sigmoid,
                                          scale=par[:, C_LNG + i:C_LNG + i + 1],
                                          bias=par[:, C_LNB + i:C_LNB + i + 1])
                last.then_inc(sig_done, 1)
                if c > 0:
                    hi(W_OUT0 + 2 + 2 * c, 0, wb_hi[:, 2 + 2 * c, :], 16 * ((W_OUT0 + 2 + 2 * c) // 2 + 1))
                    hi(W_OUT0 + 3 + 2 * c, 1, wb_hi[:, 3 + 2 * c, :], 16 * ((W_OUT0 + 3 + 2 * c) // 2 + 1))
                act.wait_ge(ya_done, c + 1)
                n = w if c < 2 else PROMPT2
                ins = act.activation(act_hi[:, 0:J, t0:t0 + n], conv_a[:, :, t0:t0 + n], ACT.Copy)
                if c == 2:
                    ins = act.activation(stk[:, 0:J, 0:SMP], conv_a[:, :, SEQ:TOK], ACT.Copy)
                ins.then_inc(yhi_done, 1)

            def gates_out(first, bank_p, bank_s):
                act.wait_ge(gt_mm, first + 1)
                act.activation(gt_p[:, :], ps[:, bank_p:bank_p + 2, :].rearrange("p a b -> p (a b)"), ACT.Copy).then_inc(gt_cp, 1)
                act.wait_ge(gt_mm, first + 2)
                act.activation(gt_s[:, :], ps[0:SMP, bank_s:bank_s + 2, :].rearrange("p a b -> p (a b)"), ACT.Copy).then_inc(gt_cp, 1)

            gates_out(0, 0, 2)
            strip_hi(W_MLP0, 0, strip_a, 0)
            strip_hi(W_MLP0 + 1, 1, strip_b, 0)

            act.wait_ge(staged_out, 16 * 7)
            act.wait_ge(sc_done, 2)
            for t in range(NT):
                n = NT + t
                if t > 0:
                    modulate(n - 1, t - 1, sc_f, M_SHF, 1, n - 1)

                def free():
                    act.wait_ge(rmw_done, t + 1)
                    act.wait_ge(tr_done, n)
                norm(n, t, x2, xn[:, 0, :], free)
            modulate(2 * NT - 1, NT - 1, sc_f, M_SHF, 1, 0)

            def mlp(b, last):
                n = W_MLP0 + 2 + 8 * b
                half = W_MLP0 // 2 + 1 + 4 * b

                def down(i, at, slot):
                    hi(n, slot, wb_hi[:, i, :], 16 * (half + at // 2 + 1))

                def strip(at, slot, count):
                    wait(act, up_done, count)
                    hi(n, slot, w_hi[:, slot, :], 16 * (half + at // 2 + 1))

                def relu_sq(i):
                    for c in range(NC):
                        q = 3 * i + c
                        r = relu[:, q % 2, 0:CW[c]]
                        act.wait_ge(up_done, 12 * b + q + 1)
                        wait(act, r2_done, 12 * b + q - 1)
                        act.activation(r, ps[:, 3 * (i % 2) + c, 0:CW[c]], ACT.Relu).then_inc(up_evac, 1)
                        act.wait_ge(up_evac, 12 * b + q + 1)
                        if c < 2:
                            act.activation(wb_hi[:, FI + i, c * CH:(c + 1) * CH], r, ACT.Square).then_inc(ffhi_done, 1)
                        else:
                            act.activation(wb_hi[:, FI + i, c * CH:SEQ], r[:, 0:PROMPT2], ACT.Square)
                            act.activation(stk[:, i, 0:SMP], r[:, PROMPT2:CW[c]], ACT.Square).then_inc(ffhi_done, 1)

                act.wait_ge(tile_done, NT * (b + 1))
                down(0, 0, 0)
                down(1, 1, 1)
                relu_sq(0)
                strip(2, 0, 12 * b + 3)
                down(2, 3, 1)
                down(3, 4, 0)
                relu_sq(1)
                strip(5, 1, 12 * b + 6)
                relu_sq(2)
                if not last:
                    strip(6, 0, 12 * b + 9)
                relu_sq(3)
                if not last:
                    strip(7, 1, 12 * b + 12)

            act.wait_ge(nlo_done, 2 * NT)
            mlp(0, False)
            gates_out(2, 6, 4)
            with act.Fori(1, NBLK - 1) as b:
                mlp(b, False)
            mlp(NBLK - 1, True)

            for t in range(NT):
                r = rows[t]
                act.wait_ge(rmw_done, NT * (NBLK + 1) - NT + t + 1)
                own(act.activation(xn[0:r, 0, :], x2[0:r, t, :], ACT.Square, accum_out=ssq[0:r, 0, t:t + 1]))
                act.activation(ssq[0:r, 1, t:t + 1], ssq[0:r, 0, t:t + 1], ACT.Sqrt, scale=1.0 / D,
                               bias=eps[0:r, :]).then_inc(std_done, 1)

        @block.vector
        def _(dve):
            ordered = [0]

            def own(ins):
                ordered[0] += 1
                ins.then_inc(dve_ord, 1)
                dve.wait_ge(dve_ord, ordered[0])

            dve.wait_ge(c_sig, 1)
            dve.tensor_tensor(ld_c[:, 1, :], ld_c[:, 0, :], ld_c[:, 1, :], ALU.mult).then_inc(c_silu, 1)
            dve.wait_ge(par_tr, 1)
            dve.tensor_copy(par[:, :], ps[:, 1, 0:N_PAR]).then_inc(par_cp, 1)
            dve.tensor_copy(caw[:, :], ps[:, 1, P:P + KA * J]).then_inc(par_cp, 1)
            dve.tensor_copy(h0[:, :, :], ps[:, 1, 256:288].rearrange("p (b j) -> p b j", j=J)).then_inc(par_cp, 1)
            dve.tensor_copy(rec_s[:, :, :, 0:KB - 1],
                            ps[:, 1, 288:384].rearrange("p (j b s) -> p j b s", j=J, s=KB - 1)).then_inc(par_cp, 1)
            for h in range(2):
                dve.wait_ge(sa_tr, h + 1)
                dve.tensor_copy(ga_s[:, :, 4 * h:4 * h + 4, 0:KA - 1],
                                ps[:, 2 + h, 0:480].rearrange("p (j b s) -> p j b s", j=J, s=KA - 1)).then_inc(sa_cp, 1)
            dve.wait_ge(par_cp, 1)
            dve.wait_ge(k_done, 1)
            e_, u_, ln_, w_ = (sp[:, n, :] for n in (1, 2, 3, 4))
            dve.tensor_scalar(u_, e_, 1.0, None, ALU.add).then_inc(k_done, 1)
            dve.wait_ge(k_done, 3)
            own(dve.tensor_scalar(w_, u_, -1.0, None, ALU.add))
            own(dve.tensor_tensor(e_, e_, w_, ALU.subtract))
            own(dve.reciprocal(w_, u_))
            own(dve.tensor_tensor(e_, e_, w_, ALU.mult))
            own(dve.tensor_tensor(ln_, ln_, e_, ALU.add))
            own(dve.tensor_scalar(w_, par[:, C_LAM:C_LAM + J], -1.0, 0.0, ALU.mult, ALU.max))
            own(dve.tensor_tensor(ln_, ln_, w_, ALU.add))
            dve.tensor_scalar(k4[:, 0, :], ln_, 4.0, None, ALU.mult).then_inc(k_done, 2)
            dve.tensor_scalar(k4[:, 1, :], ln_, -4.0, None, ALU.mult).then_inc(k_done, 2)
            dve.tensor_scalar(hb[:, 0, :], par[:, C_BGA:C_BGA + J], 0.5, None, ALU.mult).then_inc(k_done, 2)
            dve.tensor_scalar(hb[:, 1, :], par[:, C_BGX:C_BGX + J], 0.5, None, ALU.mult).then_inc(k_done, 2)

            def scales(dst, row0, col):
                g = par[:, col:col + KD].unsqueeze(2).broadcast_to([P, KD, 9])
                dve.scalar_tensor_tensor(out=dst[:, :, :], in0=mod[:, row0:row0 + KD, :], scalar=1.0,
                                         in1=g, op0=ALU.add, op1=ALU.mult).then_inc(sc_done, 1)

            def scale_rows(n, t, src, dst):
                r = rows[t]
                dve.wait_ge(std_done, n + 1)
                own(dve.reciprocal(ssq[0:r, 2, t:t + 1], ssq[0:r, 1, t:t + 1]))
                dve.tensor_scalar(dst, src[0:r, t, :], ssq[0:r, 2, t:t + 1], None, ALU.mult).then_inc(xn_done, 1)

            def modulate(n, t, scale, shift0, slot, free):
                hf = xn[:, slot, :].rearrange("p (k c) -> p k c", c=P)
                dve.wait_ge(tr_done, n + 1)
                wait(dve, nhi_done, free)
                b = bank_pair(n)
                if t < NT - 1:
                    for k in range(4):
                        last = dve.tensor_scalar(hf[:, k, :], ps[:, b, k * P:(k + 1) * P], scale[:, k, 0:1],
                                                 mod[:, shift0 + k, 0:1], ALU.mult, ALU.add)
                    last.then_inc(hf_d, 1)
                    dve.wait_ge(hf_a, hfa(n))
                else:
                    hs = hf[:, :, 0:SMP].rearrange("p k (b t) -> p k b t", t=TB)
                    src = ps[:, b:b + 2, :].rearrange("p a (k c) -> p (a k) c", c=P)[:, :, 0:SMP].rearrange(
                        "p k (b t) -> p k b t", t=TB)
                    for k in range(KD):
                        last = dve.tensor_tensor(hs[:, k], src[:, k],
                                                 scale[:, k, 1:9].unsqueeze(2).broadcast_to([P, NB, TB]), ALU.mult)
                    own(last)
                    for k in range(KD):
                        last = dve.tensor_tensor(hs[:, k], hs[:, k],
                                                 mod[:, shift0 + k, 1:9].unsqueeze(2).broadcast_to([P, NB, TB]), ALU.add)
                    last.then_inc(hf_d, 1)
                dve.wait_ge(nhi_done, n + 1)
                cols = slice(t * P, t * P + rows[t])
                dve.tensor_tensor(act_lo[:, :, cols], hf[:, :, 0:rows[t]], act_hi[:, :, cols].bitcast(F32),
                                  ALU.subtract).then_inc(nlo_done, 1)

            for t in range(3):
                scale_rows(t, t, x2, x2[0:rows[t], t, :])
            dve.wait_ge(ada_evac, ADA0)
            scales(sc_m, M_SCM, C_GMIX)
            dve.wait_ge(sc_done, 1)
            for t in range(NT):
                if t + 3 < NT:
                    scale_rows(t + 3, t + 3, x2, x2[0:rows[t + 3], t + 3, :])
                modulate(t, t, sc_m, M_SHM, t % 2, t - 1)

            def conv(src, src_s, width, taps, out, j, done, bias_col, base):
                out_s = out[:, j, SEQ:TOK].rearrange("p (b t) -> p b t", t=TB)
                for k in range(width):
                    w = taps(k)
                    win, win_s = src[:, j, k:k + SEQ], src_s[:, j, :, k:k + TB]
                    if k == 0:
                        bias = par[:, bass.ds(bias_col + j, 1)]
                        dve.tensor_scalar(out[:, j, 0:SEQ], win, w, bias, ALU.mult, ALU.add).then_inc(done, 1)
                        dve.tensor_scalar(out_s, win_s, w, bias, ALU.mult, ALU.add).then_inc(done, 1)
                    else:
                        dve.wait_ge(done, 2 * width * j + 2 * k - 1 + base)
                        dve.scalar_tensor_tensor(out=out[:, j, 0:SEQ], in0=win, scalar=w, in1=out[:, j, 0:SEQ],
                                                 op0=ALU.mult, op1=ALU.add).then_inc(done, 1)
                        dve.wait_ge(done, 2 * width * j + 2 * k + base)
                        dve.scalar_tensor_tensor(out=out_s, in0=win_s, scalar=w, in1=out_s,
                                                 op0=ALU.mult, op1=ALU.add).then_inc(done, 1)

            dve.wait_ge(sa_cp, 2)
            with dve.Fori(0, J) as j:
                dve.wait_ge(ga_ready, 2 * j + 3)
                conv(ga, ga_s, KA, lambda k: caw[:, bass.ds(j + k * J, 1)], conv_a, j, conva_tap, C_CAB, 0)
            dve.wait_ge(conva_tap, 2 * KA * J)
            with dve.Fori(0, J) as j:
                dve.wait_ge(evac_a, NC * (J + 1) + NC * j)
                conv(rec, rec_s, KB, lambda k: par[:, bass.ds(C_CBW + j + k * J, 1)], cb, j, convb_tap, C_CBB, 0)

            a_t, th_t, sx_t, m_t = (ga[:, n, 0:TOK] for n in range(4))

            def firsts(ap):
                return ap[:, SEQ:TOK].rearrange("p (b t) -> p b t", t=TB)[:, :, 0]

            for j in range(J):
                dve.wait_ge(a2_done, j + 1)
                dve.scalar_tensor_tensor(out=m_t, in0=m_t, scalar=1.0, in1=th_t, op0=ALU.add,
                                         op1=ALU.mult).then_inc(q_done, 1)
                own(dve.scalar_tensor_tensor(out=sx_t, in0=sx_t, scalar=1.0, in1=cb[:, j, :], op0=ALU.add,
                                             op1=ALU.mult))
                own(dve.tensor_tensor(tmp8[:, :], firsts(a_t), h0[:, :, j], ALU.mult))
                own(dve.memset(firsts(a_t), 0.0))
                dve.wait_ge(m_done, j + 1)
                own(dve.memset(m_t[:, 0:1], 1.0))
                own(dve.scalar_tensor_tensor(out=sx_t, in0=m_t, scalar=0.5, in1=sx_t, op0=ALU.mult,
                                             op1=ALU.mult))
                own(dve.tensor_tensor(firsts(sx_t), firsts(sx_t), tmp8[:, :], ALU.add))
                dve.tensor_tensor_scan(m_t, a_t, sx_t, 0.0, ALU.mult, ALU.add).then_inc(h_done, 1)
                dve.wait_ge(h_done, j + 1)
                dve.tensor_copy(h_end[:, j, 0:1], m_t[:, SEQ - 1:SEQ])
                dve.tensor_copy(h_end[:, j, 1:9], m_t[:, SEQ:TOK].rearrange("p (b t) -> p b t", t=TB)[:, :, TB - 1])
                dve.tensor_tensor(gel[:, j, :], m_t, gel[:, j, :], ALU.mult).then_inc(yb_done, 1)

            def over_tiles(ap, w):
                return ap.unsqueeze(1).broadcast_to([P, J, w])

            for c in range(NC):
                t0, w = c * CH, CW[c]
                dve.wait_ge(mean_done, c + 1)
                dve.tensor_tensor(conv_a[:, :, t0:t0 + w], conv_a[:, :, t0:t0 + w], over_tiles(ps[:, 6, 0:w], w),
                                  ALU.subtract).then_inc(xc_done, 1)
            for j in range(J):
                dve.wait_ge(yhi_done, j + 1)
                dve.tensor_tensor(act_lo[:, J + j, 0:SEQ], gel[:, j, 0:SEQ], act_hi[:, J + j, 0:SEQ].bitcast(F32),
                                  ALU.subtract)
                dve.tensor_tensor(stk[:, J + j, SMP:P], gel[:, j, SEQ:TOK], stk[:, J + j, 0:SMP].bitcast(F32),
                                  ALU.subtract).then_inc(ylo_done, 1)

            def normalise(c):
                t0, w = c * CH, CW[c]
                dve.wait_ge(sd_done, c + 1)
                own(dve.reciprocal(rstd[:, t0:t0 + w], rstd[:, t0:t0 + w]))
                dve.tensor_tensor(conv_a[:, :, t0:t0 + w], conv_a[:, :, t0:t0 + w], over_tiles(rstd[:, t0:t0 + w], w),
                                  ALU.mult).then_inc(xs_done, 1)

            normalise(0)
            for c in range(NC):
                t0, w = c * CH, CW[c]
                if c + 1 < NC:
                    normalise(c + 1)
                dve.wait_ge(sig_done, c + 1)
                for i in range(J):
                    last = dve.tensor_scalar(conv_a[:, i, t0:t0 + w], conv_a[:, i, t0:t0 + w],
                                             par[:, C_LNG + i:C_LNG + i + 1], par[:, C_LNB + i:C_LNB + i + 1],
                                             ALU.mult, ALU.add)
                own(last)
                dve.tensor_tensor(conv_a[:, :, t0:t0 + w], conv_a[:, :, t0:t0 + w], sq[:, :, 0:w],
                                  ALU.mult).then_inc(ya_done, 1)
                dve.wait_ge(yhi_done, J + c + 1)
                n = w if c < 2 else PROMPT2
                ins = dve.tensor_tensor(act_lo[:, 0:J, t0:t0 + n], conv_a[:, :, t0:t0 + n],
                                        act_hi[:, 0:J, t0:t0 + n].bitcast(F32), ALU.subtract)
                if c == 2:
                    ins = dve.tensor_tensor(stk[:, 0:J, SMP:P], conv_a[:, :, SEQ:TOK],
                                            stk[:, 0:J, 0:SMP].bitcast(F32), ALU.subtract)
                ins.then_inc(ylo_done, 1)

            dve.wait_ge(ada_evac, 48)
            scales(sc_f, M_SCF, C_GFFN)

            def add_tile(t, bank, first):
                src = ps[:, bank:bank + 2, :].rearrange("p a b -> p (a b)")
                if t < NT - 1:
                    dve.tensor_tensor(src, src, gt_p[:, :], ALU.mult).then_inc(gated, 1)
                    dve.wait_ge(gated, first + 1)
                    dve.tensor_tensor(x2[:, t, :], x2[:, t, :], src, ALU.add).then_inc(rmw_done, 1)
                else:
                    dve.tensor_tensor(src[0:SMP], src[0:SMP], gt_s[:, :], ALU.mult).then_inc(gated, 1)
                    dve.tensor_tensor(src[SMP:P], src[SMP:P], gt_s[:, :], ALU.mult).then_inc(gated, 1)
                    dve.wait_ge(gated, first + 2)
                    dve.tensor_tensor(x2[0:SMP, t, :], x2[0:SMP, t, :], src[0:SMP], ALU.add).then_inc(gated, 1)
                    dve.wait_ge(gated, first + 3)
                    dve.tensor_tensor(x2[0:SMP, t, :], x2[0:SMP, t, :], src[SMP:P], ALU.add).then_inc(rmw_done, 1)

            GATED = NT - 1 + 3
            dve.wait_ge(gt_cp, 2)
            dve.wait_ge(sc_done, 2)
            for t in range(NT):
                n = NT + t
                dve.wait_ge(x_in[t], 32)
                dve.wait_ge(tile_done, t + 1)
                add_tile(t, 0 if t % 2 == 0 else 2, t)
                if t > 0:
                    modulate(n - 1, t - 1, sc_f, M_SHF, 1, n - 1)
                dve.wait_ge(tr_done, n)
                scale_rows(n, t, x2, xn[0:rows[t], 0, :])
            modulate(2 * NT - 1, NT - 1, sc_f, M_SHF, 1, 2 * NT - 1)

            def squares(b):
                for q in range(12):
                    i, c = q // NC, q % NC
                    r, f = relu[:, q % 2, 0:CW[c]], relu2[:, q % 2, 0:CW[c]]
                    dve.wait_ge(up_evac, 12 * b + q + 1)
                    dve.tensor_tensor(f, r, r, ALU.mult).then_inc(r2_done, 1)
                    dve.wait_ge(r2_done, 12 * b + q + 1)
                    dve.wait_ge(ffhi_done, 12 * b + q + 1)
                    n = CH if c < 2 else PROMPT2
                    cols = slice(c * CH, c * CH + n)
                    ins = dve.tensor_tensor(wb_lo[:, FI + i, cols], f[:, 0:n], wb_hi[:, FI + i, cols].bitcast(F32),
                                            ALU.subtract)
                    if c == 2:
                        ins = dve.tensor_tensor(stk[:, i, SMP:P], f[:, PROMPT2:CW[c]], stk[:, i, 0:SMP].bitcast(F32),
                                                ALU.subtract)
                    ins.then_inc(fflo_done, 1)

            def mlp(b):
                squares(b)
                if isinstance(b, int) and b == 0:
                    dve.wait_ge(gt_cp, 4)
                for t in range(NT):
                    dve.wait_ge(tile_done, NT * (b + 1) + t + 1)
                    add_tile(t, 6 if t % 2 == 0 else 4, GATED * (b + 1) + t)

            mlp(0)
            with dve.Fori(1, NBLK) as b:
                mlp(b)
            dve.wait_ge(gf_in, 16)
            for t in range(NT):
                r = rows[t]
                dve.wait_ge(std_done, 2 * NT + t + 1)
                own(dve.reciprocal(ssq[0:r, 2, t:t + 1], ssq[0:r, 1, t:t + 1]))
                dve.scalar_tensor_tensor(out=x2[0:r, t, :], in0=x2[0:r, t, :], scalar=ssq[0:r, 2, t:t + 1],
                                         in1=raw[0:r, 0, :], op0=ALU.mult, op1=ALU.mult).then_inc(fin_y, 1)

        @block.tensor
        def _(pe):
            mm = nc.tensor.matmul
            pe.wait_ge(pool_set, 1)
            pe.wait_ge(c_silu, 1)
            for k in range(KD):
                last = nc.tensor.transpose(ps[:, 0, 9 * k:9 * k + 9], ld_c[0:9, 1, k * P:(k + 1) * P], ident[0:9, 0:9])
            last.then_inc(c_tr, 1)
            pe.wait_ge(par_in, 16 * N_ROWS_PAR)
            nc.tensor.transpose(ps[:, 1, 0:N_PAR], ld_par[0:N_PAR, 0, :], ident[0:N_PAR, 0:N_PAR])
            nc.tensor.transpose(ps[:, 1, P:P + KA * J], ld_par[0:KA * J, 1, :], ident[0:KA * J, 0:KA * J])
            nc.tensor.transpose(ps[:, 1, 256:288], ld_par[0:32, 2, :], ident[0:32, 0:32])
            for j in range(J):
                last = nc.tensor.transpose(ps[:, 1, 288 + 24 * j:312 + 24 * j], ld_sb[:, j * P:(j + 1) * P],
                                           ident[0:24, 0:24])
            last.then_inc(par_tr, 1)
            pe.wait_ge(sa_in, 32)
            for h in range(2):
                for j in range(J):
                    last = nc.tensor.transpose(ps[:, 2 + h, 120 * j:120 * j + 120], ld_sa[:, h, j * P:(j + 1) * P],
                                               ident[0:120, 0:120])
                last.then_inc(sa_tr, 1)

            def ada(e, bank, weights):
                wait(pe, ada_evac, e - 1)
                for k in range(KD):
                    last = mm(ps[:, bank, 0:9], weights(k), cT[:, k, :], start=(k == 0), stop=(k == KD - 1))
                last.then_inc(ada_done, 1)

            pe.wait_ge(c_cp, 1)
            for e in range(ADA0):
                pe.wait_ge(ada0_in[e // 4], 16)
                ada(e, 6 + e % 2, lambda k: ada0[:, e // 4, k, (e % 4) * P:(e % 4 + 1) * P])

            def turn(n, t, src):
                pe.wait_ge(xn_done, n + 1)
                if n >= 2:
                    pe.wait_ge(hf_d, n - 1)
                    pe.wait_ge(hf_a, hfa(n - 2))
                b, r = bank_pair(n), rows[t]
                for k in range(KD):
                    last = nc.tensor.transpose(ps[:, b + k // 4, (k % 4) * P:(k % 4) * P + r],
                                               src[0:r, k * P:(k + 1) * P], ident[0:r, 0:r])
                last.then_inc(tr_done, 1)

            def strip(slot, bank, c, done):
                for k in range(KD):
                    wh, wl = w_hi[:, slot, k * P:(k + 1) * P], w_lo[:, slot, k * P:(k + 1) * P]
                    xh, xl = act_hi[:, k, c * CH:c * CH + CW[c]], act_lo[:, k, c * CH:c * CH + CW[c]]
                    out = ps[:, bank + c, 0:CW[c]]
                    mm(out, wh, xh, start=(k == 0), stop=False)
                    mm(out, wh, xl, start=False, stop=False)
                    last = mm(out, wl, xh, start=False, stop=(k == KD - 1))
                last.then_inc(done, 1)

            def ada_strip(e, bank):
                pe.wait_ge(ada_in, 16 * (e - ADA0 + 1))
                ada(e, bank, lambda k: raw_ada[:, k, :])

            def step(m, first):
                for s, bank, done, out in ((0, 0, strip_a, evac_a), (1, 3, strip_b, evac_b)):
                    pe.wait_ge(hi_ready, 2 * m + s + 1)
                    pe.wait_ge(lo_ready, 2 * m + s + 1)
                    for c in range(NC):
                        if first and s == 0:
                            for t in ((0, 1, 2, 3, 4), (5, 6, 7), (8,))[c]:
                                turn(t, t, x2[:, t, :])
                            pe.wait_ge(nhi_done, min(3 * c + 3, NT))
                            pe.wait_ge(nlo_done, min(3 * c + 3, NT))
                        if not first:
                            pe.wait_ge(out, NC * m - 2 + c)
                        strip(s, bank, c, done)
                        if c == 0 and not (first and s == 0):
                            ada_strip(ADA0 + 4 * m + 2 * s, 6)
                    if first and s == 0:
                        ada_strip(ADA0, 6)
                    ada_strip(ADA0 + 4 * m + 2 * s + 1, 7)

            pe.wait_ge(par_cp, 4)
            pe.wait_ge(sa_cp, 2)
            pe.wait_ge(ada_evac, ADA0)
            step(0, True)
            with pe.Fori(1, 2 * J) as m:
                step(m, False)

            def turn_state(n, bank, r, src):
                wait(pe, st_cp, n - 1)
                for j in range(J):
                    last = nc.tensor.transpose(ps[0:r, bank, j * P:(j + 1) * P], src(j), ident[:, :])
                last.then_inc(st_tr, 1)

            pe.wait_ge(ada_evac, 48)
            pe.wait_ge(ga_ready, 2 * J + 1)
            turn_state(0, 6, KA - 1, lambda j: ga[:, j, SEQ:GA_P])
            pe.wait_ge(tails, 1)
            for h in range(2):
                turn_state(1 + h, 7 - h, 4 * (KA - 1), lambda j: tail_a[:, j, 120 * h:120 * h + 120])
            pe.wait_ge(evac_a, 2 * J * NC)
            turn_state(3, 7, KB - 1, lambda j: rec[:, j, SEQ:RB_P])
            turn_state(4, 6, NB * (KB - 1), lambda j: tail_b[:, j, :])

            pe.wait_ge(wg_in, 64)
            for j in range(J):
                pe.wait_ge(convb_tap, 2 * KB * (j + 1))
                for g, done, out in ((0, gate_a, evac_a), (1, gate_x, evac_b)):
                    for c in range(NC):
                        pe.wait_ge(out, NC * (2 * J + j) - 2 + c)
                        mm(ps[:, 3 * g + c, 0:CW[c]], wg[:, g, j, :], cb[:, j, c * CH:c * CH + CW[c]],
                           start=True, stop=True).then_inc(done, 1)

            def mean(c, bank, src, done):
                for j in range(J):
                    last = mm(ps[:, bank, 0:CW[c]], mean_w[:, :], src(j), start=(j == 0), stop=(j == J - 1))
                last.then_inc(done, 1)

            def mean_a(c):
                wait(pe, xc_done, c)
                mean(c, 6, lambda j: conv_a[:, j, c * CH:c * CH + CW[c]], mean_done)

            def var_a(c):
                pe.wait_ge(sq_done, c + 1)
                wait(pe, sd_done, c)
                mean(c, 7, lambda j: sq[:, j, 0:CW[c]], var_done)

            pe.wait_ge(conva_tap, 2 * KA * J)
            pe.wait_ge(st_cp, 5)
            mean_a(0)
            mean_a(1)
            var_a(0)
            mean_a(2)
            var_a(1)
            var_a(2)
            pe.wait_ge(yb_done, J)
            pe.wait_ge(xc_done, NC)
            for j in range(J):
                last = nc.tensor.transpose(ps[0:9, 6, j * P:(j + 1) * P], h_end[:, j, :], ident[:, :])
            last.then_inc(st_tr, 1)

            def gates(row0, bank_p, bank_s):
                for k in range(KD):
                    g = mod[:, row0 + k, :]
                    last = mm(ps[:, bank_p + k // 4, (k % 4) * P:(k % 4 + 1) * P], g[:, 0:1].broadcast_to([P, P]),
                              ident[:, :], start=True, stop=True)
                last.then_inc(gt_mm, 1)
                for k in range(KD):
                    last = mm(ps[0:SMP, bank_s + k // 4, (k % 4) * P:(k % 4 + 1) * P],
                              gt_tok[:, int(row0 == M_GTF), k, :], ident[:, :],
                              start=True, stop=True)
                last.then_inc(gt_mm, 1)

            pe.wait_ge(evac_a, 3 * J * NC)
            pe.wait_ge(evac_b, 3 * J * NC)
            pe.wait_ge(ya_done, NC)
            pe.wait_ge(tails, 2)
            gates(M_GTM, 0, 2)

            def tile_product(t, bank, n_k, act_k, ready):
                for k in range(n_k):
                    ready(k)
                    halves = [(ps[:, bank + h, :], wb_hi[:, k, h * 512:(h + 1) * 512],
                               wb_lo[:, k, h * 512:(h + 1) * 512]) for h in range(2)]
                    end = k == n_k - 1
                    if t < NT - 1:
                        ah, al = act_k(k)
                        for out, wh, wl in halves:
                            mm(out, ah, wh, start=(k == 0), stop=False)
                            mm(out, ah, wl, start=False, stop=False)
                        for out, wh, wl in halves:
                            last = mm(out, al, wh, start=False, stop=end)
                    else:
                        for out, wh, wl in halves:
                            mm(out, stk[:, k, :], wh, start=(k == 0), stop=False)
                            last = mm(out, stk[:, k, :], wl, start=False, stop=end)
                last.then_inc(tile_done, 1)

            pe.wait_ge(gt_cp, 2)
            pe.wait_ge(yhi_done, J + NC)
            pe.wait_ge(ylo_done, J + NC)

            def w_out_ready(k):
                pe.wait_ge(hi_ready, W_OUT0 + k + 1)
                pe.wait_ge(lo_ready, W_OUT0 + k + 1)

            for t in range(NT):
                wait(pe, rmw_done, t - 1)
                tile_product(t, 0 if t % 2 == 0 else 2, KD,
                             lambda k: (act_hi[:, k, t * P:(t + 1) * P], act_lo[:, k, t * P:(t + 1) * P]),
                             w_out_ready if t == 0 else lambda k: None)
                if t > 0:
                    if t == 1:
                        pe.wait_ge(st_cp, 6)
                    turn(NT + t - 1, t - 1, xn[:, 0, :])

            def mlp(b, first):
                n = W_MLP0 + 8 * b
                for i in range(FI):
                    at = (0, 1, 4, 7)[i]
                    pe.wait_ge(hi_ready, n + at + 1)
                    pe.wait_ge(lo_ready, n + at + 1)
                    if i == 1:
                        pe.wait_ge(rmw_done, NT * b + NT - 1)
                    for c in range(NC):
                        if first and i == 0:
                            if c == 0:
                                pe.wait_ge(rmw_done, NT)
                            if c == 2:
                                turn(2 * NT - 1, NT - 1, xn[:, 0, :])
                            pe.wait_ge(nhi_done, NT + min(3 * c + 3, NT))
                            pe.wait_ge(nlo_done, NT + min(3 * c + 3, NT))
                        wait(pe, up_evac, 12 * b + 3 * i + c - 5)
                        strip(i % 2, 3 * (i % 2), c, up_done)
                if first:
                    pe.wait_ge(up_evac, 12)
                    gates(M_GTF, 6, 4)
                    pe.wait_ge(gt_cp, 4)
                for t in range(NT):
                    pe.wait_ge(rmw_done, NT * (b + 1) + max(t - 1, 0))
                    if t == 1:
                        pe.wait_ge(up_evac, 12 * b + 12)

                    def ready(k):
                        if t == 0:
                            pe.wait_ge(hi_ready, n + (3, 4, 6, 7)[k])
                            pe.wait_ge(lo_ready, n + (3, 4, 6, 7)[k])
                        if t % NC == 0:
                            pe.wait_ge(ffhi_done, 12 * b + 3 * k + t // NC + 1)
                            pe.wait_ge(fflo_done, 12 * b + 3 * k + t // NC + 1)
                    tile_product(t, 6 if t % 2 == 0 else 4, FI,
                                 lambda k: (wb_hi[:, FI + k, t * P:(t + 1) * P], wb_lo[:, FI + k, t * P:(t + 1) * P]),
                                 ready)

            mlp(0, True)
            with pe.Fori(1, NBLK) as b:
                mlp(b, False)


def hfa(n):
    return n + 1 - (n >= NT - 1) - (n >= 2 * NT - 1)


_INS = ["x_prompt", "x_sample", "c_prompt", "c_sample", "state_conv_a", "state_conv_b", "state_lru_h",
        "w_ada", "b_ada", "g_mix", "w_in", "b_in", "conv_a_w", "conv_a_b", "ln_a_g", "ln_a_b", "conv_b_w",
        "conv_b_b", "w_gate_a", "b_gate_a", "w_gate_x", "b_gate_x", "lru_lambda", "w_out", "g_ffn", "w_up",
        "w_down", "g_final"]
_OUTS = [(1, SEQ, D), (NB, TB, D), (1, 1, KA - 1, WA), (1, 1, KB - 1, WA), (1, 1, WA),
         (1, NB, KA - 1, WA), (1, NB, KB - 1, WA), (1, NB, WA)]


def kernel(**inputs):
    import numpy as _np
    import concourse.bacc as _bacc
    from concourse.bass_utils import run_bass_kernel_spmd as _run

    nc = _bacc.Bacc("TRN2", target_bir_lowering=False, num_devices=1, dynamic_dma_scratch_size=1024)
    arrays, args = {}, []
    for name in _INS:
        a = _np.ascontiguousarray(inputs[name])
        arrays[f"in_{name}"] = a
        args.append(nc.dram_tensor(f"in_{name}", a.shape, mybir.dt.from_np(a.dtype), kind="ExternalInput").ap())
    for i, shape in enumerate(_OUTS):
        args.append(nc.dram_tensor(f"out_{i}", shape, F32, kind="ExternalOutput").ap())
    trunk(nc, *args)
    r = _run(nc, [arrays], core_ids=[0])
    return tuple(r.results[0][f"out_{i}"] for i in range(len(_OUTS)))
```

```python
from contextlib import ExitStack

import concourse.bass as bass
from concourse import mybir

F32 = mybir.dt.float32
F32R = mybir.dt.float32r
ALU = mybir.AluOpType
ACT = mybir.ActivationFunctionType

P = 128
D = 1024
KD = D // P
SEQ = 1024
NB, TB = 8, 8
SMP = NB * TB
TOK = SEQ + SMP
NT = SEQ // P + 1
WA = 512
J = WA // P
KA, KB = 31, 4
FF = 4096
FI = 4
NBLK = FF // (FI * P)
CH = 384
NC = 3
CW = [CH, CH, TOK - 2 * CH]
PROMPT2 = SEQ - 2 * CH
GA_P = KA - 1 + SEQ
GA_S = KA - 1 + TB
GA_W = GA_P + NB * GA_S
RB_P = KB - 1 + SEQ
RB_S = KB - 1 + TB
RB_W = RB_P + NB * RB_S
EPS = 1e-6
N_ROWS_PAR = 15

C_BIN, C_BADA, C_GMIX, C_GFFN, C_CAB, C_LNG, C_LNB, C_CBB, C_BGA, C_BGX, C_LAM, C_CBW = (
    0, 16, 64, 72, 80, 84, 88, 92, 96, 100, 104, 108)
N_PAR = C_CBW + KB * J
M_SHM, M_SCM, M_GTM, M_SHF, M_SCF, M_GTF = (8 * i for i in range(6))
GW = 512
ADA0 = 4
ADA_G = 6 * D // GW
C_LO = 32
W_OUT0 = 16
W_MLP0 = W_OUT0 + KD


def trunk(nc, x_prompt, x_sample, c_prompt, c_sample, state_conv_a, state_conv_b, state_lru_h,
          w_ada, b_ada, g_mix, w_in, b_in, conv_a_w, conv_a_b, ln_a_g, ln_a_b, conv_b_w, conv_b_b,
          w_gate_a, b_gate_a, w_gate_x, b_gate_x, lru_lambda, w_out, g_ffn, w_up, w_down, g_final,
          y_prompt, y_sample, ca_prompt, cb_prompt, h_prompt, ca_sample, cb_sample, h_sample):
    ctx = ExitStack()
    with ctx:
        def sb(name, shape, dt=F32):
            return ctx.enter_context(nc.sbuf_tensor(name, shape, dt))

        def shared(*layouts):
            out = {}
            for n, layout in enumerate(layouts):
                scope = ExitStack()
                for name, shape, dt in layout:
                    out[name] = scope.enter_context(nc.sbuf_tensor(name, shape, dt))
                if n < len(layouts) - 1:
                    scope.close()
                else:
                    ctx.push(scope)
            return out

        def sem(name):
            return ctx.enter_context(nc.semaphore(name))

        ident = sb("ident", [P, P])
        mean_w = sb("mean_w", [P, P])
        par = sb("par", [P, N_PAR])
        caw = sb("caw", [P, KA * J])
        mod = sb("mod", [P, 48, 9])
        sc_m = sb("sc_m", [P, KD, 9])
        sc_f = sb("sc_f", [P, KD, 9])
        pick = sb("pick", [P, 9])
        h_end = sb("h_end", [P, J, 9])
        h0 = sb("h0", [P, NB, J])
        hb = sb("hb", [P, 2, J])
        k4 = sb("k4", [P, 2, J])
        sp = sb("sp", [P, 5, J])
        eps = sb("eps", [P, 1])
        ssq = sb("ssq", [P, 3, NT])
        tmp8 = sb("tmp8", [P, NB])
        raw = sb("raw", [P, 2, D])
        tail_b = sb("tail_b", [P, J, NB * (KB - 1)])
        rr = shared([("tail_a", [P, J, NB * (KA - 1)], F32)],
                    [("gt_tok", [P, 2, KD, SMP], F32)])
        tail_a, gt_tok = rr["tail_a"], rr["gt_tok"]
        w_hi = sb("w_hi", [P, 2, D], F32R)
        w_lo = sb("w_lo", [P, 2, D], F32R)
        stk = sb("stk", [P, KD, P], F32R)
        rx = shared([("conv_a", [P, J, TOK], F32), ("gel", [P, J, TOK], F32)],
                    [("x2", [P, NT, D], F32)])
        conv_a, gel, x2 = rx["conv_a"], rx["gel"], rx["x2"]
        rh = shared([("ada0", [P, ADA0, KD, GW], F32)],
                    [("act_hi", [P, KD, TOK], F32R), ("act_lo", [P, KD, TOK], F32R)])
        ada0, act_hi, act_lo = rh["ada0"], rh["act_hi"], rh["act_lo"]
        rw = shared([("ld_sa", [120, 2, WA], F32), ("ld_c", [9, 2, D], F32),
                     ("ld_par", [P, 3, P], F32), ("ld_sb", [NB * (KB - 1), WA], F32)],
                    [("cb", [P, J, TOK], F32), ("ga", [P, J, GA_W], F32), ("rec", [P, J, RB_W], F32),
                     ("sg", [P, TOK], F32), ("ada_rows", [P, GW], F32)],
                    [("aw_hi", [P, 2, D], F32R), ("aw_lo", [P, 2, D], F32R)],
                    [("wb_hi", [P, KD, D], F32R), ("wb_lo", [P, KD, D], F32R)])
        ld_sa, ld_c, ld_par, ld_sb = (rw[n] for n in ("ld_sa", "ld_c", "ld_par", "ld_sb"))
        cb, ga, rec, sg, wb_hi, wb_lo = (rw[n] for n in ("cb", "ga", "rec", "sg", "wb_hi", "wb_lo"))
        ada_rows, aw_hi, aw_lo = rw["ada_rows"], rw["aw_hi"], rw["aw_lo"]
        rg = shared([("wg", [P, 2, J, P], F32)], [("rstd", [P, TOK], F32)],
                    [("gt_p", [P, D], F32), ("gt_s", [SMP, D], F32)])
        wg, rstd, gt_p, gt_s = rg["wg"], rg["rstd"], rg["gt_p"], rg["gt_s"]
        rt = shared([("sq", [P, J, CH], F32)], [("relu", [P, 2, CH], F32), ("relu2", [P, 2, CH], F32)],
                    [("stage", [P, 4, WA], F32)], [("raw_ada", [P, 2, 2 * GW], F32)], [("xn", [P, 2, D], F32)])
        raw_ada = rt["raw_ada"]
        sq, relu, relu2, stage, xn = rt["sq"], rt["relu"], rt["relu2"], rt["stage"], rt["xn"]
        ps = ctx.enter_context(nc.psum_tensor("ps", [P, 8, 512], F32))

        c_in, par_in, sb_in, sa_in, wg_in = (sem(n) for n in ("c_in", "par_in", "sb_in", "sa_in", "wg_in"))
        x_in = [sem(f"x_in{t}") for t in range(NT)]
        ada0_in = [sem(f"ada0_in{g}") for g in range(4)]
        raw_in = [sem("raw_in0"), sem("raw_in1")]
        gf_in, stored = sem("gf_in"), sem("stored")
        ada_in = [sem("ada_in0"), sem("ada_in1")]
        staged_out = sem("staged_out")
        pool_set = sem("pool_set")
        pool_ord = sem("pool_ord")
        act_ord, dve_ord = sem("act_ord"), sem("dve_ord")
        c_sig, c_silu, c_tr, c_cp = sem("c_sig"), sem("c_silu"), sem("c_tr"), sem("c_cp")
        par_tr, par_cp, sa_tr, sa_cp = sem("par_tr"), sem("par_cp"), sem("sa_tr"), sem("sa_cp")
        ada0_hi, ada0_lo, ada0_used = sem("ada0_hi"), sem("ada0_lo"), sem("ada0_used")
        ada_hi, ada_lo, ada_used = sem("ada_hi"), sem("ada_lo"), sem("ada_used")
        rows_out, ada_tr, ada_evac = sem("rows_out"), sem("ada_tr"), sem("ada_evac")
        c_zero = sem("c_zero")
        ssq_done, std_done, xn_done = sem("ssq_done"), sem("std_done"), sem("xn_done")
        tr_done, hf_d, hf_a = sem("tr_done"), sem("hf_d"), sem("hf_a")
        nhi_done, nlo_done = sem("nhi_done"), sem("nlo_done")
        sc_done = sem("sc_done")
        hi_ready, lo_ready = sem("hi_ready"), sem("lo_ready")
        strip_a, strip_b = sem("strip_a"), sem("strip_b")
        evac_a, evac_b = sem("evac_a"), sem("evac_b")
        ga_ready, conva_tap, convb_tap = sem("ga_ready"), sem("conva_tap"), sem("convb_tap")
        gated, tails = sem("gated"), sem("tails")
        st_tr, st_cp = sem("st_tr"), sem("st_cp")
        gate_a, gate_x, t_a, t_x = sem("gate_a"), sem("gate_x"), sem("t_a"), sem("t_x")
        a_done, a2_done, q_done, m_done, h_done, yb_done = (
            sem(n) for n in ("a_done", "a2_done", "q_done", "m_done", "h_done", "yb_done"))
        k_done = sem("k_done")
        mean_done, xc_done, sq_done, var_done, sd_done, xs_done, sig_done, ya_done = (
            sem(n) for n in ("mean_done", "xc_done", "sq_done", "var_done", "sd_done", "xs_done",
                             "sig_done", "ya_done"))
        yhi_done, ylo_done = sem("yhi_done"), sem("ylo_done")
        gt_mm, gt_cp = sem("gt_mm"), sem("gt_cp")
        tile_done, rmw_done = sem("tile_done"), sem("rmw_done")
        up_done, up_evac, r2_done, ffhi_done, fflo_done = (
            sem(n) for n in ("up_done", "up_evac", "r2_done", "ffhi_done", "fflo_done"))
        fin_ssq, fin_std, fin_y = sem("fin_ssq"), sem("fin_std"), sem("fin_y")

        ga_s = ga[:, :, GA_P:GA_W].rearrange("p j (b s) -> p j b s", s=GA_S)
        rec_s = rec[:, :, RB_P:RB_W].rearrange("p j (b s) -> p j b s", s=RB_S)
        win_v = w_in[0].rearrange("(k p) n -> p k n", p=P)
        wada_v = w_ada[0].rearrange("(k p) n -> p k n", p=P)
        wdown_v = w_down[0].rearrange("(n p) d -> n p d", p=P)
        wup_v = w_up[0].rearrange("(k p) n -> p k n", p=P)
        raw_k = raw[:, :, :].rearrange("p s (k n) -> p s k n", n=P)
        xs_rows = x_sample.rearrange("b t d -> (b t) d")
        ys_rows = y_sample.rearrange("b t d -> (b t) d")
        rows = [P] * (NT - 1) + [SMP]

        def wait(eng, s, value):
            if not isinstance(value, int) or value > 0:
                eng.wait_ge(s, value)

        def wait_apart(eng, s, value):
            eng.wait_ge(pool_set, 1)
            eng.wait_ge(s, value)

        def bank_pair(n):
            return 4 if n % 2 == 0 else 6

        block = ctx.enter_context(nc.Block())

        @block.sync
        def _(sp):
            def load_x(t):
                src = x_prompt[0, t * P:(t + 1) * P, :] if t < NT - 1 else xs_rows
                sp.dma_start(x2[0:rows[t], t, :], src).then_inc(x_in[t], 16)

            def load_piece(n_ge, slot, src, view):
                wait(sp, lo_ready, n_ge)
                dst = raw_k[:, slot, :, :] if view else raw[:, slot, :]
                sp.dma_start(dst, src).then_inc(raw_in[slot], 16)

            def load_ada(m, i):
                wait(sp, ada_lo, 4 * m + i - 1)
                sp.dma_start(raw_ada[:, i % 2, :].rearrange("p (k n) -> p k n", n=GW),
                             wada_v[:, 2 * i:2 * i + 2, bass.ds(m * GW + ADA0 * GW, GW)]).then_inc(ada_in[i % 2], 16)

            sp.wait_ge(c_in, 32)
            load_x(0)
            for g in range(ADA0):
                sp.dma_start(ada0[:, g, :, :], wada_v[:, :, g * GW:(g + 1) * GW]).then_inc(ada0_in[g], 16)
                if g == 0:
                    sp.wait_ge(par_in, 16 * N_ROWS_PAR)
                    sp.wait_ge(sa_in, 32)
                if g < 2:
                    load_x(g + 1)
            for s in range(2):
                load_piece(0, s, win_v[:, :, s * WA:s * WA + P], True)
            for t in range(3, NT):
                load_x(t)
            sp.wait_ge(nlo_done, NT)
            sp.wait_ge(nhi_done, NT)
            load_ada(0, 0)
            load_ada(0, 1)

            def step(m, nxt):
                if nxt is not None:
                    for s in range(2):
                        load_piece(2 * m + s + 1, s, win_v[:, :, bass.ds(nxt + s * WA, P)], True)
                load_ada(m, 2)
                load_ada(m, 3)
                if nxt is not None:
                    load_ada(m + 1, 0)
                    load_ada(m + 1, 1)

            with sp.Fori(0, J - 1) as j:
                step(j, (j + 1) * P)
            step(J - 1, 2 * WA)
            with sp.Fori(0, J - 1) as j:
                step(j + J, (j + 1) * P + 2 * WA)
            step(2 * J - 1, None)
            for k in range(KD):
                load_piece(W_OUT0 + k - 1, k % 2, w_out[0, k * P:(k + 1) * P, :], False)
            sp.wait_ge(yhi_done, J + NC)
            sp.wait_ge(ylo_done, J + NC)
            for t in range(NT):
                load_x(t)

            def down_piece(n, b, i, slot):
                load_piece(n - 1, slot, wdown_v[b * FI + i, :, :], False)

            def mlp(b, last):
                n = W_MLP0 + 2 + 8 * b
                down_piece(n, b, 0, 0)
                down_piece(n + 1, b, 1, 1)
                load_piece(n + 1, 0, wup_v[:, :, bass.ds(b * (FI * P) + 2 * P, P)], True)
                down_piece(n + 3, b, 2, 1)
                down_piece(n + 4, b, 3, 0)
                load_piece(n + 4, 1, wup_v[:, :, bass.ds(b * (FI * P) + 3 * P, P)], True)
                if not last:
                    load_piece(n + 5, 0, wup_v[:, :, bass.ds(b * (FI * P) + 4 * P, P)], True)
                    load_piece(n + 6, 1, wup_v[:, :, bass.ds(b * (FI * P) + 5 * P, P)], True)

            load_piece(W_MLP0 - 1, 0, wup_v[:, :, 0:P], True)
            load_piece(W_MLP0, 1, wup_v[:, :, P:2 * P], True)
            with sp.Fori(0, NBLK - 1) as b:
                mlp(b, False)
            mlp(NBLK - 1, True)
            sp.wait_ge(hi_ready, W_MLP0 + 8 * NBLK)
            sp.wait_ge(lo_ready, W_MLP0 + 8 * NBLK)
            sp.dma_start(raw[:, 0, :], g_final.partition_broadcast(P)).then_inc(gf_in, 16)
            for t in range(NT):
                sp.wait_ge(fin_y, t + 1)
                dst = y_prompt[0, t * P:(t + 1) * P, :] if t < NT - 1 else ys_rows
                sp.dma_start(dst, x2[0:rows[t], t, :]).then_inc(stored, 16)
            sp.wait_ge(stored, 16 * NT)

        @block.gpsimd
        def _(pool):
            pool.memset(ident[:, :], 0.0).then_inc(pool_ord, 1)
            pool.wait_ge(pool_ord, 1)
            pool.affine_select(out=ident[:, :], in_=ident[:, :], compare_op=ALU.not_equal, fill=1.0,
                               base=0, pattern=[[-1, P]], channel_multiplier=1).then_inc(pool_set, 1)
            pool.memset(mean_w[:, :], 1.0 / WA).then_inc(pool_set, 1)
            pool.memset(eps[:, :], EPS).then_inc(pool_set, 1)
            pool.memset(ga[:, :, 0:KA - 1], 0.0).then_inc(ga_ready, 1)
            pool.memset(rec[:, :, 0:KB - 1], 0.0).then_inc(pool_set, 1)
            pool.memset(wg[:, :, :, :], 0.0).then_inc(pool_set, 1)

            def lo(n, slot, dst, hi):
                pool.wait_ge(hi_ready, n + 1)
                pool.tensor_tensor(dst, raw[:, slot, :], hi.bitcast(F32), ALU.subtract).then_inc(lo_ready, 1)

            def strip_lo(n, slot, used, count):
                wait(pool, used, count)
                lo(n, slot, w_lo[:, slot, :], w_hi[:, slot, :])

            def split_ada(q, slot):
                pool.wait_ge(ada_hi, q + 1)
                pool.tensor_tensor(aw_lo[:, slot, :], raw_ada[:, slot, :],
                                   aw_hi[:, slot, :].bitcast(F32), ALU.subtract).then_inc(ada_lo, 1)

            pool.wait_ge(ada0_used, 4 * ADA0)
            strip_lo(0, 0, strip_a, 0)
            strip_lo(1, 1, strip_b, 0)
            split_ada(0, 0)
            split_ada(1, 1)

            def product(j):
                pool.wait_ge(evac_b, NC * (j + 1))
                pool.wait_ge(evac_a, NC * (j + 1))
                pool.tensor_tensor(ga[:, j, KA - 1:GA_P], ga[:, j, KA - 1:GA_P], sg[:, 0:SEQ],
                                   ALU.mult).then_inc(ga_ready, 1)
                pool.tensor_tensor(ga_s[:, j, :, KA - 1:GA_S], ga_s[:, j, :, KA - 1:GA_S],
                                   sg[:, SEQ:TOK].rearrange("p (b t) -> p b t", t=TB),
                                   ALU.mult).then_inc(ga_ready, 1)

            def step(m, glu, last):
                if not last:
                    strip_lo(2 * m + 2, 0, strip_a, NC * (m + 1))
                split_ada(4 * m + 2, 0)
                split_ada(4 * m + 3, 1)
                if glu and isinstance(m, int):
                    product(m)
                if not last:
                    strip_lo(2 * m + 3, 1, strip_b, NC * (m + 1))
                    split_ada(4 * m + 4, 0)
                if glu and not isinstance(m, int):
                    product(m)
                if not last:
                    split_ada(4 * m + 5, 1)

            step(0, True, False)
            with pool.Fori(1, J) as j:
                step(j, True, False)
            with pool.Fori(J, 2 * J - 1) as m:
                step(m, False, False)
            step(2 * J - 1, False, True)
            pool.wait_ge(ada_lo, 4 * 2 * J)
            for j in range(J):
                pool.tensor_copy(tail_a[:, j, :].rearrange("p (b s) -> p b s", b=NB), ga_s[:, j, :, TB:GA_S])
            pool.wait_ge(evac_a, 2 * J * NC)
            for j in range(J):
                last = pool.tensor_copy(tail_b[:, j, :].rearrange("p (b s) -> p b s", b=NB), rec_s[:, j, :, TB:RB_S])
            last.then_inc(tails, 1)
            pool.wait_ge(st_tr, 5)
            pool.wait_ge(ada_evac, ADA_G)
            for g, row0 in ((0, M_GTM), (1, M_GTF)):
                for k in range(KD):
                    last = pool.tensor_copy(gt_tok[:, g, k, :].rearrange("p (b t) -> p b t", t=TB),
                                            mod[:, row0 + k, 1:9].unsqueeze(2).broadcast_to([P, NB, TB]))
            last.then_inc(tails, 1)
            pool.wait_ge(yb_done, J)
            pool.wait_ge(conva_tap, 2 * KA * J)
            for k in range(KD):
                lo(W_OUT0 + k, k % 2, wb_lo[:, k, :], wb_hi[:, k, :])

            lo(W_MLP0, 0, w_lo[:, 0, :], w_hi[:, 0, :])
            lo(W_MLP0 + 1, 1, w_lo[:, 1, :], w_hi[:, 1, :])

            def mlp(b, last):
                n = W_MLP0 + 2 + 8 * b
                pool.wait_ge(tile_done, NT * (b + 1))
                lo(n, 0, wb_lo[:, 0, :], wb_hi[:, 0, :])
                lo(n + 1, 1, wb_lo[:, 1, :], wb_hi[:, 1, :])
                strip_lo(n + 2, 0, up_done, 12 * b + 3)
                lo(n + 3, 1, wb_lo[:, 2, :], wb_hi[:, 2, :])
                lo(n + 4, 0, wb_lo[:, 3, :], wb_hi[:, 3, :])
                strip_lo(n + 5, 1, up_done, 12 * b + 6)
                if not last:
                    strip_lo(n + 6, 0, up_done, 12 * b + 9)
                    strip_lo(n + 7, 1, up_done, 12 * b + 12)

            with pool.Fori(0, NBLK - 1) as b:
                mlp(b, False)
            mlp(NBLK - 1, True)

        @block.scalar
        def _(act):
            ordered = [0]

            def own(ins):
                ordered[0] += 1
                ins.then_inc(act_ord, 1)
                act.wait_ge(act_ord, ordered[0])

            def load_rows(dst, src, s):
                act.dma_start(dst, src).then_inc(s, 16)

            load_rows(ld_c[0:1, 0, :], c_prompt, c_in)
            load_rows(ld_c[1:9, 0, :], c_sample, c_in)
            for col, src in ((C_BIN, b_in), (C_BADA, b_ada), (C_CAB, conv_a_b), (C_LNG, ln_a_g),
                             (C_LNB, ln_a_b), (C_CBB, conv_b_b), (C_BGA, b_gate_a), (C_BGX, b_gate_x),
                             (C_LAM, lru_lambda), (C_GMIX, g_mix), (C_GFFN, g_ffn)):
                n = src.shape[1] // P
                load_rows(ld_par[col:col + n, 0, :], src[0].rearrange("(r p) -> r p", p=P), par_in)
            load_rows(ld_par[C_CBW:N_PAR, 0, :], conv_b_w[0].rearrange("k (j p) -> (k j) p", p=P), par_in)
            load_rows(ld_par[0:KA * J, 1, :], conv_a_w[0].rearrange("k (j p) -> (k j) p", p=P), par_in)
            load_rows(ld_par[0:NB * J, 2, :], state_lru_h[0].rearrange("b (j p) -> (b j) p", p=P), par_in)
            load_rows(ld_sb[:, :], state_conv_b[0].rearrange("b s c -> (b s) c"), par_in)
            for half in range(2):
                load_rows(ld_sa[:, half, :], state_conv_a[0, 4 * half:4 * half + 4].rearrange("b s c -> (b s) c"),
                          sa_in)


            act.wait_ge(c_in, 32)
            act.activation(ld_c[:, 1, :], ld_c[:, 0, :], ACT.Sigmoid).then_inc(c_sig, 1)
            act.wait_ge(c_tr, 1)
            act.wait_ge(c_zero, 1)
            act.activation(stk[:, :, 0:9], ps[:, 0, 0:9 * KD].rearrange("p (k c) -> p k c", c=9), ACT.Copy).then_inc(c_cp, 1)

            def norm(n, t, src, junk, wait_free):
                wait_free()
                r = rows[t]
                own(act.activation(junk[0:r, 0:D], src[0:r, t, :], ACT.Square, accum_out=ssq[0:r, 0, t:t + 1]))
                act.activation(ssq[0:r, 1, t:t + 1], ssq[0:r, 0, t:t + 1], ACT.Sqrt, scale=1.0 / D,
                               bias=eps[0:r, :]).then_inc(std_done, 1)

            def modulate(n, t, scale, shift0, slot, free):
                hf = xn[:, slot, :].rearrange("p (k c) -> p k c", c=P)
                if t < NT - 1:
                    act.wait_ge(tr_done, n + 1)
                    wait(act, nlo_done, free)
                    for k in range(4, KD):
                        last = act.activation(hf[:, k, :], ps[:, bank_pair(n) + 1, (k - 4) * P:(k - 3) * P],
                                              ACT.Identity, scale=scale[:, k, 0:1],
                                              bias=mod[:, shift0 + k, 0:1])
                    last.then_inc(hf_a, 1)
                    act.wait_ge(hf_a, hfa(n))
                act.wait_ge(hf_d, n + 1)
                act.activation(act_hi[:, :, t * P:t * P + rows[t]], hf[:, :, 0:rows[t]], ACT.Copy).then_inc(nhi_done, 1)

            def hi(n, slot, dst, loaded):
                act.wait_ge(raw_in[slot], loaded)
                act.activation(dst, raw[:, slot, :], ACT.Copy).then_inc(hi_ready, 1)

            def strip_hi(n, slot, used, count):
                wait(act, used, count)
                hi(n, slot, w_hi[:, slot, :], 16 * (n // 2 + 1))

            def group_rows(g, bank):
                act.activation(ada_rows[:, :], ps[:, bank, :], ACT.Copy).then_inc(rows_out, 1)

            def group_out(g, bank, col):
                act.wait_ge(ada_tr, g + 1)
                for i in range(4):
                    last = act.activation(mod[:, bass.ds(4 * g + i, 1), :], ps[:, bank, col + 9 * i:col + 9 * i + 9].unsqueeze(1),
                                          ACT.Identity, bias=par[:, bass.ds(C_BADA + i + 4 * g, 1)])
                last.then_inc(ada_evac, 1)

            def ada_split(m, i):
                q, slot = 4 * m + i, i % 2
                wait_apart(act, ada_in[slot], 16 * (2 * m + i // 2 + 1))
                wait(act, ada_used, q - 1)
                act.activation(aw_hi[:, slot, :], raw_ada[:, slot, :],
                               ACT.Copy).then_inc(ada_hi, 1)

            act.wait_ge(pool_set, 3)
            for g in range(ADA0):
                if g < 3:
                    norm(g, g, x2, sg, lambda: act.wait_ge(x_in[g], 16))
                act.wait_ge(ada0_in[g], 16)
                for i in range(4):
                    e = 4 * g + i
                    wait(act, ada0_used, e - 1)
                    act.activation(w_hi[:, e % 2, :], ada0[:, g, 2 * i:2 * i + 2, :].rearrange("p a b -> p (a b)"),
                                   ACT.Copy).then_inc(ada0_hi, 1)
                    if g > 0 and i == 1:
                        act.wait_ge(ada0_used, 4 * g)
                        group_rows(g - 1, 6 + (g - 1) % 2)
                if g > 0:
                    wait(act, par_cp, 1)
                    group_out(g - 1, 0, P + 36 * (g - 1))
            act.wait_ge(ada0_used, 4 * ADA0)
            group_rows(ADA0 - 1, 7)
            group_out(ADA0 - 1, 0, P + 36 * (ADA0 - 1))
            act.wait_ge(pool_set, 5)
            for g, w in ((0, w_gate_a), (1, w_gate_x)):
                for half in range(2):
                    at = slice(64 * half, 64 * half + 64)
                    act.dma_start(wg[at, g, :, at], w[0].rearrange("(j h) i o -> h i j o", h=2)[half]).then_inc(wg_in, 16)
            act.wait_ge(sc_done, 1)
            for s in range(2):
                strip_hi(s, s, strip_a, 0)
            for t in range(NT):
                if t + 3 < NT:
                    norm(t + 3, t + 3, x2, sg, lambda: act.wait_ge(x_in[t + 3], 16))
                modulate(t, t, sc_m, M_SHM, t % 2, t - 1)

            lam = par[:, C_LAM:C_LAM + J]
            own(act.activation(sp[:, 0, :], lam, ACT.Abs))
            act.activation(sp[:, 1, :], sp[:, 0, :], ACT.Exp, scale=-1.0).then_inc(k_done, 1)
            act.wait_ge(k_done, 2)
            act.activation(sp[:, 3, :], sp[:, 2, :], ACT.Ln).then_inc(k_done, 1)
            act.wait_ge(sa_tr, 2)
            ada_split(0, 0)
            ada_split(0, 1)

            def chunk_out(c, src_bank, dst_p, dst_s, func, bias, done):
                if c < 2:
                    act.activation(dst_p(c * CH, CH), ps[:, src_bank + c, 0:CH], func, bias=bias).then_inc(done, 1)
                else:
                    act.activation(dst_p(c * CH, PROMPT2), ps[:, src_bank + c, 0:PROMPT2], func, bias=bias)
                    act.activation(dst_s, ps[:, src_bank + c, PROMPT2:PROMPT2 + SMP].rearrange("p (b t) -> p b t", t=TB),
                                   func, bias=bias).then_inc(done, 1)

            def step(m, j, group_a, first, last):
                if not first:
                    wait_apart(act, ada_used, 4 * m)
                    group_rows(m + ADA0 - 1, 6)
                for c in range(NC):
                    if c == 2 and not first:
                        wait_apart(act, ada_tr, m + ADA0)
                        group_out(m + ADA0 - 1, 7, 0)
                    wait_apart(act, strip_a, NC * m + c + 1)
                    if group_a:
                        chunk_out(c, 0, lambda o, w: ga[:, j, KA - 1 + o:KA - 1 + o + w],
                                  ga_s[:, j, :, KA - 1:GA_S], ACT.Identity, par[:, bass.ds(C_BIN + j, 1)], evac_a)
                    else:
                        chunk_out(c, 0, lambda o, w: rec[:, j, KB - 1 + o:KB - 1 + o + w],
                                  rec_s[:, j, :, KB - 1:RB_S], ACT.Identity,
                                  par[:, bass.ds(C_BIN + 2 * J + j, 1)], evac_a)
                if not last:
                    act.wait_ge(raw_in[0], 16 * (m + 2))
                    act.activation(w_hi[:, 0, :], raw[:, 0, :], ACT.Copy).then_inc(hi_ready, 1)
                ada_split(m, 2)
                ada_split(m, 3)
                if group_a:
                    act.wait_ge(ga_ready, 2 * j + 1)
                for c in range(NC):
                    wait_apart(act, strip_b, NC * m + c + 1)
                    if group_a:
                        chunk_out(c, 3, lambda o, w: sg[:, o:o + w],
                                  sg[:, SEQ:TOK].rearrange("p (b t) -> p b t", t=TB), ACT.Sigmoid,
                                  par[:, bass.ds(C_BIN + J + j, 1)], evac_b)
                    else:
                        chunk_out(c, 3, lambda o, w: gel[:, j, o:o + w],
                                  gel[:, j, SEQ:TOK].rearrange("p (b t) -> p b t", t=TB), ACT.Gelu_apprx_tanh,
                                  par[:, bass.ds(C_BIN + 3 * J + j, 1)], evac_b)
                if not last:
                    act.wait_ge(raw_in[1], 16 * (m + 2))
                    act.activation(w_hi[:, 1, :], raw[:, 1, :], ACT.Copy).then_inc(hi_ready, 1)
                if not last:
                    ada_split(m + 1, 0)
                    ada_split(m + 1, 1)

            step(0, 0, True, True, False)
            with act.Fori(1, J) as j:
                step(j, j, True, False, False)
            with act.Fori(0, J - 1) as j:
                step(j + J, j, False, False, False)
            step(2 * J - 1, J - 1, False, False, True)
            act.wait_ge(ada_used, 4 * 2 * J)
            group_rows(ADA_G - 1, 6)
            act.wait_ge(ada_tr, ADA_G)
            group_out(ADA_G - 1, 7, 0)

            def staged(n, dst, bank, r):
                act.wait_ge(st_tr, n + 1)
                act.activation(dst, ps[0:r, bank, :], ACT.Copy).then_inc(st_cp, 1)
                act.wait_ge(st_cp, n + 1)

            act.wait_ge(ada_lo, 4 * 2 * J)
            half_rows = 4 * (KA - 1)
            staged(0, stage[0:KA - 1, 2, :], 6, KA - 1)
            act.dma_start(ca_prompt[0, 0], stage[0:KA - 1, 2, :]).then_inc(staged_out, 16)
            for h in range(2):
                staged(1 + h, stage[0:half_rows, h, :], 7 - h, half_rows)
                act.dma_start(ca_sample[0, 4 * h:4 * h + 4].rearrange("b s c -> (b s) c"),
                              stage[0:half_rows, h, :]).then_inc(staged_out, 16)
            staged(3, stage[64:64 + KB - 1, 2, :], 7, KB - 1)
            act.dma_start(cb_prompt[0, 0], stage[64:64 + KB - 1, 2, :]).then_inc(staged_out, 16)
            staged(4, stage[32:32 + NB * (KB - 1), 2, :], 6, NB * (KB - 1))
            act.dma_start(cb_sample[0].rearrange("b s c -> (b s) c"),
                          stage[32:32 + NB * (KB - 1), 2, :]).then_inc(staged_out, 16)

            act.wait_ge(k_done, 3 + 8)
            act.wait_ge(conva_tap, 2 * KA * J)
            ga_t = [ga[:, n, 0:TOK] for n in range(4)]
            a_t, th_t, sx_t, m_t = ga_t
            for j in range(J):
                wait(act, q_done, j)
                for c in range(NC):
                    act.wait_ge(gate_a, NC * j + c + 1)
                    act.activation(th_t[:, c * CH:c * CH + CW[c]], ps[:, c, 0:CW[c]], ACT.Tanh, scale=0.5,
                                   bias=hb[:, 0, j:j + 1]).then_inc(evac_a, 1)
                wait(act, h_done, j)
                for c in range(NC):
                    act.wait_ge(gate_x, NC * j + c + 1)
                    act.activation(sx_t[:, c * CH:c * CH + CW[c]], ps[:, 3 + c, 0:CW[c]], ACT.Tanh, scale=0.5,
                                   bias=hb[:, 1, j:j + 1]).then_inc(evac_b, 1)
                act.wait_ge(evac_a, NC * (2 * J + j + 1))
                own(act.activation(a_t, th_t, ACT.Exp, scale=k4[:, 1, j:j + 1], bias=k4[:, 1, j:j + 1]))
                act.activation(th_t, th_t, ACT.Tanh, scale=k4[:, 0, j:j + 1], bias=k4[:, 0, j:j + 1])
                wait(act, yb_done, j)
                act.activation(m_t, a_t, ACT.Square).then_inc(a2_done, 1)
                act.wait_ge(q_done, j + 1)
                act.activation(m_t, m_t, ACT.Sqrt).then_inc(m_done, 1)

            for c in range(NC):
                t0, w = c * CH, CW[c]
                act.wait_ge(xc_done, c + 1)
                if c == 0:
                    act.wait_ge(staged_out, 16 * 5)
                else:
                    act.wait_ge(var_done, c)
                act.activation(sq[:, :, 0:w], conv_a[:, :, t0:t0 + w], ACT.Square).then_inc(sq_done, 1)
                act.wait_ge(var_done, c + 1)
                act.activation(rstd[:, t0:t0 + w], ps[:, 7, 0:w], ACT.Sqrt, bias=eps[:, :]).then_inc(sd_done, 1)
            act.wait_ge(st_tr, 6)
            act.activation(stage[0:9, 3, :], ps[0:9, 6, :], ACT.Copy).then_inc(st_cp, 1)
            act.wait_ge(st_cp, 6)
            act.dma_start(h_prompt[0], stage[0:1, 3, :]).then_inc(staged_out, 16)
            act.dma_start(h_sample[0], stage[1:9, 3, :]).then_inc(staged_out, 16)

            act.wait_ge(strip_b, NC * 2 * J)
            for j in range(J):
                act.wait_ge(yb_done, j + 1)
                act.activation(act_hi[:, J + j, 0:SEQ], gel[:, j, 0:SEQ], ACT.Copy)
                act.activation(stk[:, J + j, 0:SMP], gel[:, j, SEQ:TOK], ACT.Copy).then_inc(yhi_done, 1)
            for k in range(4):
                hi(W_OUT0 + k, k % 2, wb_hi[:, k, :], 16 * ((W_OUT0 + k) // 2 + 1))
            for c in range(NC):
                t0, w = c * CH, CW[c]
                act.wait_ge(xs_done, c + 1)
                wait(act, ya_done, c)
                for i in range(J):
                    last = act.activation(sq[:, i, 0:w], conv_a[:, i, t0:t0 + w], ACT.Sigmoid,
                                          scale=par[:, C_LNG + i:C_LNG + i + 1],
                                          bias=par[:, C_LNB + i:C_LNB + i + 1])
                last.then_inc(sig_done, 1)
                if c > 0:
                    hi(W_OUT0 + 2 + 2 * c, 0, wb_hi[:, 2 + 2 * c, :], 16 * ((W_OUT0 + 2 + 2 * c) // 2 + 1))
                    hi(W_OUT0 + 3 + 2 * c, 1, wb_hi[:, 3 + 2 * c, :], 16 * ((W_OUT0 + 3 + 2 * c) // 2 + 1))
                act.wait_ge(ya_done, c + 1)
                n = w if c < 2 else PROMPT2
                ins = act.activation(act_hi[:, 0:J, t0:t0 + n], conv_a[:, :, t0:t0 + n], ACT.Copy)
                if c == 2:
                    ins = act.activation(stk[:, 0:J, 0:SMP], conv_a[:, :, SEQ:TOK], ACT.Copy)
                ins.then_inc(yhi_done, 1)

            def gates_out(first, bank_p, bank_s):
                act.wait_ge(gt_mm, first + 1)
                act.activation(gt_p[:, :], ps[:, bank_p:bank_p + 2, :].rearrange("p a b -> p (a b)"), ACT.Copy).then_inc(gt_cp, 1)
                act.wait_ge(gt_mm, first + 2)
                act.activation(gt_s[:, :], ps[0:SMP, bank_s:bank_s + 2, :].rearrange("p a b -> p (a b)"), ACT.Copy).then_inc(gt_cp, 1)

            gates_out(0, 0, 2)
            strip_hi(W_MLP0, 0, strip_a, 0)
            strip_hi(W_MLP0 + 1, 1, strip_b, 0)

            act.wait_ge(staged_out, 16 * 7)
            act.wait_ge(sc_done, 2)
            for t in range(NT):
                n = NT + t
                if t > 0:
                    modulate(n - 1, t - 1, sc_f, M_SHF, 1, n - 1)

                def free():
                    act.wait_ge(rmw_done, t + 1)
                    act.wait_ge(tr_done, n)
                norm(n, t, x2, xn[:, 0, :], free)
            modulate(2 * NT - 1, NT - 1, sc_f, M_SHF, 1, 0)

            def mlp(b, last):
                n = W_MLP0 + 2 + 8 * b
                half = W_MLP0 // 2 + 1 + 4 * b

                def down(i, at, slot):
                    hi(n, slot, wb_hi[:, i, :], 16 * (half + at // 2 + 1))

                def strip(at, slot, count):
                    wait(act, up_done, count)
                    hi(n, slot, w_hi[:, slot, :], 16 * (half + at // 2 + 1))

                def relu_sq(i):
                    for c in range(NC):
                        q = 3 * i + c
                        r = relu[:, q % 2, 0:CW[c]]
                        act.wait_ge(up_done, 12 * b + q + 1)
                        wait(act, r2_done, 12 * b + q - 1)
                        act.activation(r, ps[:, 3 * (i % 2) + c, 0:CW[c]], ACT.Relu).then_inc(up_evac, 1)
                        act.wait_ge(up_evac, 12 * b + q + 1)
                        if c < 2:
                            act.activation(wb_hi[:, FI + i, c * CH:(c + 1) * CH], r, ACT.Square).then_inc(ffhi_done, 1)
                        else:
                            act.activation(wb_hi[:, FI + i, c * CH:SEQ], r[:, 0:PROMPT2], ACT.Square)
                            act.activation(stk[:, i, 0:SMP], r[:, PROMPT2:CW[c]], ACT.Square).then_inc(ffhi_done, 1)

                act.wait_ge(tile_done, NT * (b + 1))
                down(0, 0, 0)
                down(1, 1, 1)
                relu_sq(0)
                strip(2, 0, 12 * b + 3)
                down(2, 3, 1)
                down(3, 4, 0)
                relu_sq(1)
                strip(5, 1, 12 * b + 6)
                relu_sq(2)
                if not last:
                    strip(6, 0, 12 * b + 9)
                relu_sq(3)
                if not last:
                    strip(7, 1, 12 * b + 12)

            act.wait_ge(nlo_done, 2 * NT)
            mlp(0, False)
            gates_out(2, 6, 4)
            with act.Fori(1, NBLK - 1) as b:
                mlp(b, False)
            mlp(NBLK - 1, True)

            for t in range(NT):
                r = rows[t]
                act.wait_ge(rmw_done, NT * (NBLK + 1) - NT + t + 1)
                own(act.activation(xn[0:r, 0, :], x2[0:r, t, :], ACT.Square, accum_out=ssq[0:r, 0, t:t + 1]))
                act.activation(ssq[0:r, 1, t:t + 1], ssq[0:r, 0, t:t + 1], ACT.Sqrt, scale=1.0 / D,
                               bias=eps[0:r, :]).then_inc(std_done, 1)

        @block.vector
        def _(dve):
            ordered = [0]

            def own(ins):
                ordered[0] += 1
                ins.then_inc(dve_ord, 1)
                dve.wait_ge(dve_ord, ordered[0])

            dve.wait_ge(c_sig, 1)
            dve.tensor_tensor(ld_c[:, 1, :], ld_c[:, 0, :], ld_c[:, 1, :], ALU.mult).then_inc(c_silu, 1)
            dve.wait_ge(pool_set, 1)
            dve.tensor_scalar(stk[:, :, :], ident[:, :].unsqueeze(1).broadcast_to([P, KD, P]), 0.0, None,
                              ALU.mult).then_inc(c_zero, 1)
            dve.tensor_tensor(pick[:, :], ident[:, 0:9], ident[:, C_LO:C_LO + 9], ALU.add).then_inc(c_zero, 1)
            dve.wait_ge(par_tr, 1)
            dve.tensor_copy(par[:, :], ps[:, 1, 0:N_PAR]).then_inc(par_cp, 1)
            dve.tensor_copy(caw[:, :], ps[:, 1, P:P + KA * J]).then_inc(par_cp, 1)
            dve.tensor_copy(h0[:, :, :], ps[:, 1, 256:288].rearrange("p (b j) -> p b j", j=J)).then_inc(par_cp, 1)
            dve.tensor_copy(rec_s[:, :, :, 0:KB - 1],
                            ps[:, 1, 288:384].rearrange("p (j b s) -> p j b s", j=J, s=KB - 1)).then_inc(par_cp, 1)
            dve.wait_ge(c_cp, 1)
            dve.tensor_tensor(stk[:, :, C_LO:C_LO + 9], ps[:, 0, 0:9 * KD].rearrange("p (k c) -> p k c", c=9),
                              stk[:, :, 0:9].bitcast(F32), ALU.subtract).then_inc(c_cp, 1)
            for h in range(2):
                dve.wait_ge(sa_tr, h + 1)
                dve.tensor_copy(ga_s[:, :, 4 * h:4 * h + 4, 0:KA - 1],
                                ps[:, 2 + h, 0:480].rearrange("p (j b s) -> p j b s", j=J, s=KA - 1)).then_inc(sa_cp, 1)
            def scales(dst, row0, col):
                g = par[:, col:col + KD].unsqueeze(2).broadcast_to([P, KD, 9])
                dve.scalar_tensor_tensor(out=dst[:, :, :], in0=mod[:, row0:row0 + KD, :], scalar=1.0,
                                         in1=g, op0=ALU.add, op1=ALU.mult).then_inc(sc_done, 1)

            def scale_rows(n, t, src, dst):
                r = rows[t]
                dve.wait_ge(std_done, n + 1)
                own(dve.reciprocal(ssq[0:r, 2, t:t + 1], ssq[0:r, 1, t:t + 1]))
                dve.tensor_scalar(dst, src[0:r, t, :], ssq[0:r, 2, t:t + 1], None, ALU.mult).then_inc(xn_done, 1)

            def modulate(n, t, scale, shift0, slot, free):
                hf = xn[:, slot, :].rearrange("p (k c) -> p k c", c=P)
                dve.wait_ge(tr_done, n + 1)
                wait(dve, nhi_done, free)
                b = bank_pair(n)
                if t < NT - 1:
                    for k in range(4):
                        last = dve.tensor_scalar(hf[:, k, :], ps[:, b, k * P:(k + 1) * P], scale[:, k, 0:1],
                                                 mod[:, shift0 + k, 0:1], ALU.mult, ALU.add)
                    last.then_inc(hf_d, 1)
                    dve.wait_ge(hf_a, hfa(n))
                else:
                    hs = hf[:, :, 0:SMP].rearrange("p k (b t) -> p k b t", t=TB)
                    src = ps[:, b:b + 2, :].rearrange("p a (k c) -> p (a k) c", c=P)[:, :, 0:SMP].rearrange(
                        "p k (b t) -> p k b t", t=TB)
                    for k in range(KD):
                        last = dve.tensor_tensor(hs[:, k], src[:, k],
                                                 scale[:, k, 1:9].unsqueeze(2).broadcast_to([P, NB, TB]), ALU.mult)
                    own(last)
                    for k in range(KD):
                        last = dve.tensor_tensor(hs[:, k], hs[:, k],
                                                 mod[:, shift0 + k, 1:9].unsqueeze(2).broadcast_to([P, NB, TB]), ALU.add)
                    last.then_inc(hf_d, 1)
                dve.wait_ge(nhi_done, n + 1)
                cols = slice(t * P, t * P + rows[t])
                dve.tensor_tensor(act_lo[:, :, cols], hf[:, :, 0:rows[t]], act_hi[:, :, cols].bitcast(F32),
                                  ALU.subtract).then_inc(nlo_done, 1)

            for g in range(ADA0):
                for i in range(4):
                    e = 4 * g + i
                    dve.wait_ge(ada0_hi, e + 1)
                    dve.tensor_tensor(w_lo[:, e % 2, :], ada0[:, g, 2 * i:2 * i + 2, :].rearrange("p a b -> p (a b)"),
                                      w_hi[:, e % 2, :].bitcast(F32), ALU.subtract).then_inc(ada0_lo, 1)
                if g < 3:
                    scale_rows(g, g, x2, x2[0:rows[g], g, :])
            dve.wait_ge(ada_evac, ADA0)
            scales(sc_m, M_SCM, C_GMIX)
            dve.wait_ge(sc_done, 1)
            for t in range(NT):
                if t + 3 < NT:
                    scale_rows(t + 3, t + 3, x2, x2[0:rows[t + 3], t + 3, :])
                modulate(t, t, sc_m, M_SHM, t % 2, t - 1)

            dve.wait_ge(par_cp, 1)
            dve.wait_ge(k_done, 1)
            e_, u_, ln_, w_ = (sp[:, n, :] for n in (1, 2, 3, 4))
            dve.tensor_scalar(u_, e_, 1.0, None, ALU.add).then_inc(k_done, 1)
            dve.wait_ge(k_done, 3)
            own(dve.tensor_scalar(w_, u_, -1.0, None, ALU.add))
            own(dve.tensor_tensor(e_, e_, w_, ALU.subtract))
            own(dve.reciprocal(w_, u_))
            own(dve.tensor_tensor(e_, e_, w_, ALU.mult))
            own(dve.tensor_tensor(ln_, ln_, e_, ALU.add))
            own(dve.tensor_scalar(w_, par[:, C_LAM:C_LAM + J], -1.0, 0.0, ALU.mult, ALU.max))
            own(dve.tensor_tensor(ln_, ln_, w_, ALU.add))
            dve.tensor_scalar(k4[:, 0, :], ln_, 4.0, None, ALU.mult).then_inc(k_done, 2)
            dve.tensor_scalar(k4[:, 1, :], ln_, -4.0, None, ALU.mult).then_inc(k_done, 2)
            dve.tensor_scalar(hb[:, 0, :], par[:, C_BGA:C_BGA + J], 0.5, None, ALU.mult).then_inc(k_done, 2)
            dve.tensor_scalar(hb[:, 1, :], par[:, C_BGX:C_BGX + J], 0.5, None, ALU.mult).then_inc(k_done, 2)

            def conv(src, src_s, width, taps, out, j, done, bias_col, base):
                out_s = out[:, j, SEQ:TOK].rearrange("p (b t) -> p b t", t=TB)
                for k in range(width):
                    w = taps(k)
                    win, win_s = src[:, j, k:k + SEQ], src_s[:, j, :, k:k + TB]
                    if k == 0:
                        bias = par[:, bass.ds(bias_col + j, 1)]
                        dve.tensor_scalar(out[:, j, 0:SEQ], win, w, bias, ALU.mult, ALU.add).then_inc(done, 1)
                        dve.tensor_scalar(out_s, win_s, w, bias, ALU.mult, ALU.add).then_inc(done, 1)
                    else:
                        dve.wait_ge(done, 2 * width * j + 2 * k - 1 + base)
                        dve.scalar_tensor_tensor(out=out[:, j, 0:SEQ], in0=win, scalar=w, in1=out[:, j, 0:SEQ],
                                                 op0=ALU.mult, op1=ALU.add).then_inc(done, 1)
                        dve.wait_ge(done, 2 * width * j + 2 * k + base)
                        dve.scalar_tensor_tensor(out=out_s, in0=win_s, scalar=w, in1=out_s,
                                                 op0=ALU.mult, op1=ALU.add).then_inc(done, 1)

            dve.wait_ge(sa_cp, 2)
            with dve.Fori(0, J) as j:
                dve.wait_ge(ga_ready, 2 * j + 3)
                conv(ga, ga_s, KA, lambda k: caw[:, bass.ds(j + k * J, 1)], conv_a, j, conva_tap, C_CAB, 0)
            dve.wait_ge(conva_tap, 2 * KA * J)
            dve.wait_ge(ada_used, 4 * 2 * J)
            with dve.Fori(0, J) as j:
                dve.wait_ge(evac_a, NC * (J + 1) + NC * j)
                conv(rec, rec_s, KB, lambda k: par[:, bass.ds(C_CBW + j + k * J, 1)], cb, j, convb_tap, C_CBB, 0)

            a_t, th_t, sx_t, m_t = (ga[:, n, 0:TOK] for n in range(4))

            def firsts(ap):
                return ap[:, SEQ:TOK].rearrange("p (b t) -> p b t", t=TB)[:, :, 0]

            for j in range(J):
                dve.wait_ge(a2_done, j + 1)
                dve.scalar_tensor_tensor(out=m_t, in0=m_t, scalar=1.0, in1=th_t, op0=ALU.add,
                                         op1=ALU.mult).then_inc(q_done, 1)
                own(dve.scalar_tensor_tensor(out=sx_t, in0=sx_t, scalar=1.0, in1=cb[:, j, :], op0=ALU.add,
                                             op1=ALU.mult))
                own(dve.tensor_tensor(tmp8[:, :], firsts(a_t), h0[:, :, j], ALU.mult))
                own(dve.memset(firsts(a_t), 0.0))
                dve.wait_ge(m_done, j + 1)
                own(dve.memset(m_t[:, 0:1], 1.0))
                own(dve.scalar_tensor_tensor(out=sx_t, in0=m_t, scalar=0.5, in1=sx_t, op0=ALU.mult,
                                             op1=ALU.mult))
                own(dve.tensor_tensor(firsts(sx_t), firsts(sx_t), tmp8[:, :], ALU.add))
                dve.tensor_tensor_scan(m_t, a_t, sx_t, 0.0, ALU.mult, ALU.add).then_inc(h_done, 1)
                dve.wait_ge(h_done, j + 1)
                dve.tensor_copy(h_end[:, j, 0:1], m_t[:, SEQ - 1:SEQ])
                dve.tensor_copy(h_end[:, j, 1:9], m_t[:, SEQ:TOK].rearrange("p (b t) -> p b t", t=TB)[:, :, TB - 1])
                dve.tensor_tensor(gel[:, j, :], m_t, gel[:, j, :], ALU.mult).then_inc(yb_done, 1)

            def over_tiles(ap, w):
                return ap.unsqueeze(1).broadcast_to([P, J, w])

            for c in range(NC):
                t0, w = c * CH, CW[c]
                dve.wait_ge(mean_done, c + 1)
                dve.tensor_tensor(conv_a[:, :, t0:t0 + w], conv_a[:, :, t0:t0 + w], over_tiles(ps[:, 6, 0:w], w),
                                  ALU.subtract).then_inc(xc_done, 1)
            for j in range(J):
                dve.wait_ge(yhi_done, j + 1)
                dve.tensor_tensor(act_lo[:, J + j, 0:SEQ], gel[:, j, 0:SEQ], act_hi[:, J + j, 0:SEQ].bitcast(F32),
                                  ALU.subtract)
                dve.tensor_tensor(stk[:, J + j, SMP:P], gel[:, j, SEQ:TOK], stk[:, J + j, 0:SMP].bitcast(F32),
                                  ALU.subtract).then_inc(ylo_done, 1)

            def normalise(c):
                t0, w = c * CH, CW[c]
                dve.wait_ge(sd_done, c + 1)
                own(dve.reciprocal(rstd[:, t0:t0 + w], rstd[:, t0:t0 + w]))
                dve.tensor_tensor(conv_a[:, :, t0:t0 + w], conv_a[:, :, t0:t0 + w], over_tiles(rstd[:, t0:t0 + w], w),
                                  ALU.mult).then_inc(xs_done, 1)

            normalise(0)
            for c in range(NC):
                t0, w = c * CH, CW[c]
                if c + 1 < NC:
                    normalise(c + 1)
                dve.wait_ge(sig_done, c + 1)
                for i in range(J):
                    last = dve.tensor_scalar(conv_a[:, i, t0:t0 + w], conv_a[:, i, t0:t0 + w],
                                             par[:, C_LNG + i:C_LNG + i + 1], par[:, C_LNB + i:C_LNB + i + 1],
                                             ALU.mult, ALU.add)
                own(last)
                dve.tensor_tensor(conv_a[:, :, t0:t0 + w], conv_a[:, :, t0:t0 + w], sq[:, :, 0:w],
                                  ALU.mult).then_inc(ya_done, 1)
                dve.wait_ge(yhi_done, J + c + 1)
                n = w if c < 2 else PROMPT2
                ins = dve.tensor_tensor(act_lo[:, 0:J, t0:t0 + n], conv_a[:, :, t0:t0 + n],
                                        act_hi[:, 0:J, t0:t0 + n].bitcast(F32), ALU.subtract)
                if c == 2:
                    ins = dve.tensor_tensor(stk[:, 0:J, SMP:P], conv_a[:, :, SEQ:TOK],
                                            stk[:, 0:J, 0:SMP].bitcast(F32), ALU.subtract)
                ins.then_inc(ylo_done, 1)

            dve.wait_ge(ada_evac, ADA_G)
            scales(sc_f, M_SCF, C_GFFN)

            def add_tile(t, bank, first):
                src = ps[:, bank:bank + 2, :].rearrange("p a b -> p (a b)")
                if t < NT - 1:
                    dve.tensor_tensor(src, src, gt_p[:, :], ALU.mult).then_inc(gated, 1)
                    dve.wait_ge(gated, first + 1)
                    dve.tensor_tensor(x2[:, t, :], x2[:, t, :], src, ALU.add).then_inc(rmw_done, 1)
                else:
                    dve.tensor_tensor(src[0:SMP], src[0:SMP], gt_s[:, :], ALU.mult).then_inc(gated, 1)
                    dve.tensor_tensor(src[SMP:P], src[SMP:P], gt_s[:, :], ALU.mult).then_inc(gated, 1)
                    dve.wait_ge(gated, first + 2)
                    dve.tensor_tensor(x2[0:SMP, t, :], x2[0:SMP, t, :], src[0:SMP], ALU.add).then_inc(gated, 1)
                    dve.wait_ge(gated, first + 3)
                    dve.tensor_tensor(x2[0:SMP, t, :], x2[0:SMP, t, :], src[SMP:P], ALU.add).then_inc(rmw_done, 1)

            GATED = NT - 1 + 3
            dve.wait_ge(gt_cp, 2)
            dve.wait_ge(sc_done, 2)
            for t in range(NT):
                n = NT + t
                dve.wait_ge(x_in[t], 32)
                dve.wait_ge(tile_done, t + 1)
                add_tile(t, 0 if t % 2 == 0 else 2, t)
                if t > 0:
                    modulate(n - 1, t - 1, sc_f, M_SHF, 1, n - 1)
                dve.wait_ge(tr_done, n)
                scale_rows(n, t, x2, xn[0:rows[t], 0, :])
            modulate(2 * NT - 1, NT - 1, sc_f, M_SHF, 1, 2 * NT - 1)

            def squares(b):
                for q in range(12):
                    i, c = q // NC, q % NC
                    r, f = relu[:, q % 2, 0:CW[c]], relu2[:, q % 2, 0:CW[c]]
                    dve.wait_ge(up_evac, 12 * b + q + 1)
                    dve.tensor_tensor(f, r, r, ALU.mult).then_inc(r2_done, 1)
                    dve.wait_ge(r2_done, 12 * b + q + 1)
                    dve.wait_ge(ffhi_done, 12 * b + q + 1)
                    n = CH if c < 2 else PROMPT2
                    cols = slice(c * CH, c * CH + n)
                    ins = dve.tensor_tensor(wb_lo[:, FI + i, cols], f[:, 0:n], wb_hi[:, FI + i, cols].bitcast(F32),
                                            ALU.subtract)
                    if c == 2:
                        ins = dve.tensor_tensor(stk[:, i, SMP:P], f[:, PROMPT2:CW[c]], stk[:, i, 0:SMP].bitcast(F32),
                                                ALU.subtract)
                    ins.then_inc(fflo_done, 1)

            def mlp(b, last):
                squares(b)
                if last:
                    dve.wait_ge(gf_in, 16)
                if isinstance(b, int) and b == 0:
                    dve.wait_ge(gt_cp, 4)
                for t in range(NT):
                    dve.wait_ge(tile_done, NT * (b + 1) + t + 1)
                    add_tile(t, 6 if t % 2 == 0 else 4, GATED * (b + 1) + t)
                    if last and t > 0:
                        final(t - 1)
                if last:
                    final(NT - 1)

            def final(t):
                r = rows[t]
                dve.wait_ge(std_done, 2 * NT + t + 1)
                own(dve.reciprocal(ssq[0:r, 2, t:t + 1], ssq[0:r, 1, t:t + 1]))
                dve.scalar_tensor_tensor(out=x2[0:r, t, :], in0=x2[0:r, t, :], scalar=ssq[0:r, 2, t:t + 1],
                                         in1=raw[0:r, 0, :], op0=ALU.mult, op1=ALU.mult).then_inc(fin_y, 1)

            mlp(0, False)
            with dve.Fori(1, NBLK - 1) as b:
                mlp(b, False)
            mlp(NBLK - 1, True)

        @block.tensor
        def _(pe):
            mm = nc.tensor.matmul
            pe.wait_ge(pool_set, 1)
            pe.wait_ge(c_silu, 1)
            for k in range(KD):
                last = nc.tensor.transpose(ps[:, 0, 9 * k:9 * k + 9], ld_c[0:9, 1, k * P:(k + 1) * P], ident[0:9, 0:9])
            last.then_inc(c_tr, 1)
            pe.wait_ge(par_in, 16 * N_ROWS_PAR)
            nc.tensor.transpose(ps[:, 1, 0:N_PAR], ld_par[0:N_PAR, 0, :], ident[0:N_PAR, 0:N_PAR])
            nc.tensor.transpose(ps[:, 1, P:P + KA * J], ld_par[0:KA * J, 1, :], ident[0:KA * J, 0:KA * J])
            nc.tensor.transpose(ps[:, 1, 256:288], ld_par[0:32, 2, :], ident[0:32, 0:32])
            for j in range(J):
                last = nc.tensor.transpose(ps[:, 1, 288 + 24 * j:312 + 24 * j], ld_sb[:, j * P:(j + 1) * P],
                                           ident[0:24, 0:24])
            last.then_inc(par_tr, 1)
            pe.wait_ge(sa_in, 32)
            for h in range(2):
                for j in range(J):
                    last = nc.tensor.transpose(ps[:, 2 + h, 120 * j:120 * j + 120], ld_sa[:, h, j * P:(j + 1) * P],
                                               ident[0:120, 0:120])
                last.then_inc(sa_tr, 1)

            def ada(i, bank, wh, wl, used):
                for h in range(2):
                    c = stk[:, 2 * i + h, :]
                    mm(ps[:, bank, :], c, wh[:, h * GW:(h + 1) * GW], start=(i == 0 and h == 0), stop=False)
                    last = mm(ps[:, bank, :], c, wl[:, h * GW:(h + 1) * GW], start=False, stop=(i == 3 and h == 1))
                last.then_inc(used, 1)

            def group_turn(g, bank, col):
                pe.wait_ge(rows_out, g + 1)
                for i in range(4):
                    last = mm(ps[:, bank, col + 9 * i:col + 9 * i + 9], ada_rows[:, i * P:(i + 1) * P], pick[:, :],
                              start=True, stop=True)
                last.then_inc(ada_tr, 1)

            def turn(n, t, src):
                pe.wait_ge(xn_done, n + 1)
                if n >= 2:
                    pe.wait_ge(hf_d, n - 1)
                    pe.wait_ge(hf_a, hfa(n - 2))
                b, r = bank_pair(n), rows[t]
                for k in range(KD):
                    last = nc.tensor.transpose(ps[:, b + k // 4, (k % 4) * P:(k % 4) * P + r],
                                               src[0:r, k * P:(k + 1) * P], ident[0:r, 0:r])
                last.then_inc(tr_done, 1)

            pe.wait_ge(c_cp, 2)
            pe.wait_ge(c_zero, 2)
            for g in range(ADA0):
                for i in range(4):
                    e = 4 * g + i
                    pe.wait_ge(ada0_hi, e + 1)
                    pe.wait_ge(ada0_lo, e + 1)
                    if i == 0 and g >= 2:
                        pe.wait_ge(rows_out, g - 1)
                    ada(i, 6 + g % 2, w_hi[:, e % 2, :], w_lo[:, e % 2, :], ada0_used)
                    if i == 2 and g > 0:
                        group_turn(g - 1, 0, P + 36 * (g - 1))
            turn(0, 0, x2[:, 0, :])
            group_turn(ADA0 - 1, 0, P + 36 * (ADA0 - 1))

            def strip(slot, bank, c, done):
                for k in range(KD):
                    wh, wl = w_hi[:, slot, k * P:(k + 1) * P], w_lo[:, slot, k * P:(k + 1) * P]
                    xh, xl = act_hi[:, k, c * CH:c * CH + CW[c]], act_lo[:, k, c * CH:c * CH + CW[c]]
                    out = ps[:, bank + c, 0:CW[c]]
                    mm(out, wh, xh, start=(k == 0), stop=False)
                    mm(out, wh, xl, start=False, stop=False)
                    last = mm(out, wl, xh, start=False, stop=(k == KD - 1))
                last.then_inc(done, 1)

            def step(m, first):
                for s, bank, done, out in ((0, 0, strip_a, evac_a), (1, 3, strip_b, evac_b)):
                    pe.wait_ge(hi_ready, 2 * m + s + 1)
                    pe.wait_ge(lo_ready, 2 * m + s + 1)
                    for c in range(NC):
                        if first and s == 0:
                            for t in ((1, 2, 3, 4), (5, 6, 7), (8,))[c]:
                                turn(t, t, x2[:, t, :])
                            pe.wait_ge(nhi_done, min(3 * c + 3, NT))
                            pe.wait_ge(nlo_done, min(3 * c + 3, NT))
                        if not first:
                            pe.wait_ge(out, NC * m - 2 + c)
                        strip(s, bank, c, done)
                        if c == 0 and s == 0 and not first:
                            group_turn(m + ADA0 - 1, 7, 0)
                        if first and s == 0:
                            pieces = ((), (), (0, 1))[c]
                        else:
                            pieces = ((), (2 * s,), (2 * s + 1,))[c]
                        for i in pieces:
                            pe.wait_ge(ada_hi, 4 * m + i + 1)
                            pe.wait_ge(ada_lo, 4 * m + i + 1)
                            if i == 0 and first:
                                pe.wait_ge(hf_d, NT)
                                pe.wait_ge(hf_a, hfa(NT - 1))
                            ada(i, 6, aw_hi[:, i % 2, :], aw_lo[:, i % 2, :], ada_used)

            pe.wait_ge(par_cp, 4)
            pe.wait_ge(sa_cp, 2)
            pe.wait_ge(ada_evac, ADA0)
            step(0, True)
            with pe.Fori(1, 2 * J) as m:
                step(m, False)

            group_turn(ADA_G - 1, 7, 0)

            def turn_state(n, bank, r, src):
                wait(pe, st_cp, n - 1)
                for j in range(J):
                    last = nc.tensor.transpose(ps[0:r, bank, j * P:(j + 1) * P], src(j), ident[:, :])
                last.then_inc(st_tr, 1)

            pe.wait_ge(ada_evac, ADA_G)
            pe.wait_ge(ga_ready, 2 * J + 1)
            turn_state(0, 6, KA - 1, lambda j: ga[:, j, SEQ:GA_P])
            pe.wait_ge(tails, 1)
            for h in range(2):
                turn_state(1 + h, 7 - h, 4 * (KA - 1), lambda j: tail_a[:, j, 120 * h:120 * h + 120])
            pe.wait_ge(evac_a, 2 * J * NC)
            turn_state(3, 7, KB - 1, lambda j: rec[:, j, SEQ:RB_P])
            turn_state(4, 6, NB * (KB - 1), lambda j: tail_b[:, j, :])

            pe.wait_ge(wg_in, 64)
            for j in range(J):
                pe.wait_ge(convb_tap, 2 * KB * (j + 1))
                for g, done, out in ((0, gate_a, evac_a), (1, gate_x, evac_b)):
                    for c in range(NC):
                        pe.wait_ge(out, NC * (2 * J + j) - 2 + c)
                        mm(ps[:, 3 * g + c, 0:CW[c]], wg[:, g, j, :], cb[:, j, c * CH:c * CH + CW[c]],
                           start=True, stop=True).then_inc(done, 1)

            def mean(c, bank, src, done):
                for j in range(J):
                    last = mm(ps[:, bank, 0:CW[c]], mean_w[:, :], src(j), start=(j == 0), stop=(j == J - 1))
                last.then_inc(done, 1)

            def mean_a(c):
                wait(pe, xc_done, c)
                mean(c, 6, lambda j: conv_a[:, j, c * CH:c * CH + CW[c]], mean_done)

            def var_a(c):
                pe.wait_ge(sq_done, c + 1)
                wait(pe, sd_done, c)
                mean(c, 7, lambda j: sq[:, j, 0:CW[c]], var_done)

            pe.wait_ge(conva_tap, 2 * KA * J)
            pe.wait_ge(st_cp, 5)
            mean_a(0)
            mean_a(1)
            var_a(0)
            mean_a(2)
            var_a(1)
            var_a(2)
            pe.wait_ge(yb_done, J)
            pe.wait_ge(xc_done, NC)
            for j in range(J):
                last = nc.tensor.transpose(ps[0:9, 6, j * P:(j + 1) * P], h_end[:, j, :], ident[:, :])
            last.then_inc(st_tr, 1)

            def gates(row0, bank_p, bank_s):
                for k in range(KD):
                    g = mod[:, row0 + k, :]
                    last = mm(ps[:, bank_p + k // 4, (k % 4) * P:(k % 4 + 1) * P], g[:, 0:1].broadcast_to([P, P]),
                              ident[:, :], start=True, stop=True)
                last.then_inc(gt_mm, 1)
                for k in range(KD):
                    last = mm(ps[0:SMP, bank_s + k // 4, (k % 4) * P:(k % 4 + 1) * P],
                              gt_tok[:, int(row0 == M_GTF), k, :], ident[:, :],
                              start=True, stop=True)
                last.then_inc(gt_mm, 1)

            pe.wait_ge(evac_a, 3 * J * NC)
            pe.wait_ge(evac_b, 3 * J * NC)
            pe.wait_ge(ya_done, NC)
            pe.wait_ge(tails, 2)
            gates(M_GTM, 0, 2)

            def tile_product(t, bank, n_k, act_k, ready):
                for k in range(n_k):
                    ready(k)
                    halves = [(ps[:, bank + h, :], wb_hi[:, k, h * 512:(h + 1) * 512],
                               wb_lo[:, k, h * 512:(h + 1) * 512]) for h in range(2)]
                    end = k == n_k - 1
                    if t < NT - 1:
                        ah, al = act_k(k)
                        for out, wh, wl in halves:
                            mm(out, ah, wh, start=(k == 0), stop=False)
                            mm(out, ah, wl, start=False, stop=False)
                        for out, wh, wl in halves:
                            last = mm(out, al, wh, start=False, stop=end)
                    else:
                        for out, wh, wl in halves:
                            mm(out, stk[:, k, :], wh, start=(k == 0), stop=False)
                            last = mm(out, stk[:, k, :], wl, start=False, stop=end)
                last.then_inc(tile_done, 1)

            pe.wait_ge(gt_cp, 2)
            pe.wait_ge(yhi_done, J + NC)
            pe.wait_ge(ylo_done, J + NC)

            def w_out_ready(k):
                pe.wait_ge(hi_ready, W_OUT0 + k + 1)
                pe.wait_ge(lo_ready, W_OUT0 + k + 1)

            for t in range(NT):
                wait(pe, rmw_done, t - 1)
                tile_product(t, 0 if t % 2 == 0 else 2, KD,
                             lambda k: (act_hi[:, k, t * P:(t + 1) * P], act_lo[:, k, t * P:(t + 1) * P]),
                             w_out_ready if t == 0 else lambda k: None)
                if t > 0:
                    if t == 1:
                        pe.wait_ge(st_cp, 6)
                    turn(NT + t - 1, t - 1, xn[:, 0, :])

            def mlp(b, first):
                n = W_MLP0 + 8 * b
                for i in range(FI):
                    at = (0, 1, 4, 7)[i]
                    pe.wait_ge(hi_ready, n + at + 1)
                    pe.wait_ge(lo_ready, n + at + 1)
                    if i == 1:
                        pe.wait_ge(rmw_done, NT * b + NT - 1)
                    for c in range(NC):
                        if first and i == 0:
                            if c == 0:
                                pe.wait_ge(rmw_done, NT)
                            if c == 2:
                                turn(2 * NT - 1, NT - 1, xn[:, 0, :])
                            pe.wait_ge(nhi_done, NT + min(3 * c + 3, NT))
                            pe.wait_ge(nlo_done, NT + min(3 * c + 3, NT))
                        wait(pe, up_evac, 12 * b + 3 * i + c - 5)
                        strip(i % 2, 3 * (i % 2), c, up_done)
                if first:
                    pe.wait_ge(up_evac, 12)
                    gates(M_GTF, 6, 4)
                    pe.wait_ge(gt_cp, 4)
                for t in range(NT):
                    pe.wait_ge(rmw_done, NT * (b + 1) + max(t - 1, 0))
                    if t == 1:
                        pe.wait_ge(up_evac, 12 * b + 12)

                    def ready(k):
                        if t == 0:
                            pe.wait_ge(hi_ready, n + (3, 4, 6, 7)[k])
                            pe.wait_ge(lo_ready, n + (3, 4, 6, 7)[k])
                        if t % NC == 0:
                            pe.wait_ge(ffhi_done, 12 * b + 3 * k + t // NC + 1)
                            pe.wait_ge(fflo_done, 12 * b + 3 * k + t // NC + 1)
                    tile_product(t, 6 if t % 2 == 0 else 4, FI,
                                 lambda k: (wb_hi[:, FI + k, t * P:(t + 1) * P], wb_lo[:, FI + k, t * P:(t + 1) * P]),
                                 ready)

            mlp(0, True)
            with pe.Fori(1, NBLK) as b:
                mlp(b, False)


def hfa(n):
    return n + 1 - (n >= NT - 1) - (n >= 2 * NT - 1)


_INS = ["x_prompt", "x_sample", "c_prompt", "c_sample", "state_conv_a", "state_conv_b", "state_lru_h",
        "w_ada", "b_ada", "g_mix", "w_in", "b_in", "conv_a_w", "conv_a_b", "ln_a_g", "ln_a_b", "conv_b_w",
        "conv_b_b", "w_gate_a", "b_gate_a", "w_gate_x", "b_gate_x", "lru_lambda", "w_out", "g_ffn", "w_up",
        "w_down", "g_final"]
_OUTS = [(1, SEQ, D), (NB, TB, D), (1, 1, KA - 1, WA), (1, 1, KB - 1, WA), (1, 1, WA),
         (1, NB, KA - 1, WA), (1, NB, KB - 1, WA), (1, NB, WA)]


def kernel(**inputs):
    import numpy as _np
    import concourse.bacc as _bacc
    from concourse.bass_utils import run_bass_kernel_spmd as _run

    nc = _bacc.Bacc("TRN2", target_bir_lowering=False, num_devices=1, dynamic_dma_scratch_size=1024)
    arrays, args = {}, []
    for name in _INS:
        a = _np.ascontiguousarray(inputs[name])
        arrays[f"in_{name}"] = a
        args.append(nc.dram_tensor(f"in_{name}", a.shape, mybir.dt.from_np(a.dtype), kind="ExternalInput").ap())
    for i, shape in enumerate(_OUTS):
        args.append(nc.dram_tensor(f"out_{i}", shape, F32, kind="ExternalOutput").ap())
    trunk(nc, *args)
    r = _run(nc, [arrays], core_ids=[0])
    return tuple(r.results[0][f"out_{i}"] for i in range(len(_OUTS)))
```

```python
from contextlib import ExitStack

import concourse.bass as bass
from concourse import mybir

F32 = mybir.dt.float32
F32R = mybir.dt.float32r
ALU = mybir.AluOpType
ACT = mybir.ActivationFunctionType
AX = mybir.AxisListType

P = 128
D = 1024
KD = D // P
SEQ = 1024
NB, TB = 8, 8
SMP = NB * TB
TOK = SEQ + SMP
NT = SEQ // P + 1
WA = 512
J = WA // P
KA, KB = 31, 4
FF = 4096
FI = 4
NBLK = FF // (FI * P)
CH = 384
NC = 3
CW = [CH, CH, TOK - 2 * CH]
PROMPT2 = SEQ - 2 * CH
GA_P = KA - 1 + SEQ
GA_S = KA - 1 + TB
GA_W = GA_P + NB * GA_S
RB_P = KB - 1 + SEQ
RB_S = KB - 1 + TB
RB_W = RB_P + NB * RB_S
STEPS_A = KA + 2
EPS = 1e-6
N_ROWS_PAR = 15

C_BIN, C_BADA, C_GMIX, C_GFFN, C_CAB, C_LNG, C_LNB, C_CBB, C_BGA, C_BGX, C_LAM, C_CBW = (
    0, 16, 64, 72, 80, 84, 88, 92, 96, 100, 104, 108)
N_PAR = C_CBW + KB * J
M_SHM, M_SCM, M_GTM, M_SHF, M_SCF, M_GTF = (8 * i for i in range(6))
GW = 512
ADA0 = 4
ADA_G = 6 * D // GW
AHEAD = 4
C_LO = 32
W_OUT0 = 16
W_MLP0 = W_OUT0 + KD


def trunk(nc, x_prompt, x_sample, c_prompt, c_sample, state_conv_a, state_conv_b, state_lru_h,
          w_ada, b_ada, g_mix, w_in, b_in, conv_a_w, conv_a_b, ln_a_g, ln_a_b, conv_b_w, conv_b_b,
          w_gate_a, b_gate_a, w_gate_x, b_gate_x, lru_lambda, w_out, g_ffn, w_up, w_down, g_final,
          y_prompt, y_sample, ca_prompt, cb_prompt, h_prompt, ca_sample, cb_sample, h_sample):
    ctx = ExitStack()
    with ctx:
        def sb(name, shape, dt=F32):
            return ctx.enter_context(nc.sbuf_tensor(name, shape, dt))

        def shared(*layouts):
            out = {}
            for n, layout in enumerate(layouts):
                scope = ExitStack()
                for name, shape, dt in layout:
                    out[name] = scope.enter_context(nc.sbuf_tensor(name, shape, dt))
                if n < len(layouts) - 1:
                    scope.close()
                else:
                    ctx.push(scope)
            return out

        def sem(name):
            return ctx.enter_context(nc.semaphore(name))

        ident = sb("ident", [P, P])
        mean_w = sb("mean_w", [P, P])
        par = sb("par", [P, N_PAR])
        caw = sb("caw", [P, KA * J])
        mod = sb("mod", [P, 48, 9])
        sc_m = sb("sc_m", [P, KD, 9])
        sc_f = sb("sc_f", [P, KD, 9])
        pick = sb("pick", [P, 9])
        h_end = sb("h_end", [P, J, 9])
        h0 = sb("h0", [P, NB, J])
        hb = sb("hb", [P, 2, J])
        k4 = sb("k4", [P, 2, J])
        sp = sb("sp", [P, 5, J])
        eps = sb("eps", [P, 1])
        ssq = sb("ssq", [P, 3, NT])
        h0_a = sb("h0_a", [P, NB])
        raw = sb("raw", [P, 2, D])
        tail_b = sb("tail_b", [P, J, NB * (KB - 1)])
        tail_bp = sb("tail_bp", [P, J, KB - 1])
        rr = shared([("tail_a", [P, J, NB * (KA - 1)], F32)],
                    [("gt_tok", [P, 2, KD, SMP], F32)])
        tail_a, gt_tok = rr["tail_a"], rr["gt_tok"]
        w_hi = sb("w_hi", [P, 2, D], F32R)
        w_lo = sb("w_lo", [P, 2, D], F32R)
        stk = sb("stk", [P, KD, P], F32R)
        rx = shared([("conv_a_below", [P, J, TOK], F32), ("smp_prod", [P, 2, SMP, KA], F32)],
                    [("conv_a", [P, J, TOK], F32), ("gel", [P, J, TOK], F32)],
                    [("x2", [P, NT, D], F32)])
        conv_a, smp_prod, gel, x2 = rx["conv_a"], rx["smp_prod"], rx["gel"], rx["x2"]
        rh = shared([("ada0", [P, ADA0, KD, GW], F32)],
                    [("act_hi", [P, KD, TOK], F32R), ("act_lo", [P, KD, TOK], F32R)])
        ada0, act_hi, act_lo = rh["ada0"], rh["act_hi"], rh["act_lo"]
        rw = shared([("ld_sa", [120, 2, WA], F32), ("ld_c", [9, 2, D], F32),
                     ("ld_par", [P, 3, P], F32), ("ld_sb", [NB * (KB - 1), WA], F32)],
                    [("lru", [P, J, TOK], F32), ("ga", [P, J, GA_W], F32), ("rec", [P, J, RB_W], F32),
                     ("sg", [P, TOK], F32), ("ada_rows", [P, GW], F32),
                     ("tail_p", [P, J, KA - 1], F32)],
                    [("aw_hi", [P, 2, D], F32R), ("aw_lo", [P, 2, D], F32R)],
                    [("wb_hi", [P, KD, D], F32R), ("wb_lo", [P, KD, D], F32R)])
        ld_sa, ld_c, ld_par, ld_sb = (rw[n] for n in ("ld_sa", "ld_c", "ld_par", "ld_sb"))
        lru, ga, rec, sg, wb_hi, wb_lo = (rw[n] for n in ("lru", "ga", "rec", "sg", "wb_hi", "wb_lo"))
        tail_p = rw["tail_p"]
        cb = ga[:, :, 0:TOK]
        ada_rows, aw_hi, aw_lo = rw["ada_rows"], rw["aw_hi"], rw["aw_lo"]
        rg = shared([("gt_p", [P, D], F32), ("gt_s", [SMP, D], F32)],
                    [("wg", [P, 2, J, P], F32), ("rstd", [P, TOK], F32)])
        wg, rstd, gt_p, gt_s = rg["wg"], rg["rstd"], rg["gt_p"], rg["gt_s"]
        rt = shared([("sq", [P, J, CH], F32)], [("relu", [P, 2, CH], F32), ("relu2", [P, 2, CH], F32)],
                    [("stage", [P, 4, WA], F32)], [("raw_ada", [P, 2, 2 * GW], F32)], [("xn", [P, 2, D], F32)])
        raw_ada = rt["raw_ada"]
        sq, relu, relu2, stage, xn = rt["sq"], rt["relu"], rt["relu2"], rt["stage"], rt["xn"]
        ps = ctx.enter_context(nc.psum_tensor("ps", [P, 8, 512], F32))

        c_in, par_in, sa_in, wg_in = (sem(n) for n in ("c_in", "par_in", "sa_in", "wg_in"))
        x_in = [sem(f"x_in{t}") for t in range(NT)]
        ada0_in = [sem(f"ada0_in{g}") for g in range(4)]
        raw_in = [sem("raw_in0"), sem("raw_in1")]
        gf_in, stored = sem("gf_in"), sem("stored")
        ada_in = [sem("ada_in0"), sem("ada_in1")]
        staged_out = sem("staged_out")
        pool_set = sem("pool_set")
        pool_ord = sem("pool_ord")
        act_ord, dve_ord = sem("act_ord"), sem("dve_ord")
        c_sig, c_silu, c_tr, c_cp = sem("c_sig"), sem("c_silu"), sem("c_tr"), sem("c_cp")
        par_tr, par_cp, sa_tr, sa_cp = sem("par_tr"), sem("par_cp"), sem("sa_tr"), sem("sa_cp")
        ada0_hi, ada0_lo, ada0_used = sem("ada0_hi"), sem("ada0_lo"), sem("ada0_used")
        ada_hi, ada_lo, ada_used = sem("ada_hi"), sem("ada_lo"), sem("ada_used")
        rows_out, ada_tr, ada_evac = sem("rows_out"), sem("ada_tr"), sem("ada_evac")
        c_zero = sem("c_zero")
        std_done, xn_done = sem("std_done"), sem("xn_done")
        tr_done, hf_d, hf_a = sem("tr_done"), sem("hf_d"), sem("hf_a")
        nhi_done, nlo_done = sem("nhi_done"), sem("nlo_done")
        sc_done = sem("sc_done")
        hi_ready, lo_ready = sem("hi_ready"), sem("lo_ready")
        strip_a, strip_b = sem("strip_a"), sem("strip_b")
        evac_a, evac_b = sem("evac_a"), sem("evac_b")
        ga_ready, conva_tap, convb_tap = sem("ga_ready"), sem("conva_tap"), sem("convb_tap")
        smp_ready, smp_sum = sem("smp_ready"), sem("smp_sum")
        gated, tails = sem("gated"), sem("tails")
        st_tr, st_cp = sem("st_tr"), sem("st_cp")
        gate_a, gate_x = sem("gate_a"), sem("gate_x")
        a_done, th_done, q_done, m_done, h_done, yb_done = (
            sem(n) for n in ("a_done", "th_done", "q_done", "m_done", "h_done", "yb_done"))
        k_done = sem("k_done")
        mean_done, xc_done, sq_done, var_done, sd_done, xs_done, sig_done, ya_done = (
            sem(n) for n in ("mean_done", "xc_done", "sq_done", "var_done", "sd_done", "xs_done",
                             "sig_done", "ya_done"))
        yhi_done, ylo_done = sem("yhi_done"), sem("ylo_done")
        gt_mm, gt_cp = sem("gt_mm"), sem("gt_cp")
        tile_done, rmw_done = sem("tile_done"), sem("rmw_done")
        up_done, up_evac, r2_done, ffhi_done, fflo_done = (
            sem(n) for n in ("up_done", "up_evac", "r2_done", "ffhi_done", "fflo_done"))
        fin_y = sem("fin_y")

        ga_s = ga[:, :, GA_P:GA_W].rearrange("p j (b s) -> p j b s", s=GA_S)
        caw_j = caw[:, :].rearrange("p (k j) -> p j k", j=J)
        prod_v = smp_prod[:, :, :, :].rearrange("p s (b t) k -> p s b t k", t=TB)
        rec_s = rec[:, :, RB_P:RB_W].rearrange("p j (b s) -> p j b s", s=RB_S)
        win_v = w_in[0].rearrange("(k p) n -> p k n", p=P)
        wada_v = w_ada[0].rearrange("(k p) n -> p k n", p=P)
        wdown_v = w_down[0].rearrange("(n p) d -> n p d", p=P)
        wup_v = w_up[0].rearrange("(k p) n -> p k n", p=P)
        raw_k = raw[:, :, :].rearrange("p s (k n) -> p s k n", n=P)
        xs_rows = x_sample.rearrange("b t d -> (b t) d")
        ys_rows = y_sample.rearrange("b t d -> (b t) d")
        rows = [P] * (NT - 1) + [SMP]

        a_t = [lru[:, j, :] for j in range(J)]
        m_t = [rec[:, j, 0:TOK] for j in range(J)]

        def wait(eng, s, value):
            if not isinstance(value, int) or value > 0:
                eng.wait_ge(s, value)

        def wait_apart(eng, s, value):
            eng.wait_ge(pool_set, 1)
            eng.wait_ge(s, value)

        def up_bank(i, c):
            return 3 * (i % 2) + (c + 2) % NC

        def bank_pair(n):
            return 4 if n % 2 == 0 else 6

        block = ctx.enter_context(nc.Block())

        @block.sync
        def _(sp):
            def load_x(t):
                src = x_prompt[0, t * P:(t + 1) * P, :] if t < NT - 1 else xs_rows
                sp.dma_start(x2[0:rows[t], t, :], src).then_inc(x_in[t], 16)

            def load_piece(n_ge, slot, src, view):
                wait(sp, lo_ready, n_ge)
                dst = raw_k[:, slot, :, :] if view else raw[:, slot, :]
                sp.dma_start(dst, src).then_inc(raw_in[slot], 16)

            def load_ada(m, i):
                wait(sp, ada_lo, 4 * m + i - 1)
                sp.dma_start(raw_ada[:, i % 2, :].rearrange("p (k n) -> p k n", n=GW),
                             wada_v[:, 2 * i:2 * i + 2, bass.ds(m * GW + ADA0 * GW, GW)]).then_inc(ada_in[i % 2], 16)

            sp.wait_ge(c_in, 32)
            load_x(0)
            for g in range(ADA0):
                sp.dma_start(ada0[:, g, :, :], wada_v[:, :, g * GW:(g + 1) * GW]).then_inc(ada0_in[g], 16)
                if g == 0:
                    sp.wait_ge(par_in, 16 * N_ROWS_PAR)
                    sp.wait_ge(sa_in, 32)
                if g < 2:
                    load_x(g + 1)
            for s in range(2):
                load_piece(0, s, win_v[:, :, s * WA:s * WA + P], True)
            for t in range(3, NT):
                load_x(t)
            sp.wait_ge(nlo_done, NT)
            sp.wait_ge(nhi_done, NT)
            load_ada(0, 0)
            load_ada(0, 1)

            def step(m, nxt, apart=WA):
                if nxt is not None:
                    for s in range(2):
                        load_piece(2 * m + s + 1, s, win_v[:, :, bass.ds(nxt + s * apart, P)], True)
                load_ada(m, 2)
                load_ada(m, 3)
                if nxt is not None:
                    load_ada(m + 1, 0)
                    load_ada(m + 1, 1)

            with sp.Fori(0, J - 1) as j:
                step(j, (j + 1) * P)
            step(J - 1, 2 * WA, P)
            with sp.Fori(0, J - 1) as j:
                step(j + J, (j + 1) * (2 * P) + 2 * WA, P)
            step(2 * J - 1, None)
            for k in range(KD):
                load_piece(W_OUT0 + k - 1, k % 2, w_out[0, k * P:(k + 1) * P, :], False)
            sp.wait_ge(yhi_done, J + NC)
            sp.wait_ge(ylo_done, J + NC)
            for t in range(NT):
                load_x(t)

            def down_piece(n, b, i, slot):
                load_piece(n - 1, slot, wdown_v[b * FI + i, :, :], False)

            def mlp(b, last):
                n = W_MLP0 + 2 + 8 * b
                down_piece(n, b, 0, 0)
                down_piece(n + 1, b, 1, 1)
                load_piece(n + 1, 0, wup_v[:, :, bass.ds(b * (FI * P) + 2 * P, P)], True)
                down_piece(n + 3, b, 2, 1)
                down_piece(n + 4, b, 3, 0)
                load_piece(n + 4, 1, wup_v[:, :, bass.ds(b * (FI * P) + 3 * P, P)], True)
                if not last:
                    load_piece(n + 5, 0, wup_v[:, :, bass.ds(b * (FI * P) + 4 * P, P)], True)
                    load_piece(n + 6, 1, wup_v[:, :, bass.ds(b * (FI * P) + 5 * P, P)], True)

            load_piece(W_MLP0 - 1, 0, wup_v[:, :, 0:P], True)
            load_piece(W_MLP0, 1, wup_v[:, :, P:2 * P], True)
            with sp.Fori(0, NBLK - 1) as b:
                mlp(b, False)
            mlp(NBLK - 1, True)
            sp.wait_ge(hi_ready, W_MLP0 + 8 * NBLK)
            sp.wait_ge(lo_ready, W_MLP0 + 8 * NBLK)
            sp.dma_start(raw[:, 0, :], g_final.partition_broadcast(P)).then_inc(gf_in, 16)
            for t in range(NT):
                sp.wait_ge(fin_y, t + 1)
                dst = y_prompt[0, t * P:(t + 1) * P, :] if t < NT - 1 else ys_rows
                sp.dma_start(dst, x2[0:rows[t], t, :]).then_inc(stored, 16)
            sp.wait_ge(stored, 16 * NT)

        @block.gpsimd
        def _(pool):
            pool.memset(ident[:, :], 0.0).then_inc(pool_ord, 1)
            pool.wait_ge(pool_ord, 1)
            pool.affine_select(out=ident[:, :], in_=ident[:, :], compare_op=ALU.not_equal, fill=1.0,
                               base=0, pattern=[[-1, P]], channel_multiplier=1).then_inc(pool_set, 1)
            pool.memset(mean_w[:, :], 1.0 / WA).then_inc(pool_set, 1)
            pool.memset(eps[:, :], EPS).then_inc(pool_set, 1)
            pool.memset(ga[:, :, 0:KA - 1], 0.0).then_inc(ga_ready, 1)
            pool.memset(rec[:, :, 0:KB - 1], 0.0).then_inc(pool_set, 1)
            pool.memset(wg[:, :, :, :], 0.0).then_inc(pool_set, 1)

            def lo(n, slot, dst, hi):
                pool.wait_ge(hi_ready, n + 1)
                pool.tensor_tensor(dst, raw[:, slot, :], hi.bitcast(F32), ALU.subtract).then_inc(lo_ready, 1)

            def strip_lo(n, slot, used, count):
                wait(pool, used, count)
                lo(n, slot, w_lo[:, slot, :], w_hi[:, slot, :])

            def split_ada(q, slot):
                pool.wait_ge(ada_hi, q + 1)
                pool.tensor_tensor(aw_lo[:, slot, :], raw_ada[:, slot, :],
                                   aw_hi[:, slot, :].bitcast(F32), ALU.subtract).then_inc(ada_lo, 1)

            pool.wait_ge(ada0_used, 4 * ADA0)
            strip_lo(0, 0, strip_a, 0)
            strip_lo(1, 1, strip_b, 0)
            split_ada(0, 0)
            split_ada(1, 1)

            def product(j):
                pool.wait_ge(evac_b, NC * (j + 1))
                pool.wait_ge(evac_a, NC * (j + 1))
                pool.tensor_tensor(ga[:, j, KA - 1:GA_P], ga[:, j, KA - 1:GA_P], sg[:, 0:SEQ],
                                   ALU.mult).then_inc(ga_ready, 1)
                pool.tensor_tensor(ga_s[:, j, :, KA - 1:GA_S], ga_s[:, j, :, KA - 1:GA_S],
                                   sg[:, SEQ:TOK].rearrange("p (b t) -> p b t", t=TB),
                                   ALU.mult).then_inc(ga_ready, 1)

            def sample_taps(j, slot):
                pool.wait_ge(ga_ready, 2 * j + 3)
                wait(pool, smp_sum, j - 1)
                for t in range(TB):
                    last = pool.tensor_tensor(prod_v[:, slot, :, t, :], ga_s[:, j, :, t:t + KA],
                                              caw_j[:, bass.ds(j, 1), :].broadcast_to([P, NB, KA]), ALU.mult)
                last.then_inc(smp_ready, 1)

            def step(m, glu, first, last):
                if not last:
                    strip_lo(2 * m + 2, 0, strip_a, NC * (m + 1))
                split_ada(4 * m + 2, 0)
                split_ada(4 * m + 3, 1)
                if glu and first:
                    product(m)
                    pool.wait_ge(sa_cp, 2)
                    pool.wait_ge(tr_done, NT)
                if not last:
                    strip_lo(2 * m + 3, 1, strip_b, NC * (m + 1))
                    split_ada(4 * m + 4, 0)
                if glu and not first:
                    product(m)
                if not last:
                    split_ada(4 * m + 5, 1)
                if glu:
                    sample_taps(m, m % 2)

            step(0, True, True, False)
            step(1, True, False, False)
            with pool.Fori(2, J) as m:
                step(m, True, False, False)
            step(J, False, False, False)
            pool.wait_ge(ga_ready, 2 * J + 1)
            for j in range(J):
                pool.tensor_copy(tail_a[:, j, :].rearrange("p (b s) -> p b s", b=NB), ga_s[:, j, :, TB:GA_S])
            pool.tensor_copy(tail_p[:, :, :], ga[:, :, SEQ:GA_P]).then_inc(tails, 1)
            with pool.Fori(J + 1, 2 * J - 1) as m:
                step(m, False, False, False)
            step(2 * J - 1, False, False, True)
            pool.wait_ge(evac_a, 2 * J * NC)
            pool.wait_ge(evac_b, 2 * J * NC)
            for j in range(J):
                pool.tensor_copy(tail_b[:, j, :].rearrange("p (b s) -> p b s", b=NB), rec_s[:, j, :, TB:RB_S])
            pool.tensor_copy(tail_bp[:, :, :], rec[:, :, SEQ:RB_P]).then_inc(tails, 1)
            pool.wait_ge(st_tr, 5)
            pool.wait_ge(ada_evac, ADA_G)
            for g, row0 in ((0, M_GTM), (1, M_GTF)):
                for k in range(KD):
                    last = pool.tensor_copy(gt_tok[:, g, k, :].rearrange("p (b t) -> p b t", t=TB),
                                            mod[:, row0 + k, 1:9].unsqueeze(2).broadcast_to([P, NB, TB]))
            last.then_inc(tails, 1)
            pool.wait_ge(yb_done, J)
            pool.wait_ge(conva_tap, STEPS_A * J)
            for k in range(0, KD, 2):
                pool.wait_ge(lo_ready, W_OUT0 + k)
                lo(W_OUT0 + k, k % 2, wb_lo[:, k, :], wb_hi[:, k, :])
            pool.wait_ge(lo_ready, W_OUT0 + KD)

            lo(W_MLP0, 0, w_lo[:, 0, :], w_hi[:, 0, :])
            lo(W_MLP0 + 1, 1, w_lo[:, 1, :], w_hi[:, 1, :])

            def mlp(b, last):
                n = W_MLP0 + 2 + 8 * b
                pool.wait_ge(tile_done, NT * (b + 1))
                lo(n, 0, wb_lo[:, 0, :], wb_hi[:, 0, :])
                lo(n + 1, 1, wb_lo[:, 1, :], wb_hi[:, 1, :])
                strip_lo(n + 2, 0, up_done, 12 * b + 3)
                lo(n + 3, 1, wb_lo[:, 2, :], wb_hi[:, 2, :])
                lo(n + 4, 0, wb_lo[:, 3, :], wb_hi[:, 3, :])
                strip_lo(n + 5, 1, up_done, 12 * b + 6)
                if not last:
                    strip_lo(n + 6, 0, up_done, 12 * b + 9)
                    strip_lo(n + 7, 1, up_done, 12 * b + 12)

            with pool.Fori(0, NBLK - 1) as b:
                mlp(b, False)
            mlp(NBLK - 1, True)

        @block.scalar
        def _(act):
            ordered = [0]

            def own(ins):
                ordered[0] += 1
                ins.then_inc(act_ord, 1)
                act.wait_ge(act_ord, ordered[0])

            def load_rows(dst, src, s):
                act.dma_start(dst, src).then_inc(s, 16)

            load_rows(ld_c[0:1, 0, :], c_prompt, c_in)
            load_rows(ld_c[1:9, 0, :], c_sample, c_in)
            for col, src in ((C_BIN, b_in), (C_BADA, b_ada), (C_CAB, conv_a_b), (C_LNG, ln_a_g),
                             (C_LNB, ln_a_b), (C_CBB, conv_b_b), (C_BGA, b_gate_a), (C_BGX, b_gate_x),
                             (C_LAM, lru_lambda), (C_GMIX, g_mix), (C_GFFN, g_ffn)):
                n = src.shape[1] // P
                load_rows(ld_par[col:col + n, 0, :], src[0].rearrange("(r p) -> r p", p=P), par_in)
            load_rows(ld_par[C_CBW:N_PAR, 0, :], conv_b_w[0].rearrange("k (j p) -> (k j) p", p=P), par_in)
            load_rows(ld_par[0:KA * J, 1, :], conv_a_w[0].rearrange("k (j p) -> (k j) p", p=P), par_in)
            load_rows(ld_par[0:NB * J, 2, :], state_lru_h[0].rearrange("b (j p) -> (b j) p", p=P), par_in)
            load_rows(ld_sb[:, :], state_conv_b[0].rearrange("b s c -> (b s) c"), par_in)
            for half in range(2):
                load_rows(ld_sa[:, half, :], state_conv_a[0, 4 * half:4 * half + 4].rearrange("b s c -> (b s) c"),
                          sa_in)

            act.wait_ge(c_in, 32)
            act.activation(ld_c[:, 1, :], ld_c[:, 0, :], ACT.Sigmoid).then_inc(c_sig, 1)
            act.wait_ge(c_tr, 1)
            act.wait_ge(c_zero, 1)
            act.activation(stk[:, :, 0:9], ps[:, 0, 0:9 * KD].rearrange("p (k c) -> p k c", c=9), ACT.Copy).then_inc(c_cp, 1)

            def norm(n, t, src, junk, wait_free):
                wait_free()
                r = rows[t]
                own(act.activation(junk[0:r, 0:D], src[0:r, t, :], ACT.Square, accum_out=ssq[0:r, 0, t:t + 1]))
                act.activation(ssq[0:r, 1, t:t + 1], ssq[0:r, 0, t:t + 1], ACT.Sqrt, scale=1.0 / D,
                               bias=eps[0:r, :]).then_inc(std_done, 1)

            def modulate(n, t, scale, shift0, slot, free, between=lambda: None):
                hf = xn[:, slot, :].rearrange("p (k c) -> p k c", c=P)
                if t < NT - 1:
                    act.wait_ge(tr_done, n + 1)
                    wait(act, nlo_done, free)
                    for k in range(4, KD):
                        last = act.activation(hf[:, k, :], ps[:, bank_pair(n) + 1, (k - 4) * P:(k - 3) * P],
                                              ACT.Identity, scale=scale[:, k, 0:1],
                                              bias=mod[:, shift0 + k, 0:1])
                    last.then_inc(hf_a, 1)
                    between()
                    act.wait_ge(hf_a, hfa(n))
                act.wait_ge(hf_d, n + 1)
                act.activation(act_hi[:, :, t * P:t * P + rows[t]], hf[:, :, 0:rows[t]], ACT.Copy).then_inc(nhi_done, 1)

            def hi(n, slot, dst, loaded):
                act.wait_ge(raw_in[slot], loaded)
                act.activation(dst, raw[:, slot, :], ACT.Copy).then_inc(hi_ready, 1)

            def strip_hi(n, slot, used, count):
                wait(act, used, count)
                hi(n, slot, w_hi[:, slot, :], 16 * (n // 2 + 1))

            def group_rows(g, bank):
                act.activation(ada_rows[:, :], ps[:, bank, :], ACT.Copy).then_inc(rows_out, 1)

            def group_out(g, bank, col):
                act.wait_ge(ada_tr, g + 1)
                for i in range(4):
                    last = act.activation(mod[:, bass.ds(4 * g + i, 1), :], ps[:, bank, col + 9 * i:col + 9 * i + 9].unsqueeze(1),
                                          ACT.Identity, bias=par[:, bass.ds(C_BADA + i + 4 * g, 1)])
                last.then_inc(ada_evac, 1)

            def ada_split(m, i):
                q, slot = 4 * m + i, i % 2
                wait_apart(act, ada_in[slot], 16 * (2 * m + i // 2 + 1))
                wait(act, ada_used, q - 1)
                act.activation(aw_hi[:, slot, :], raw_ada[:, slot, :],
                               ACT.Copy).then_inc(ada_hi, 1)

            act.wait_ge(pool_set, 3)
            for g in range(ADA0):
                if g < 3:
                    norm(g, g, x2, sg, lambda: act.wait_ge(x_in[g], 16))
                act.wait_ge(ada0_in[g], 16)
                for i in range(4):
                    e = 4 * g + i
                    wait(act, ada0_used, e - 1)
                    act.activation(w_hi[:, e % 2, :], ada0[:, g, 2 * i:2 * i + 2, :].rearrange("p a b -> p (a b)"),
                                   ACT.Copy).then_inc(ada0_hi, 1)
                    if g > 0 and i == 1:
                        act.wait_ge(ada0_used, 4 * g)
                        group_rows(g - 1, 6 + (g - 1) % 2)
                if g > 0:
                    wait(act, par_cp, 1)
                    group_out(g - 1, 0, P + 36 * (g - 1))
            act.wait_ge(ada0_used, 4 * ADA0)
            group_rows(ADA0 - 1, 7)
            group_out(ADA0 - 1, 0, P + 36 * (ADA0 - 1))
            act.wait_ge(pool_set, 5)
            for g, w in ((0, w_gate_a), (1, w_gate_x)):
                for half in range(2):
                    at = slice(64 * half, 64 * half + 64)
                    act.dma_start(wg[at, g, :, at], w[0].rearrange("(j h) i o -> h i j o", h=2)[half]).then_inc(wg_in, 16)
            norm(AHEAD - 1, AHEAD - 1, x2, sg, lambda: act.wait_ge(x_in[AHEAD - 1], 16))
            act.wait_ge(sc_done, 1)
            def norm_ahead(t):
                if t < NT:
                    norm(t, t, x2, sg, lambda: act.wait_ge(x_in[t], 16))

            for t in range(NT):
                modulate(t, t, sc_m, M_SHM, t % 2, t - 1, lambda: norm_ahead(t + AHEAD))
                if t == 0:
                    for s in range(2):
                        strip_hi(s, s, strip_a, 0)

            lam = par[:, C_LAM:C_LAM + J]
            own(act.activation(sp[:, 0, :], lam, ACT.Abs))
            act.activation(sp[:, 1, :], sp[:, 0, :], ACT.Exp, scale=-1.0).then_inc(k_done, 1)
            act.wait_ge(k_done, 2)
            act.activation(sp[:, 3, :], sp[:, 2, :], ACT.Ln).then_inc(k_done, 1)
            act.wait_ge(sa_tr, 2)
            ada_split(0, 0)
            ada_split(0, 1)

            def chunk_out(c, src_bank, dst_p, dst_s, func, bias, done):
                if c < 2:
                    act.activation(dst_p(c * CH, CH), ps[:, src_bank, 0:CH], func, bias=bias).then_inc(done, 1)
                else:
                    act.activation(dst_p(c * CH, PROMPT2), ps[:, src_bank, 0:PROMPT2], func, bias=bias)
                    act.activation(dst_s, ps[:, src_bank, PROMPT2:PROMPT2 + SMP].rearrange("p (b t) -> p b t", t=TB),
                                   func, bias=bias).then_inc(done, 1)

            def value_out(c, bank, j):
                chunk_out(c, bank, lambda o, w: ga[:, j, KA - 1 + o:KA - 1 + o + w], ga_s[:, j, :, KA - 1:GA_S],
                          ACT.Identity, par[:, bass.ds(C_BIN + j, 1)], evac_a)

            def gate_out(c, bank, j):
                chunk_out(c, bank, lambda o, w: sg[:, o:o + w], sg[:, SEQ:TOK].rearrange("p (b t) -> p b t", t=TB),
                          ACT.Sigmoid, par[:, bass.ds(C_BIN + J + j, 1)], evac_b)

            def rec_out(c, bank, j, done):
                chunk_out(c, bank, lambda o, w: rec[:, j, KB - 1 + o:KB - 1 + o + w], rec_s[:, j, :, KB - 1:RB_S],
                          ACT.Identity, par[:, bass.ds(C_BIN + 2 * J + j, 1)], done)

            def gelu_out(c, bank, j, done):
                chunk_out(c, bank, lambda o, w: gel[:, j, o:o + w],
                          gel[:, j, SEQ:TOK].rearrange("p (b t) -> p b t", t=TB), ACT.Gelu_apprx_tanh,
                          par[:, bass.ds(C_BIN + 3 * J + j, 1)], done)

            def step(m, first, last, out_a, out_b):
                if not first:
                    wait_apart(act, ada_used, 4 * m)
                    group_rows(m + ADA0 - 1, 6)
                for c in range(NC):
                    if c == 2 and not first:
                        wait_apart(act, ada_tr, m + ADA0)
                        group_out(m + ADA0 - 1, 7, 0)
                    wait_apart(act, strip_a, NC * m + c + 1)
                    out_a(c, 2 if first and c == 2 else c % 2)
                if not last:
                    act.wait_ge(raw_in[0], 16 * (m + 2))
                    act.activation(w_hi[:, 0, :], raw[:, 0, :], ACT.Copy).then_inc(hi_ready, 1)
                ada_split(m, 2)
                ada_split(m, 3)
                for c in range(NC):
                    wait_apart(act, strip_b, NC * m + c + 1)
                    out_b(c, (c + 1) % 2)
                if not last:
                    act.wait_ge(raw_in[1], 16 * (m + 2))
                    act.activation(w_hi[:, 1, :], raw[:, 1, :], ACT.Copy).then_inc(hi_ready, 1)
                if not last:
                    ada_split(m + 1, 0)
                    ada_split(m + 1, 1)

            def glu_step(j, first):
                def out_b(c, bank):
                    if c == 0:
                        act.wait_ge(ga_ready, 2 * j + 1)
                    gate_out(c, bank, j)
                step(j, first, False, lambda c, bank: value_out(c, bank, j), out_b)

            def rec_step(q):
                step(q + J, False, False, lambda c, bank: rec_out(c, bank, 2 * q, evac_a),
                     lambda c, bank: rec_out(c, bank, 2 * q + 1, evac_b))

            def gelu_step(q, last):
                def out_a(c, bank):
                    if q == 0 and c == 0:
                        act.wait_ge(smp_sum, J)
                    gelu_out(c, bank, 2 * q, evac_a)
                step(q + J + J // 2, False, last, out_a,
                     lambda c, bank: gelu_out(c, bank, 2 * q + 1, evac_b))

            glu_step(0, True)
            with act.Fori(1, J) as j:
                glu_step(j, False)
            with act.Fori(0, J // 2) as q:
                rec_step(q)
            gelu_step(0, False)
            gelu_step(1, True)
            act.wait_ge(ada_used, 4 * 2 * J)
            group_rows(ADA_G - 1, 6)
            act.wait_ge(ada_tr, ADA_G)
            group_out(ADA_G - 1, 7, 0)

            act.wait_ge(k_done, 3 + 8)
            act.wait_ge(strip_b, NC * 2 * J)
            act.wait_ge(ada_used, 4 * 2 * J)

            def layer_norm(c):
                t0, w = c * CH, CW[c]
                act.wait_ge(xc_done, c + 1)
                if c == 0:
                    act.wait_ge(staged_out, 16 * 5)
                act.activation(sq[:, :, 0:w], conv_a[:, :, t0:t0 + w], ACT.Square).then_inc(sq_done, 1)
                act.wait_ge(var_done, c + 1)
                act.activation(rstd[:, t0:t0 + w], ps[:, 7, 0:w], ACT.Sqrt, bias=eps[:, :]).then_inc(sd_done, 1)

            def yb_hi(j):
                act.activation(act_hi[:, J + j, 0:SEQ], gel[:, j, 0:SEQ], ACT.Copy)
                act.activation(stk[:, J + j, 0:SMP], gel[:, j, SEQ:TOK], ACT.Copy).then_inc(yhi_done, 1)

            act.wait_ge(convb_tap, 2 * KB * J)
            act.wait_ge(tails, 2)
            for j in range(J):
                for c in range(NC):
                    act.wait_ge(gate_a, NC * j + c + 1)
                    act.activation(m_t[j][:, c * CH:c * CH + CW[c]], ps[:, c, 0:CW[c]], ACT.Tanh, scale=0.5,
                                   bias=hb[:, 0, j:j + 1]).then_inc(evac_a, 1)
                act.wait_ge(evac_a, NC * (2 * J + j + 1))
                act.activation(a_t[j], m_t[j], ACT.Exp, scale=k4[:, 1, j:j + 1], bias=k4[:, 1, j:j + 1]).then_inc(a_done, 1)
                act.wait_ge(a_done, j + 1)
                act.activation(m_t[j], m_t[j], ACT.Tanh, scale=k4[:, 0, j:j + 1], bias=k4[:, 0, j:j + 1]).then_inc(th_done, 1)
                wait(act, q_done, j)
                for c in range(NC):
                    act.wait_ge(gate_x, NC * j + c + 1)
                    act.activation(sg[:, c * CH:c * CH + CW[c]], ps[:, 3 + c, 0:CW[c]], ACT.Tanh, scale=0.5,
                                   bias=hb[:, 1, j:j + 1]).then_inc(evac_b, 1)
            for j in range(J):
                act.wait_ge(q_done, j + 1)
                act.activation(m_t[j], m_t[j], ACT.Sqrt).then_inc(m_done, 1)

            def staged(n, dst, bank, r):
                act.wait_ge(st_tr, n + 1)
                act.activation(dst, ps[0:r, bank, :], ACT.Copy).then_inc(st_cp, 1)
                act.wait_ge(st_cp, n + 1)

            act.wait_ge(ada_lo, 4 * 2 * J)
            half_rows = 4 * (KA - 1)
            staged(0, stage[0:KA - 1, 2, :], 6, KA - 1)
            act.dma_start(ca_prompt[0, 0], stage[0:KA - 1, 2, :]).then_inc(staged_out, 16)
            for h in range(2):
                staged(1 + h, stage[0:half_rows, h, :], 7 - h, half_rows)
                act.dma_start(ca_sample[0, 4 * h:4 * h + 4].rearrange("b s c -> (b s) c"),
                              stage[0:half_rows, h, :]).then_inc(staged_out, 16)
            staged(3, stage[64:64 + KB - 1, 2, :], 7, KB - 1)
            act.dma_start(cb_prompt[0, 0], stage[64:64 + KB - 1, 2, :]).then_inc(staged_out, 16)
            staged(4, stage[32:32 + NB * (KB - 1), 2, :], 6, NB * (KB - 1))
            act.dma_start(cb_sample[0].rearrange("b s c -> (b s) c"),
                          stage[32:32 + NB * (KB - 1), 2, :]).then_inc(staged_out, 16)

            def w_out_hi(k):
                hi(W_OUT0 + k, k % 2, wb_hi[:, k, :], 16 * ((W_OUT0 + k) // 2 + 1))

            def swish_gate(c):
                t0, w = c * CH, CW[c]
                act.wait_ge(xs_done, c + 1)
                wait(act, ya_done, c)
                act.activation(sq[:, :, 0:w], conv_a[:, :, t0:t0 + w], ACT.Sigmoid).then_inc(sig_done, 1)

            def ya_hi(c):
                act.wait_ge(ya_done, c + 1)
                t0, n = c * CH, CW[c] if c < 2 else PROMPT2
                ins = act.activation(act_hi[:, 0:J, t0:t0 + n], conv_a[:, :, t0:t0 + n], ACT.Copy)
                if c == 2:
                    ins = act.activation(stk[:, 0:J, 0:SMP], conv_a[:, :, SEQ:TOK], ACT.Copy)
                ins.then_inc(yhi_done, 1)

            layer_norm(0)
            layer_norm(1)
            act.wait_ge(yb_done, J)
            w_out_hi(0)
            w_out_hi(1)
            layer_norm(2)
            w_out_hi(2)
            swish_gate(0)
            for j in range(J):
                yb_hi(j)
                if j == 1:
                    w_out_hi(3)
            ya_hi(0)
            w_out_hi(4)
            act.wait_ge(st_tr, 6)
            act.activation(stage[0:9, 3, :], ps[0:9, 6, :], ACT.Copy).then_inc(st_cp, 1)
            act.wait_ge(st_cp, 6)
            act.dma_start(h_prompt[0], stage[0:1, 3, :]).then_inc(staged_out, 16)
            act.dma_start(h_sample[0], stage[1:9, 3, :]).then_inc(staged_out, 16)

            swish_gate(1)
            w_out_hi(5)
            ya_hi(1)
            w_out_hi(6)
            swish_gate(2)
            ya_hi(2)
            w_out_hi(7)

            def gates_out(first, bank_p, bank_s):
                act.wait_ge(gt_mm, first + 1)
                act.activation(gt_p[:, :], ps[:, bank_p:bank_p + 2, :].rearrange("p a b -> p (a b)"), ACT.Copy).then_inc(gt_cp, 1)
                act.wait_ge(gt_mm, first + 2)
                act.wait_ge(xs_done, NC)
                act.activation(gt_s[:, :], ps[0:SMP, bank_s:bank_s + 2, :].rearrange("p a b -> p (a b)"), ACT.Copy).then_inc(gt_cp, 1)

            gates_out(0, 4, 6)
            act.wait_ge(staged_out, 16 * 7)
            act.wait_ge(sc_done, 2)
            for t in range(NT):
                n = NT + t
                if t == 3:
                    strip_hi(W_MLP0, 0, strip_a, 0)
                    strip_hi(W_MLP0 + 1, 1, strip_b, 0)
                if t > 0:
                    modulate(n - 1, t - 1, sc_f, M_SHF, 1, n - 1)

                def free():
                    act.wait_ge(rmw_done, t + 1)
                    act.wait_ge(tr_done, n)
                norm(n, t, x2, xn[:, 0, :], free)
            modulate(2 * NT - 1, NT - 1, sc_f, M_SHF, 1, 0)

            def mlp(b, last):
                n = W_MLP0 + 2 + 8 * b
                half = W_MLP0 // 2 + 1 + 4 * b

                def down(i, at, slot):
                    hi(n, slot, wb_hi[:, i, :], 16 * (half + at // 2 + 1))

                def strip(at, slot, count):
                    wait(act, up_done, count)
                    hi(n, slot, w_hi[:, slot, :], 16 * (half + at // 2 + 1))

                def relu_sq(i):
                    for c in range(NC):
                        q = 3 * i + c
                        r = relu[:, q % 2, 0:CW[c]]
                        act.wait_ge(up_done, 12 * b + q + 1)
                        wait(act, r2_done, 12 * b + q - 1)
                        act.activation(r, ps[:, up_bank(i, c), 0:CW[c]], ACT.Relu).then_inc(up_evac, 1)
                        act.wait_ge(up_evac, 12 * b + q + 1)
                        if c < 2:
                            act.activation(wb_hi[:, FI + i, c * CH:(c + 1) * CH], r, ACT.Square).then_inc(ffhi_done, 1)
                        else:
                            act.activation(wb_hi[:, FI + i, c * CH:SEQ], r[:, 0:PROMPT2], ACT.Square)
                            act.activation(stk[:, i, 0:SMP], r[:, PROMPT2:CW[c]], ACT.Square).then_inc(ffhi_done, 1)

                act.wait_ge(tile_done, NT * (b + 1))
                down(0, 0, 0)
                down(1, 1, 1)
                relu_sq(0)
                strip(2, 0, 12 * b + 3)
                down(2, 3, 1)
                down(3, 4, 0)
                relu_sq(1)
                strip(5, 1, 12 * b + 6)
                relu_sq(2)
                if not last:
                    strip(6, 0, 12 * b + 9)
                relu_sq(3)
                if not last:
                    strip(7, 1, 12 * b + 12)

            act.wait_ge(nlo_done, 2 * NT)
            mlp(0, False)
            gates_out(2, 6, 4)
            with act.Fori(1, NBLK - 1) as b:
                mlp(b, False)
            mlp(NBLK - 1, True)

            for t in range(NT):
                r = rows[t]
                act.wait_ge(rmw_done, NT * (NBLK + 1) - NT + t + 1)
                own(act.activation(xn[0:r, 0, :], x2[0:r, t, :], ACT.Square, accum_out=ssq[0:r, 0, t:t + 1]))
                act.activation(ssq[0:r, 1, t:t + 1], ssq[0:r, 0, t:t + 1], ACT.Sqrt, scale=1.0 / D,
                               bias=eps[0:r, :]).then_inc(std_done, 1)

        @block.vector
        def _(dve):
            ordered = [0]

            def own(ins):
                ordered[0] += 1
                ins.then_inc(dve_ord, 1)
                dve.wait_ge(dve_ord, ordered[0])

            dve.wait_ge(c_sig, 1)
            dve.tensor_tensor(ld_c[:, 1, :], ld_c[:, 0, :], ld_c[:, 1, :], ALU.mult).then_inc(c_silu, 1)
            dve.wait_ge(pool_set, 1)
            dve.tensor_scalar(stk[:, :, :], ident[:, :].unsqueeze(1).broadcast_to([P, KD, P]), 0.0, None,
                              ALU.mult).then_inc(c_zero, 1)
            dve.tensor_tensor(pick[:, :], ident[:, 0:9], ident[:, C_LO:C_LO + 9], ALU.add).then_inc(c_zero, 1)
            dve.wait_ge(par_tr, 1)
            dve.tensor_copy(par[:, :], ps[:, 1, 0:N_PAR]).then_inc(par_cp, 1)
            dve.tensor_copy(caw[:, :], ps[:, 1, P:P + KA * J]).then_inc(par_cp, 1)
            dve.tensor_copy(h0[:, :, :], ps[:, 1, 256:288].rearrange("p (b j) -> p b j", j=J)).then_inc(par_cp, 1)
            dve.tensor_copy(rec_s[:, :, :, 0:KB - 1],
                            ps[:, 1, 288:384].rearrange("p (j b s) -> p j b s", j=J, s=KB - 1)).then_inc(par_cp, 1)
            dve.wait_ge(c_cp, 1)
            dve.tensor_tensor(stk[:, :, C_LO:C_LO + 9], ps[:, 0, 0:9 * KD].rearrange("p (k c) -> p k c", c=9),
                              stk[:, :, 0:9].bitcast(F32), ALU.subtract).then_inc(c_cp, 1)
            for h in range(2):
                dve.wait_ge(sa_tr, h + 1)
                dve.tensor_copy(ga_s[:, :, 4 * h:4 * h + 4, 0:KA - 1],
                                ps[:, 2 + h, 0:480].rearrange("p (j b s) -> p j b s", j=J, s=KA - 1)).then_inc(sa_cp, 1)
            def scales(dst, row0, col):
                g = par[:, col:col + KD].unsqueeze(2).broadcast_to([P, KD, 9])
                dve.scalar_tensor_tensor(out=dst[:, :, :], in0=mod[:, row0:row0 + KD, :], scalar=1.0,
                                         in1=g, op0=ALU.add, op1=ALU.mult).then_inc(sc_done, 1)

            def scale_rows(n, t, src, dst):
                r = rows[t]
                dve.wait_ge(std_done, n + 1)
                own(dve.reciprocal(ssq[0:r, 2, t:t + 1], ssq[0:r, 1, t:t + 1]))
                dve.tensor_scalar(dst, src[0:r, t, :], ssq[0:r, 2, t:t + 1], None, ALU.mult).then_inc(xn_done, 1)

            def modulate(n, t, scale, shift0, slot, free, between=lambda: None):
                hf = xn[:, slot, :].rearrange("p (k c) -> p k c", c=P)
                dve.wait_ge(tr_done, n + 1)
                wait(dve, nhi_done, free)
                b = bank_pair(n)
                if t < NT - 1:
                    for k in range(4):
                        last = dve.tensor_scalar(hf[:, k, :], ps[:, b, k * P:(k + 1) * P], scale[:, k, 0:1],
                                                 mod[:, shift0 + k, 0:1], ALU.mult, ALU.add)
                    last.then_inc(hf_d, 1)
                    between()
                    dve.wait_ge(hf_a, hfa(n))
                else:
                    hs = hf[:, :, 0:SMP].rearrange("p k (b t) -> p k b t", t=TB)
                    src = ps[:, b:b + 2, :].rearrange("p a (k c) -> p (a k) c", c=P)[:, :, 0:SMP].rearrange(
                        "p k (b t) -> p k b t", t=TB)
                    for k in range(KD):
                        last = dve.tensor_tensor(hs[:, k], src[:, k],
                                                 scale[:, k, 1:9].unsqueeze(2).broadcast_to([P, NB, TB]), ALU.mult)
                    own(last)
                    for k in range(KD):
                        last = dve.tensor_tensor(hs[:, k], hs[:, k],
                                                 mod[:, shift0 + k, 1:9].unsqueeze(2).broadcast_to([P, NB, TB]), ALU.add)
                    last.then_inc(hf_d, 1)
                dve.wait_ge(nhi_done, n + 1)
                cols = slice(t * P, t * P + rows[t])
                dve.tensor_tensor(act_lo[:, :, cols], hf[:, :, 0:rows[t]], act_hi[:, :, cols].bitcast(F32),
                                  ALU.subtract).then_inc(nlo_done, 1)

            for g in range(ADA0):
                for i in range(4):
                    e = 4 * g + i
                    dve.wait_ge(ada0_hi, e + 1)
                    dve.tensor_tensor(w_lo[:, e % 2, :], ada0[:, g, 2 * i:2 * i + 2, :].rearrange("p a b -> p (a b)"),
                                      w_hi[:, e % 2, :].bitcast(F32), ALU.subtract).then_inc(ada0_lo, 1)
                if g < 3:
                    scale_rows(g, g, x2, x2[0:rows[g], g, :])
            scale_rows(AHEAD - 1, AHEAD - 1, x2, x2[:, AHEAD - 1, :])
            dve.wait_ge(ada_evac, ADA0)
            scales(sc_m, M_SCM, C_GMIX)
            dve.wait_ge(sc_done, 1)

            def scale_ahead(t):
                if t < NT:
                    scale_rows(t, t, x2, x2[0:rows[t], t, :])

            for t in range(NT):
                modulate(t, t, sc_m, M_SHM, t % 2, t - 1, lambda: scale_ahead(t + AHEAD))

            dve.wait_ge(par_cp, 1)
            dve.wait_ge(k_done, 1)
            e_, u_, ln_, w_ = (sp[:, n, :] for n in (1, 2, 3, 4))
            dve.tensor_scalar(u_, e_, 1.0, None, ALU.add).then_inc(k_done, 1)
            dve.wait_ge(k_done, 3)
            own(dve.tensor_scalar(w_, u_, -1.0, None, ALU.add))
            own(dve.tensor_tensor(e_, e_, w_, ALU.subtract))
            own(dve.reciprocal(w_, u_))
            own(dve.tensor_tensor(e_, e_, w_, ALU.mult))
            own(dve.tensor_tensor(ln_, ln_, e_, ALU.add))
            own(dve.tensor_scalar(w_, par[:, C_LAM:C_LAM + J], -1.0, 0.0, ALU.mult, ALU.max))
            own(dve.tensor_tensor(ln_, ln_, w_, ALU.add))
            dve.tensor_scalar(k4[:, 0, :], ln_, 4.0, None, ALU.mult).then_inc(k_done, 2)
            dve.tensor_scalar(k4[:, 1, :], ln_, -4.0, None, ALU.mult).then_inc(k_done, 2)
            dve.tensor_scalar(hb[:, 0, :], par[:, C_BGA:C_BGA + J], 0.5, None, ALU.mult).then_inc(k_done, 2)
            dve.tensor_scalar(hb[:, 1, :], par[:, C_BGX:C_BGX + J], 0.5, None, ALU.mult).then_inc(k_done, 2)

            def conv(src, src_s, width, taps, out, j, done, bias_col, base):
                out_s = out[:, j, SEQ:TOK].rearrange("p (b t) -> p b t", t=TB)
                for k in range(width):
                    w = taps(k)
                    win, win_s = src[:, j, k:k + SEQ], src_s[:, j, :, k:k + TB]
                    if k == 0:
                        bias = par[:, bass.ds(bias_col + j, 1)]
                        dve.tensor_scalar(out[:, j, 0:SEQ], win, w, bias, ALU.mult, ALU.add).then_inc(done, 1)
                        dve.tensor_scalar(out_s, win_s, w, bias, ALU.mult, ALU.add).then_inc(done, 1)
                    else:
                        dve.wait_ge(done, 2 * width * j + 2 * k - 1 + base)
                        dve.scalar_tensor_tensor(out=out[:, j, 0:SEQ], in0=win, scalar=w, in1=out[:, j, 0:SEQ],
                                                 op0=ALU.mult, op1=ALU.add).then_inc(done, 1)
                        dve.wait_ge(done, 2 * width * j + 2 * k + base)
                        dve.scalar_tensor_tensor(out=out_s, in0=win_s, scalar=w, in1=out_s,
                                                 op0=ALU.mult, op1=ALU.add).then_inc(done, 1)

            acc = [ps[:, 2 + 2 * n:4 + 2 * n, :].rearrange("p a b -> p (a b)") for n in range(2)]

            def conv_a_tile(j):
                out, out_s, bias = conv_a[:, j, 0:SEQ], conv_a[:, j, SEQ:TOK], par[:, bass.ds(C_CAB + j, 1)]
                for k in range(KA):
                    w, win, a = caw[:, bass.ds(j + k * J, 1)], ga[:, j, k:k + SEQ], acc[k % 2]
                    if k == 0:
                        dve.tensor_scalar(a, win, w, bias, ALU.mult, ALU.add).then_inc(conva_tap, 1)
                    elif k == 1:
                        dve.tensor_scalar(a, win, w, None, ALU.mult).then_inc(conva_tap, 1)
                    else:
                        if k == KA // 4:
                            dve.wait_ge(smp_ready, j + 1)
                            dve.tensor_reduce(out_s, smp_prod[:, j % 2, :, :], AX.X, ALU.add).then_inc(smp_sum, 1)
                        dve.wait_ge(conva_tap, STEPS_A * j + k - 1)
                        dve.scalar_tensor_tensor(out=out if k == KA - 1 else a, in0=win, scalar=w, in1=a,
                                                 op0=ALU.mult, op1=ALU.add).then_inc(conva_tap, 1)
                dve.wait_ge(conva_tap, STEPS_A * j + KA)
                dve.tensor_tensor(out, out, acc[1], ALU.add).then_inc(conva_tap, 1)
                dve.wait_ge(smp_sum, j + 1)
                dve.tensor_scalar(out_s, out_s, bias, None, ALU.add).then_inc(conva_tap, 1)
                dve.wait_ge(conva_tap, STEPS_A * (j + 1))

            dve.wait_ge(sa_cp, 2)
            with dve.Fori(0, J) as j:
                dve.wait_ge(ga_ready, 2 * j + 3)
                conv_a_tile(j)
            dve.wait_ge(tails, 1)
            with dve.Fori(0, J // 2) as q:
                for s, out in ((0, evac_a), (1, evac_b)):
                    dve.wait_ge(out, NC * (J + 1) + NC * q)
                    j = 2 * q + s
                    conv(rec, rec_s, KB, lambda k: par[:, bass.ds(C_CBW + j + k * J, 1)], cb, j, convb_tap, C_CBB, 0)

            def over_tiles(ap, w):
                return ap.unsqueeze(1).broadcast_to([P, J, w])

            for c in range(NC):
                t0, w = c * CH, CW[c]
                dve.wait_ge(mean_done, c + 1)
                dve.tensor_tensor(conv_a[:, :, t0:t0 + w], conv_a[:, :, t0:t0 + w], over_tiles(ps[:, 2 + c, 0:w], w),
                                  ALU.subtract).then_inc(xc_done, 1)
            def normalise(c):
                t0, w = c * CH, CW[c]
                dve.wait_ge(sd_done, c + 1)
                own(dve.reciprocal(rstd[:, t0:t0 + w], rstd[:, t0:t0 + w]))
                own(dve.tensor_tensor(conv_a[:, :, t0:t0 + w], conv_a[:, :, t0:t0 + w], over_tiles(rstd[:, t0:t0 + w], w),
                                      ALU.mult))
                for i in range(J):
                    last = dve.tensor_scalar(conv_a[:, i, t0:t0 + w], conv_a[:, i, t0:t0 + w],
                                             par[:, C_LNG + i:C_LNG + i + 1], par[:, C_LNB + i:C_LNB + i + 1],
                                             ALU.mult, ALU.add)
                last.then_inc(xs_done, 1)

            for j in range(J):
                dve.wait_ge(evac_b, NC * (2 * J + j + 1))
                own(dve.scalar_tensor_tensor(out=cb[:, j, :], in0=sg[:, :], scalar=1.0, in1=cb[:, j, :], op0=ALU.add,
                                             op1=ALU.mult))
                dve.wait_ge(a_done, j + 1)
                own(dve.tensor_tensor(sg[:, :], a_t[j], a_t[j], ALU.mult))
                dve.wait_ge(th_done, j + 1)
                dve.scalar_tensor_tensor(out=m_t[j], in0=sg[:, :], scalar=1.0, in1=m_t[j], op0=ALU.add,
                                         op1=ALU.mult).then_inc(q_done, 1)

            def firsts(ap):
                return ap[:, SEQ:TOK].rearrange("p (b t) -> p b t", t=TB)[:, :, 0]

            for j in range(J):
                own(dve.tensor_tensor(h0_a[:, :], firsts(a_t[j]), h0[:, :, j], ALU.mult))
                own(dve.memset(firsts(a_t[j]), 0.0))
                dve.wait_ge(m_done, j + 1)
                own(dve.memset(m_t[j][:, 0:1], 1.0))
                own(dve.scalar_tensor_tensor(out=cb[:, j, :], in0=m_t[j], scalar=0.5, in1=cb[:, j, :], op0=ALU.mult,
                                             op1=ALU.mult))
                own(dve.tensor_tensor(firsts(cb[:, j, :]), firsts(cb[:, j, :]), h0_a[:, :], ALU.add))
                dve.tensor_tensor_scan(m_t[j], a_t[j], cb[:, j, :], 0.0, ALU.mult, ALU.add).then_inc(h_done, 1)
                dve.wait_ge(h_done, j + 1)
                dve.tensor_copy(h_end[:, j, 0:1], m_t[j][:, SEQ - 1:SEQ])
                dve.tensor_copy(h_end[:, j, 1:9], m_t[j][:, SEQ:TOK].rearrange("p (b t) -> p b t", t=TB)[:, :, TB - 1])
                dve.tensor_tensor(gel[:, j, :], m_t[j], gel[:, j, :], ALU.mult).then_inc(yb_done, 1)


            def swish(c):
                t0, w = c * CH, CW[c]
                dve.wait_ge(sig_done, c + 1)
                dve.tensor_tensor(conv_a[:, :, t0:t0 + w], conv_a[:, :, t0:t0 + w], sq[:, :, 0:w],
                                  ALU.mult).then_inc(ya_done, 1)

            def ya_lo(c):
                t0, w = c * CH, CW[c]
                dve.wait_ge(yhi_done, J + c + 1)
                n = w if c < 2 else PROMPT2
                ins = dve.tensor_tensor(act_lo[:, 0:J, t0:t0 + n], conv_a[:, :, t0:t0 + n],
                                        act_hi[:, 0:J, t0:t0 + n].bitcast(F32), ALU.subtract)
                if c == 2:
                    ins = dve.tensor_tensor(stk[:, 0:J, SMP:P], conv_a[:, :, SEQ:TOK],
                                            stk[:, 0:J, 0:SMP].bitcast(F32), ALU.subtract)
                ins.then_inc(ylo_done, 1)

            def w_out_lo(k):
                dve.wait_ge(hi_ready, W_OUT0 + k + 1)
                dve.wait_ge(lo_ready, W_OUT0 + k)
                dve.tensor_tensor(wb_lo[:, k, :], raw[:, k % 2, :], wb_hi[:, k, :].bitcast(F32),
                                  ALU.subtract).then_inc(lo_ready, 1)

            normalise(0)
            w_out_lo(1)
            normalise(1)
            swish(0)
            for j in range(J):
                dve.wait_ge(yhi_done, j + 1)
                dve.tensor_tensor(act_lo[:, J + j, 0:SEQ], gel[:, j, 0:SEQ], act_hi[:, J + j, 0:SEQ].bitcast(F32),
                                  ALU.subtract)
                dve.tensor_tensor(stk[:, J + j, SMP:P], gel[:, j, SEQ:TOK], stk[:, J + j, 0:SMP].bitcast(F32),
                                  ALU.subtract).then_inc(ylo_done, 1)
                if j == 1:
                    w_out_lo(3)
            ya_lo(0)
            normalise(2)
            w_out_lo(5)
            for c in range(1, NC):
                swish(c)
                ya_lo(c)
            w_out_lo(7)

            dve.wait_ge(ada_evac, ADA_G)
            scales(sc_f, M_SCF, C_GFFN)

            def add_tile(t, bank, first):
                src = ps[:, bank:bank + 2, :].rearrange("p a b -> p (a b)")
                if t < NT - 1:
                    dve.tensor_tensor(src, src, gt_p[:, :], ALU.mult).then_inc(gated, 1)
                    dve.wait_ge(gated, first + 1)
                    dve.tensor_tensor(x2[:, t, :], x2[:, t, :], src, ALU.add).then_inc(rmw_done, 1)
                else:
                    dve.tensor_tensor(src[0:SMP], src[0:SMP], gt_s[:, :], ALU.mult).then_inc(gated, 1)
                    dve.tensor_tensor(src[SMP:P], src[SMP:P], gt_s[:, :], ALU.mult).then_inc(gated, 1)
                    dve.wait_ge(gated, first + 2)
                    dve.tensor_tensor(x2[0:SMP, t, :], x2[0:SMP, t, :], src[0:SMP], ALU.add).then_inc(gated, 1)
                    dve.wait_ge(gated, first + 3)
                    dve.tensor_tensor(x2[0:SMP, t, :], x2[0:SMP, t, :], src[SMP:P], ALU.add).then_inc(rmw_done, 1)

            GATED = NT - 1 + 3
            dve.wait_ge(gt_cp, 2)
            dve.wait_ge(sc_done, 2)
            for t in range(NT):
                n = NT + t
                dve.wait_ge(x_in[t], 32)
                dve.wait_ge(tile_done, t + 1)
                add_tile(t, 0 if t % 2 == 0 else 2, t)
                if t > 0:
                    modulate(n - 1, t - 1, sc_f, M_SHF, 1, n - 1)
                dve.wait_ge(tr_done, n)
                scale_rows(n, t, x2, xn[0:rows[t], 0, :])
            modulate(2 * NT - 1, NT - 1, sc_f, M_SHF, 1, 2 * NT - 1)

            def squares(b):
                for q in range(12):
                    i, c = q // NC, q % NC
                    r, f = relu[:, q % 2, 0:CW[c]], relu2[:, q % 2, 0:CW[c]]
                    dve.wait_ge(up_evac, 12 * b + q + 1)
                    dve.tensor_tensor(f, r, r, ALU.mult).then_inc(r2_done, 1)
                    dve.wait_ge(r2_done, 12 * b + q + 1)
                    dve.wait_ge(ffhi_done, 12 * b + q + 1)
                    n = CH if c < 2 else PROMPT2
                    cols = slice(c * CH, c * CH + n)
                    ins = dve.tensor_tensor(wb_lo[:, FI + i, cols], f[:, 0:n], wb_hi[:, FI + i, cols].bitcast(F32),
                                            ALU.subtract)
                    if c == 2:
                        ins = dve.tensor_tensor(stk[:, i, SMP:P], f[:, PROMPT2:CW[c]], stk[:, i, 0:SMP].bitcast(F32),
                                                ALU.subtract)
                    ins.then_inc(fflo_done, 1)

            def mlp(b, last):
                squares(b)
                if last:
                    dve.wait_ge(gf_in, 16)
                if isinstance(b, int) and b == 0:
                    dve.wait_ge(gt_cp, 4)
                for t in range(NT):
                    dve.wait_ge(tile_done, NT * (b + 1) + t + 1)
                    add_tile(t, 6 if t % 2 == 0 else 4, GATED * (b + 1) + t)
                    if last and t > 0:
                        final(t - 1)
                if last:
                    final(NT - 1)

            def final(t):
                r = rows[t]
                dve.wait_ge(std_done, 2 * NT + t + 1)
                own(dve.reciprocal(ssq[0:r, 2, t:t + 1], ssq[0:r, 1, t:t + 1]))
                dve.scalar_tensor_tensor(out=x2[0:r, t, :], in0=x2[0:r, t, :], scalar=ssq[0:r, 2, t:t + 1],
                                         in1=raw[0:r, 0, :], op0=ALU.mult, op1=ALU.mult).then_inc(fin_y, 1)

            mlp(0, False)
            with dve.Fori(1, NBLK - 1) as b:
                mlp(b, False)
            mlp(NBLK - 1, True)

        @block.tensor
        def _(pe):
            mm = nc.tensor.matmul
            pe.wait_ge(pool_set, 1)
            pe.wait_ge(c_silu, 1)
            for k in range(KD):
                last = nc.tensor.transpose(ps[:, 0, 9 * k:9 * k + 9], ld_c[0:9, 1, k * P:(k + 1) * P], ident[0:9, 0:9])
            last.then_inc(c_tr, 1)
            pe.wait_ge(par_in, 16 * N_ROWS_PAR)
            nc.tensor.transpose(ps[:, 1, 0:N_PAR], ld_par[0:N_PAR, 0, :], ident[0:N_PAR, 0:N_PAR])
            nc.tensor.transpose(ps[:, 1, P:P + KA * J], ld_par[0:KA * J, 1, :], ident[0:KA * J, 0:KA * J])
            nc.tensor.transpose(ps[:, 1, 256:288], ld_par[0:32, 2, :], ident[0:32, 0:32])
            for j in range(J):
                last = nc.tensor.transpose(ps[:, 1, 288 + 24 * j:312 + 24 * j], ld_sb[:, j * P:(j + 1) * P],
                                           ident[0:24, 0:24])
            last.then_inc(par_tr, 1)
            pe.wait_ge(sa_in, 32)
            for h in range(2):
                for j in range(J):
                    last = nc.tensor.transpose(ps[:, 2 + h, 120 * j:120 * j + 120], ld_sa[:, h, j * P:(j + 1) * P],
                                               ident[0:120, 0:120])
                last.then_inc(sa_tr, 1)

            def ada(i, bank, wh, wl, used):
                for h in range(2):
                    c = stk[:, 2 * i + h, :]
                    mm(ps[:, bank, :], c, wh[:, h * GW:(h + 1) * GW], start=(i == 0 and h == 0), stop=False)
                    last = mm(ps[:, bank, :], c, wl[:, h * GW:(h + 1) * GW], start=False, stop=(i == 3 and h == 1))
                last.then_inc(used, 1)

            def group_turn(g, bank, col):
                pe.wait_ge(rows_out, g + 1)
                for i in range(4):
                    last = mm(ps[:, bank, col + 9 * i:col + 9 * i + 9], ada_rows[:, i * P:(i + 1) * P], pick[:, :],
                              start=True, stop=True)
                last.then_inc(ada_tr, 1)

            def turn(n, t, src):
                pe.wait_ge(xn_done, n + 1)
                if n >= 2:
                    pe.wait_ge(hf_d, n - 1)
                    pe.wait_ge(hf_a, hfa(n - 2))
                b, r = bank_pair(n), rows[t]
                for k in range(KD):
                    last = nc.tensor.transpose(ps[:, b + k // 4, (k % 4) * P:(k % 4) * P + r],
                                               src[0:r, k * P:(k + 1) * P], ident[0:r, 0:r])
                last.then_inc(tr_done, 1)

            pe.wait_ge(c_cp, 2)
            pe.wait_ge(c_zero, 2)
            for g in range(ADA0):
                for i in range(4):
                    e = 4 * g + i
                    pe.wait_ge(ada0_hi, e + 1)
                    pe.wait_ge(ada0_lo, e + 1)
                    if i == 0 and g >= 2:
                        pe.wait_ge(rows_out, g - 1)
                    ada(i, 6 + g % 2, w_hi[:, e % 2, :], w_lo[:, e % 2, :], ada0_used)
                    if i == 2 and g > 0:
                        group_turn(g - 1, 0, P + 36 * (g - 1))
            turn(0, 0, x2[:, 0, :])
            group_turn(ADA0 - 1, 0, P + 36 * (ADA0 - 1))

            def strip(slot, bank, c, done):
                for k in range(KD):
                    wh, wl = w_hi[:, slot, k * P:(k + 1) * P], w_lo[:, slot, k * P:(k + 1) * P]
                    xh, xl = act_hi[:, k, c * CH:c * CH + CW[c]], act_lo[:, k, c * CH:c * CH + CW[c]]
                    out = ps[:, bank, 0:CW[c]]
                    mm(out, wh, xh, start=(k == 0), stop=False)
                    mm(out, wh, xl, start=False, stop=False)
                    last = mm(out, wl, xh, start=False, stop=(k == KD - 1))
                last.then_inc(done, 1)

            def mean(c, bank, src, done):
                for j in range(J):
                    last = mm(ps[:, bank, 0:CW[c]], mean_w[:, :], src(j), start=(j == 0), stop=(j == J - 1))
                last.then_inc(done, 1)

            def mean_a(c):
                if c == 0:
                    pe.wait_ge(conva_tap, STEPS_A * J)
                mean(c, 2 + c, lambda j: conv_a[:, j, c * CH:c * CH + CW[c]], mean_done)

            def var_a(c):
                pe.wait_ge(sq_done, c + 1)
                wait(pe, sd_done, c)
                mean(c, 7, lambda j: sq[:, j, 0:CW[c]], var_done)

            def step(m, first, last=False):
                for s, done in ((0, strip_a), (1, strip_b)):
                    if first and s == 0:
                        for t in (1, 2, 3, 4):
                            turn(t, t, x2[:, t, :])
                    pe.wait_ge(hi_ready, 2 * m + s + 1)
                    pe.wait_ge(lo_ready, 2 * m + s + 1)
                    for c in range(NC):
                        if first and s == 0:
                            for t in ((), (5, 6, 7), (8,))[c]:
                                turn(t, t, x2[:, t, :])
                            pe.wait_ge(nhi_done, min(3 * c + 3, NT))
                            pe.wait_ge(nlo_done, min(3 * c + 3, NT))
                        out, count = ((evac_b, NC * m - 1), (evac_b, NC * m), (evac_a, NC * m + 1),
                                      (evac_a, NC * m + 2), (evac_a, NC * m + 3), (evac_b, NC * m + 1))[3 * s + c]
                        if first and s == 0:
                            strip(0, c, c, done)
                        else:
                            wait(pe, out, count)
                            strip(s, (s + c) % 2, c, done)
                        if c == 0 and s == 0 and not first:
                            group_turn(m + ADA0 - 1, 7, 0)
                        if first:
                            pieces = () if s == 0 else ((0,), (1,), (2, 3))[c]
                        else:
                            pieces = ((), (2 * s,), (2 * s + 1,))[c]
                        for i in pieces:
                            pe.wait_ge(ada_hi, 4 * m + i + 1)
                            pe.wait_ge(ada_lo, 4 * m + i + 1)
                            if i == 0 and first:
                                pe.wait_ge(hf_d, NT)
                                pe.wait_ge(hf_a, hfa(NT - 1))
                            ada(i, 6, aw_hi[:, i % 2, :], aw_lo[:, i % 2, :], ada_used)
                        if last and s == 1:
                            mean_a(c)

            pe.wait_ge(par_cp, 4)
            pe.wait_ge(sa_cp, 2)
            pe.wait_ge(ada_evac, ADA0)
            step(0, True)
            with pe.Fori(1, 2 * J - 1) as m:
                step(m, False)
            step(2 * J - 1, False, True)

            group_turn(ADA_G - 1, 7, 0)

            pe.wait_ge(wg_in, 64)
            pe.wait_ge(xc_done, NC)
            for j in range(J):
                pe.wait_ge(convb_tap, 2 * KB * (j + 1))
                for g, done, out in ((0, gate_a, evac_a), (1, gate_x, evac_b)):
                    for c in range(NC):
                        if j > 0:
                            pe.wait_ge(out, NC * (2 * J + j) - 2 + c)
                        mm(ps[:, 3 * g + c, 0:CW[c]], wg[:, g, j, :], cb[:, j, c * CH:c * CH + CW[c]],
                           start=True, stop=True).then_inc(done, 1)

            def turn_state(n, bank, r, src):
                wait(pe, st_cp, n - 1)
                for j in range(J):
                    last = nc.tensor.transpose(ps[0:r, bank, j * P:(j + 1) * P], src(j), ident[:, :])
                last.then_inc(st_tr, 1)

            pe.wait_ge(ada_evac, ADA_G)
            pe.wait_ge(tails, 1)
            turn_state(0, 6, KA - 1, lambda j: tail_p[:, j, :])
            for h in range(2):
                turn_state(1 + h, 7 - h, 4 * (KA - 1), lambda j: tail_a[:, j, 120 * h:120 * h + 120])
            pe.wait_ge(evac_a, 2 * J * NC)
            pe.wait_ge(evac_b, 2 * J * NC)
            pe.wait_ge(tails, 2)
            turn_state(3, 7, KB - 1, lambda j: tail_bp[:, j, :])
            turn_state(4, 6, NB * (KB - 1), lambda j: tail_b[:, j, :])

            for c in range(NC):
                var_a(c)
            pe.wait_ge(yb_done, J)
            pe.wait_ge(xc_done, NC)
            for j in range(J):
                last = nc.tensor.transpose(ps[0:9, 6, j * P:(j + 1) * P], h_end[:, j, :], ident[:, :])
            last.then_inc(st_tr, 1)

            def gates(row0, bank_p, bank_s):
                for k in range(KD):
                    g = mod[:, row0 + k, :]
                    last = mm(ps[:, bank_p + k // 4, (k % 4) * P:(k % 4 + 1) * P], g[:, 0:1].broadcast_to([P, P]),
                              ident[:, :], start=True, stop=True)
                last.then_inc(gt_mm, 1)
                for k in range(KD):
                    last = mm(ps[0:SMP, bank_s + k // 4, (k % 4) * P:(k % 4 + 1) * P],
                              gt_tok[:, int(row0 == M_GTF), k, :], ident[:, :],
                              start=True, stop=True)
                last.then_inc(gt_mm, 1)

            pe.wait_ge(evac_a, 3 * J * NC)
            pe.wait_ge(evac_b, 3 * J * NC)
            pe.wait_ge(st_cp, 6)
            pe.wait_ge(tails, 3)
            gates(M_GTM, 4, 6)

            def tile_product(t, bank, n_k, act_k, ready):
                for k in range(n_k):
                    ready(k)
                    halves = [(ps[:, bank + h, :], wb_hi[:, k, h * 512:(h + 1) * 512],
                               wb_lo[:, k, h * 512:(h + 1) * 512]) for h in range(2)]
                    end = k == n_k - 1
                    if t < NT - 1:
                        ah, al = act_k(k)
                        for out, wh, wl in halves:
                            mm(out, ah, wh, start=(k == 0), stop=False)
                            mm(out, ah, wl, start=False, stop=False)
                        for out, wh, wl in halves:
                            last = mm(out, al, wh, start=False, stop=end)
                    else:
                        for out, wh, wl in halves:
                            mm(out, stk[:, k, :], wh, start=(k == 0), stop=False)
                            last = mm(out, stk[:, k, :], wl, start=False, stop=end)
                last.then_inc(tile_done, 1)


            def w_out_ready(k):
                pe.wait_ge(hi_ready, W_OUT0 + k + 1)
                pe.wait_ge(lo_ready, W_OUT0 + k + 1)

            for t in range(NT):
                wait(pe, rmw_done, t - 1)
                if t % NC == 0:
                    pe.wait_ge(yhi_done, J + t // NC + 1)
                    pe.wait_ge(ylo_done, J + t // NC + 1)
                elif t == NT - 1:
                    pe.wait_ge(yhi_done, J + NC)
                    pe.wait_ge(ylo_done, J + NC)
                tile_product(t, 0 if t % 2 == 0 else 2, KD,
                             lambda k: (act_hi[:, k, t * P:(t + 1) * P], act_lo[:, k, t * P:(t + 1) * P]),
                             w_out_ready if t == 0 else lambda k: None)
                if t > 0:
                    if t == 1:
                        pe.wait_ge(gt_cp, 2)
                    turn(NT + t - 1, t - 1, xn[:, 0, :])

            def mlp(b, first):
                n = W_MLP0 + 8 * b
                for i in range(FI):
                    at = (0, 1, 4, 7)[i]
                    pe.wait_ge(hi_ready, n + at + 1)
                    pe.wait_ge(lo_ready, n + at + 1)
                    if i == 1:
                        pe.wait_ge(rmw_done, NT * b + NT - 1)
                    for c in range(NC):
                        if first and i == 0:
                            if c < 2:
                                pe.wait_ge(rmw_done, NT - 1 + c)
                            if c == 2:
                                turn(2 * NT - 1, NT - 1, xn[:, 0, :])
                            pe.wait_ge(nhi_done, NT + min(3 * c + 3, NT))
                            pe.wait_ge(nlo_done, NT + min(3 * c + 3, NT))
                        wait(pe, up_evac, 12 * b + 3 * i + c - 5)
                        strip(i % 2, up_bank(i, c), c, up_done)
                if first:
                    pe.wait_ge(up_evac, 12)
                    gates(M_GTF, 6, 4)
                    pe.wait_ge(gt_cp, 4)
                for t in range(NT):
                    pe.wait_ge(rmw_done, NT * (b + 1) + max(t - 1, 0))
                    if t == 1:
                        pe.wait_ge(up_evac, 12 * b + 12)

                    def ready(k):
                        if t == 0:
                            pe.wait_ge(hi_ready, n + (3, 4, 6, 7)[k])
                            pe.wait_ge(lo_ready, n + (3, 4, 6, 7)[k])
                        if t % NC == 0:
                            pe.wait_ge(ffhi_done, 12 * b + 3 * k + t // NC + 1)
                            pe.wait_ge(fflo_done, 12 * b + 3 * k + t // NC + 1)
                    tile_product(t, 6 if t % 2 == 0 else 4, FI,
                                 lambda k: (wb_hi[:, FI + k, t * P:(t + 1) * P], wb_lo[:, FI + k, t * P:(t + 1) * P]),
                                 ready)

            mlp(0, True)
            with pe.Fori(1, NBLK) as b:
                mlp(b, False)


def hfa(n):
    return n + 1 - (n >= NT - 1) - (n >= 2 * NT - 1)


_INS = ["x_prompt", "x_sample", "c_prompt", "c_sample", "state_conv_a", "state_conv_b", "state_lru_h",
        "w_ada", "b_ada", "g_mix", "w_in", "b_in", "conv_a_w", "conv_a_b", "ln_a_g", "ln_a_b", "conv_b_w",
        "conv_b_b", "w_gate_a", "b_gate_a", "w_gate_x", "b_gate_x", "lru_lambda", "w_out", "g_ffn", "w_up",
        "w_down", "g_final"]
_OUTS = [(1, SEQ, D), (NB, TB, D), (1, 1, KA - 1, WA), (1, 1, KB - 1, WA), (1, 1, WA),
         (1, NB, KA - 1, WA), (1, NB, KB - 1, WA), (1, NB, WA)]


def kernel(**inputs):
    import numpy as _np
    import concourse.bacc as _bacc
    from concourse.bass_utils import run_bass_kernel_spmd as _run

    nc = _bacc.Bacc("TRN2", target_bir_lowering=False, num_devices=1, dynamic_dma_scratch_size=1024)
    arrays, args = {}, []
    for name in _INS:
        a = _np.ascontiguousarray(inputs[name])
        arrays[f"in_{name}"] = a
        args.append(nc.dram_tensor(f"in_{name}", a.shape, mybir.dt.from_np(a.dtype), kind="ExternalInput").ap())
    for i, shape in enumerate(_OUTS):
        args.append(nc.dram_tensor(f"out_{i}", shape, F32, kind="ExternalOutput").ap())
    trunk(nc, *args)
    r = _run(nc, [arrays], core_ids=[0])
    return tuple(r.results[0][f"out_{i}"] for i in range(len(_OUTS)))
```
